# Optimizing a Trainium2 kernel written in Bass

```python
import math
import jax, jax.numpy as jnp
from jax import lax
import numpy as np

D_MODEL = 1024
BATCH = 1
SEQ = 256
DEPTH = 2

N_MIXERS = 2
EPS = 1e-6
ML_H = 4
ML_DV = 2 * D_MODEL // ML_H
ML_DQK = ML_DV // 2
ML_QK = ML_H * ML_DQK
ML_V = ML_H * ML_DV
ML_PROJ = 2 * ML_QK + 2 * ML_V + 2 * ML_H
ML_CHUNK = 64
CONV_K = 4
DA_DH = 64
DA_DV = 2 * DA_DH
DA_H = D_MODEL // DA_DV
DA_QK = DA_H * 2 * DA_DH
DA_PROJ = 2 * DA_QK + DA_H * DA_DV
DA_EPS = 1e-5
Q_BLOCK = 128
N_GROUPS = 4
EXPERTS_PER_GROUP = 8
N_EXPERTS = N_GROUPS * EXPERTS_PER_GROUP
TOP_K_IN_GROUP = 2
D_EXPERT = D_MODEL // 4
TOK_BLOCK = 128

kernel_name = 'hybrid_mlstm_diffattn_hmoe'

def rmsnorm(x, g, eps=EPS):
    xf = x.astype(jnp.float32)
    y = xf * lax.rsqrt(jnp.mean(xf * xf, axis=-1, keepdims=True) + eps)
    return (y * g.astype(jnp.float32)).astype(x.dtype)

def causal_conv(u, w):
    K = w.shape[0]
    S = u.shape[1]
    up = jnp.pad(u, ((0, 0), (K - 1, 0), (0, 0)))
    return sum(up[:, j:j + S] * w[j] for j in range(K))

def mlstm_mixer(h, w_in, conv_w, b_i, b_f, norm_g, w_out):
    B, S, _ = h.shape
    f32 = jnp.float32
    p = h @ w_in
    qk = jax.nn.silu(causal_conv(p[..., :2 * ML_QK], conv_w))
    q = qk[..., :ML_QK] * (ML_DQK ** -0.5)
    k = qk[..., ML_QK:]
    v = p[..., 2 * ML_QK:2 * ML_QK + ML_V]
    o = p[..., 2 * ML_QK + ML_V:2 * ML_QK + 2 * ML_V]
    gates = p[..., 2 * ML_QK + 2 * ML_V:].astype(f32)
    i_pre = gates[..., :ML_H] + b_i.astype(f32)
    log_f = jax.nn.log_sigmoid(gates[..., ML_H:] + b_f.astype(f32))
    nc = S // ML_CHUNK

    def to_chunks(t, d):
        return t.astype(f32).reshape(B, nc, ML_CHUNK, ML_H, d).transpose(1, 0, 3, 2, 4)

    def gate_chunks(g):
        return g.reshape(B, nc, ML_CHUNK, ML_H).transpose(1, 0, 3, 2)

    qc, kc, vc = to_chunks(q, ML_DQK), to_chunks(k, ML_DQK), to_chunks(v, ML_DV)
    ic, fc = gate_chunks(i_pre), gate_chunks(log_f)
    causal = jnp.tril(jnp.ones((ML_CHUNK, ML_CHUNK), dtype=bool))

    def step(carry, inp):
        C, n, m = carry
        qt, kt, vt, it, lf = inp
        b = jnp.cumsum(lf, axis=-1)
        dmat = b[..., :, None] - b[..., None, :] + it[..., None, :]
        dmat = jnp.where(causal, dmat, -jnp.inf)
        inter_log = b + m[..., None]
        m_t = jnp.maximum(inter_log, jnp.max(dmat, axis=-1))
        wts = jnp.exp(dmat - m_t[..., None])
        scores = jnp.einsum('bhtd,bhsd->bhts', qt, kt) * wts
        inter_scale = jnp.exp(inter_log - m_t)
        num = jnp.einsum('bhts,bhsv->bhtv', scores, vt) + inter_scale[..., None] * jnp.einsum('bhvd,bhtd->bhtv', C, qt)
        den = jnp.sum(scores, axis=-1) + inter_scale * jnp.einsum('bhd,bhtd->bht', n, qt)
        h_out = num / jnp.maximum(jnp.abs(den), jnp.exp(-m_t))[..., None]
        bL = b[..., -1]
        log_w = bL[..., None] - b + it
        m_new = jnp.maximum(bL + m, jnp.max(log_w, axis=-1))
        ws = jnp.exp(log_w - m_new[..., None])
        decay = jnp.exp(bL + m - m_new)
        C_new = decay[..., None, None] * C + jnp.einsum('bhsv,bhsd->bhvd', vt * ws[..., None], kt)
        n_new = decay[..., None] * n + jnp.einsum('bhs,bhsd->bhd', ws, kt)
        return (C_new, n_new, m_new), h_out

    init = (jnp.zeros((B, ML_H, ML_DV, ML_DQK), f32), jnp.zeros((B, ML_H, ML_DQK), f32), jnp.zeros((B, ML_H), f32))
    _, hs = lax.scan(step, init, (qc, kc, vc, ic, fc))
    hs = hs.transpose(1, 0, 3, 2, 4).reshape(B, S, ML_H, ML_DV)
    hs = rmsnorm(hs, norm_g.reshape(ML_H, ML_DV)).reshape(B, S, ML_V)
    y = (hs * jax.nn.sigmoid(o.astype(f32))).astype(h.dtype)
    return y @ w_out

def diff_attention(h, w_in, lam_q1, lam_k1, lam_q2, lam_k2, norm_g, w_out, lambda_init):
    B, S, _ = h.shape
    f32 = jnp.float32
    p = (h @ w_in).astype(f32)
    q = p[..., :DA_QK].reshape(B, S, DA_H, 2, DA_DH) * (DA_DH ** -0.5)
    k = p[..., DA_QK:2 * DA_QK].reshape(B, S, DA_H, 2, DA_DH)
    v = p[..., 2 * DA_QK:].reshape(B, S, DA_H, DA_DV)
    lam = (jnp.exp(jnp.sum(lam_q1.astype(f32) * lam_k1.astype(f32)))
           - jnp.exp(jnp.sum(lam_q2.astype(f32) * lam_k2.astype(f32))) + lambda_init)
    nq = S // Q_BLOCK
    qb = q.reshape(B, nq, Q_BLOCK, DA_H, 2, DA_DH).transpose(1, 0, 2, 3, 4, 5)
    kpos = jnp.arange(S)

    def one_block(args):
        qblk, start = args
        s = jnp.einsum('bqhcd,bkhcd->bhcqk', qblk, k)
        qpos = start + jnp.arange(Q_BLOCK)
        causal = kpos[None, :] <= qpos[:, None]
        pr = jax.nn.softmax(jnp.where(causal, s, -jnp.inf), axis=-1)
        a = pr[:, :, 0] - lam * pr[:, :, 1]
        return jnp.einsum('bhqk,bkhe->bqhe', a, v)

    o = lax.map(one_block, (qb, jnp.arange(nq) * Q_BLOCK))
    o = o.transpose(1, 0, 2, 3, 4).reshape(B, S, DA_H, DA_DV)
    o = rmsnorm(o, norm_g, DA_EPS) * (1.0 - lambda_init)
    return o.reshape(B, S, DA_H * DA_DV).astype(h.dtype) @ w_out

def hier_moe(h, w_group, b_group, w_expert, b_expert, w_gu, w_down):
    B, S, D = h.shape
    T = B * S
    f32 = jnp.float32
    xt = h.reshape(T, D)
    g_logits = (xt @ w_group).astype(f32) + b_group.astype(f32)
    g_prob = jax.nn.softmax(g_logits, axis=-1)
    _, g_idx = lax.top_k(g_logits, 1)
    g_w = jnp.take_along_axis(g_prob, g_idx, axis=-1)
    e_logits = ((xt @ w_expert).astype(f32) + b_expert.astype(f32)).reshape(T, N_GROUPS, EXPERTS_PER_GROUP)
    e_logits = jnp.take_along_axis(e_logits, g_idx[:, :, None], axis=1)[:, 0]
    e_prob = jax.nn.softmax(e_logits, axis=-1)
    top_w, top_idx = lax.top_k(e_prob, TOP_K_IN_GROUP)
    top_w = top_w / jnp.sum(top_w, axis=-1, keepdims=True)
    within = jnp.sum(jax.nn.one_hot(top_idx, EXPERTS_PER_GROUP, dtype=f32) * top_w[..., None], axis=1)
    gate = (jax.nn.one_hot(g_idx[:, 0], N_GROUPS, dtype=f32)[:, :, None]
            * (g_w * within)[:, None, :]).reshape(T, N_EXPERTS)
    nb = T // TOK_BLOCK

    def expert_block(args):
        xb, gb = args
        gu = jnp.einsum('td,edf->tef', xb, w_gu)
        a = jax.nn.silu(gu[..., :D_EXPERT]) * gu[..., D_EXPERT:] * gb[..., None].astype(xb.dtype)
        return jnp.einsum('tef,efd->td', a, w_down)

    y = lax.map(expert_block, (xt.reshape(nb, TOK_BLOCK, D), gate.reshape(nb, TOK_BLOCK, N_EXPERTS)))
    return y.reshape(B, S, D)

def setup_inputs(seed: int = 0) -> dict:
    key = jax.random.key(seed)
    ks = jax.random.split(key, 32)
    n_a = (DEPTH + 1) // 2
    n_b = DEPTH // 2
    D = D_MODEL

    def nrm(k, shape, scale):
        return jax.random.normal(k, shape, jnp.float32) * scale

    return {
        'x': nrm(ks[0], (BATCH, SEQ, D), 1.0),
        'norm_mix': 1.0 + nrm(ks[1], (DEPTH, D), 0.01),
        'norm_ffn': 1.0 + nrm(ks[2], (DEPTH, D), 0.01),
        'ml_w_in': nrm(ks[3], (n_a, D, ML_PROJ), D ** -0.5),
        'ml_conv': nrm(ks[4], (n_a, CONV_K, 2 * ML_QK), 0.5),
        'ml_b_i': nrm(ks[5], (n_a, ML_H), 0.1),
        'ml_b_f': jnp.linspace(3.0, 6.0, ML_H)[None, :] + nrm(ks[6], (n_a, ML_H), 0.01),
        'ml_norm': 1.0 + nrm(ks[7], (n_a, ML_V), 0.01),
        'ml_w_out': nrm(ks[8], (n_a, ML_V, D), ML_V ** -0.5),
        'da_w_in': nrm(ks[9], (n_b, D, DA_PROJ), D ** -0.5),
        'da_lq1': nrm(ks[10], (n_b, DA_DH), 0.1),
        'da_lk1': nrm(ks[11], (n_b, DA_DH), 0.1),
        'da_lq2': nrm(ks[12], (n_b, DA_DH), 0.1),
        'da_lk2': nrm(ks[13], (n_b, DA_DH), 0.1),
        'da_norm': 1.0 + nrm(ks[14], (n_b, DA_DV), 0.01),
        'da_w_out': nrm(ks[15], (n_b, DA_H * DA_DV, D), (DA_H * DA_DV) ** -0.5),
        'moe_w_group': nrm(ks[16], (DEPTH, D, N_GROUPS), D ** -0.5),
        'moe_b_group': nrm(ks[17], (DEPTH, N_GROUPS), 0.01),
        'moe_w_expert': nrm(ks[18], (DEPTH, D, N_EXPERTS), D ** -0.5),
        'moe_b_expert': nrm(ks[19], (DEPTH, N_EXPERTS), 0.01),
        'moe_w_gu': nrm(ks[20], (DEPTH, N_EXPERTS, D, 2 * D_EXPERT), D ** -0.5),
        'moe_w_down': nrm(ks[21], (DEPTH, N_EXPERTS, D_EXPERT, D), D_EXPERT ** -0.5),
        'final_norm': 1.0 + nrm(ks[22], (D,), 0.01),
    }

def reference(x, norm_mix, norm_ffn, ml_w_in, ml_conv, ml_b_i, ml_b_f, ml_norm, ml_w_out,
              da_w_in, da_lq1, da_lk1, da_lq2, da_lk2, da_norm, da_w_out,
              moe_w_group, moe_b_group, moe_w_expert, moe_b_expert, moe_w_gu, moe_w_down,
              final_norm):
    for i in range(DEPTH):
        hn = rmsnorm(x, norm_mix[i])
        j = i // N_MIXERS
        if i % N_MIXERS == 0:
            mix = mlstm_mixer(hn, ml_w_in[j], ml_conv[j], ml_b_i[j], ml_b_f[j], ml_norm[j], ml_w_out[j])
        else:
            lambda_init = 0.8 - 0.6 * math.exp(-0.3 * i)
            mix = diff_attention(hn, da_w_in[j], da_lq1[j], da_lk1[j], da_lq2[j], da_lk2[j],
                                 da_norm[j], da_w_out[j], lambda_init)
        x = x + mix
        x = x + hier_moe(rmsnorm(x, norm_ffn[i]), moe_w_group[i], moe_b_group[i], moe_w_expert[i],
                         moe_b_expert[i], moe_w_gu[i], moe_w_down[i])
    return rmsnorm(x, final_norm)


_drawn_inputs = setup_inputs


def setup_inputs(seed=0):
    import zlib

    import numpy as np

    out = dict(_drawn_inputs(seed))
    spreads = {}
    factors = {'ml_b_i': 64.0,
     'ml_norm': 12.755,
     'da_lq1': 6.59,
     'da_norm': 31.059,
     'moe_b_group': 26.403,
     'moe_b_expert': 10.792,
     'final_norm': 30.831,
     'norm_ffn': 6.371}
    for name, (base, spread) in spreads.items():
        noise = np.random.default_rng([zlib.crc32(name.encode()), seed]).standard_normal(out[name].shape)
        drawn = base * np.exp(spread * noise) if base else spread * noise
        out[name] = __import__('jax').numpy.asarray(drawn.astype(out[name].dtype))
    for name, factor in factors.items():
        out[name] = (out[name] * factor).astype(out[name].dtype)
    return out
```

```python
import math
from contextlib import ExitStack

import concourse.bass as bass
from concourse import mybir

F32 = mybir.dt.float32
ALU = mybir.AluOpType
ACT = mybir.ActivationFunctionType
AX_X = mybir.AxisListType.X

P = 128
D = 1024
T = 256
NT = T // P
DC = D // P
EPS = 1e-6
HM = 4
DQK = 256
DV = 512
QC = 2 * HM * DQK // P
VM = HM * DV
VC = VM // P
TAPS = 4
HA = 8
DH = 64
DVA = 128
DA_EPS = 1e-5
G = 4
EG = 8
E = G * EG
F = D // 4
LOGITS = G + E
BIG = 1e30
LAMBDA_INIT = 0.8 - 0.6 * math.exp(-0.3 * 1)

UNIT = 2048
RING = 12
UE = 3
EB = RING // UE
TURNS = E // EB
U_ML_IN = 24
U_ML_OUT = 8
U_MOE = UE * E
U_DA_IN = 12
U_DA_OUT = 4
U0_ML_OUT = U_ML_IN
U0_MOE0 = U0_ML_OUT + U_ML_OUT
U0_DA_IN = U0_MOE0 + U_MOE
U0_DA_OUT = U0_DA_IN + U_DA_IN
U0_MOE1 = U0_DA_OUT + U_DA_OUT
U_ALL = U0_MOE1 + U_MOE

C_CONV = 0
C_MLN = TAPS * QC
C_DAN = C_MLN + VC
N_COLS = C_DAN + 1


def program(nc, x, norm_mix, norm_ffn, ml_w_in, ml_conv, ml_b_i, ml_b_f, ml_norm, ml_w_out,
            da_w_in, da_lq1, da_lk1, da_lq2, da_lk2, da_norm, da_w_out,
            moe_w_group, moe_b_group, moe_w_expert, moe_b_expert, moe_w_gu, moe_w_down,
            final_norm, out):
    with ExitStack() as ctx:
        def sb(name, shape, dt=F32):
            return ctx.enter_context(nc.sbuf_tensor(name, shape, dt))

        def sem(name):
            return ctx.enter_context(nc.semaphore(name))

        ring = sb("ring", [P, RING, UNIT])
        xres = sb("xres", [P, NT, D])
        xn = sb("xn", [P, NT, D])
        xT = sb("xT", [P, DC, T])
        big = sb("big", [P, 12 * 1024])
        qkT = big[:, 0:QC * T].rearrange("p (c t) -> p c t", c=QC)
        v_sb = big[:, 4096:8192].rearrange("p (i v) -> p i v", i=NT)
        og = big[:, 8192:12288].rearrange("p (i v) -> p i v", i=NT)
        vA = big[:, 4096:6144].rearrange("p (i v) -> p i v", i=NT)
        yT = big[:, 0:VC * T].rearrange("p (c t) -> p c t", c=VC)
        work = sb("work", [P, 2, 512])
        sT = sb("sT", [P, 2, 384])
        wT = sb("wT", [P, 2, 384])
        conv_u = sb("conv_u", [P, 2, T])
        ident = sb("ident", [P, P])
        neg_ts = sb("neg_ts", [P, P])
        neg_qk = sb("neg_qk", [P, T])
        ones = sb("ones", [P, P])
        head_sel = sb("head_sel", [HM, HM, P])
        eps_col = sb("eps_col", [P, 2])
        par_rows = sb("par_rows", [N_COLS, P])
        par = sb("par", [P, N_COLS])
        g_mix = sb("g_mix", [P, 2, DC])
        g_ffn = sb("g_ffn", [P, 2, DC])
        g_fin = sb("g_fin", [P, D])
        w_gate = sb("w_gate", [P, DC, 2 * HM])
        b_i = sb("b_i", [HM, 1])
        b_f = sb("b_f", [HM, 1])
        w_rout = sb("w_rout", [P, 2, DC, LOGITS])
        b_rout = sb("b_rout", [P, 2, NT, LOGITS])
        lam_in = sb("lam_in", [P, 4, DH])
        lam_s = sb("lam_s", [P, 8])
        st = sb("st", [P, 64])
        gr = xn[0:HM, :, :].rearrange("h i (r t) -> h (i r) t", t=T)
        gc = sb("gc", [P, NT, 2 * HM])
        lg = sb("lg", [P, NT, LOGITS])
        rt = sb("rt", [P, 6, NT, E])
        gate = sb("gate", [P, NT, E])
        rank_w = sb("rank_w", [P, E])
        a_sb = sb("a_sb", [P, 2, F])
        sg_sb = sb("sg_sb", [P, 2, F])
        aT = sb("aT", [P, 2, 2, P])
        ps = ctx.enter_context(nc.psum_tensor("ps", [P, 8, 512], F32))

        unit_loaded = [sem(f"unit_loaded{i}") for i in range(RING)]
        unit_used = sem("unit_used")
        x_loaded = sem("x_loaded")
        par_loaded = sem("par_loaded")
        consts_loaded = sem("consts_loaded")
        tables_made = sem("tables_made")
        pool_step = sem("pool_step")
        par_T = sem("par_T")
        par_ready = sem("par_ready")
        act_step = sem("act_step")
        dve_step = sem("dve_step")
        squares = sem("squares")
        ms_ready = sem("ms_ready")
        root_ready = sem("root_ready")
        xn_ready = sem("xn_ready")
        xn_T = sem("xn_T")
        xT_act = sem("xT_act")
        xT_dve = sem("xT_dve")
        gates_mm = sem("gates_mm")
        gates_read = sem("gates_read")
        gate_exp = sem("gate_exp")
        gate_pre = sem("gate_pre")
        gate_rows = sem("gate_rows")
        gate_emt = sem("gate_emt")
        gate_cols_mm = sem("gate_cols_mm")
        gate_cols = sem("gate_cols")
        rows_bcast = sem("rows_bcast")
        qk_mm = sem("qk_mm")
        qk_read = sem("qk_read")
        conv_done = sem("conv_done")
        qk_ready = sem("qk_ready")
        vo_mm = sem("vo_mm")
        vo_read = sem("vo_read")
        sc_mm = sem("sc_mm")
        dm_ready = sem("dm_ready")
        wt_ready = sem("wt_ready")
        s_ready = sem("s_ready")
        pv_mm = sem("pv_mm")
        h_ready = sem("h_ready")
        hsq = sem("hsq")
        hms = sem("hms")
        hroot = sem("hroot")
        y_ready = sem("y_ready")
        y_T = sem("y_T")
        yT_act = sem("yT_act")
        yT_dve = sem("yT_dve")
        mix_mm = sem("mix_mm")
        res_done = sem("res_done")
        log_mm = sem("log_mm")
        gneg = sem("gneg")
        gsum = sem("gsum")
        ediff = sem("ediff")
        eexp = sem("eexp")
        gate_ready = sem("gate_ready")
        acc_zero = sem("acc_zero")
        gu_mm = sem("gu_mm")
        silu_done = sem("silu_done")
        a_ready = sem("a_ready")
        a_T = sem("a_T")
        aT_ready = sem("aT_ready")
        moe_mm = sem("moe_mm")
        down_mm = sem("down_mm")
        lam_p = sem("lam_p")
        lam_e = sem("lam_e")
        asc_mm = sem("asc_mm")
        asc_masked = sem("asc_masked")
        asc_max = sem("asc_max")
        aex = sem("aex")
        aw_ready = sem("aw_ready")
        aw_T = sem("aw_T")
        awT_ready = sem("awT_ready")
        apv = sem("apv")
        apv_read = sem("apv_read")
        out_ready = sem("out_ready")
        out_stored = sem("out_stored")

        wm_in = ml_w_in[0].rearrange("(p c) n -> p c n", c=DC)
        wd_in = da_w_in[0].rearrange("(p c) n -> p c n", c=DC)
        wm_out = ml_w_out[0].rearrange("(c p) n -> p c n", p=P)
        wd_out = da_w_out[0].rearrange("(c p) n -> p c n", p=P)

        def unit(u):
            return ring[:, u % RING, :]

        def unit_is_there(eng, u):
            eng.wait_ge(unit_loaded[u % RING], 16 * (u // RING + 1))

        block = ctx.enter_context(nc.Block())

        @block.sync
        def _(sp):
            def load(u, src, shape):
                if u >= RING:
                    sp.wait_ge(unit_used, u - RING + 1)
                dst = unit(u).rearrange("p (c n) -> p c n", c=shape)
                sp.dma_start(dst, src).then_inc(unit_loaded[u % RING], 16)

            def load_in(u0, w, blocks):
                for nb in range(blocks):
                    for k in range(2):
                        load(u0 + 2 * nb + k, w[:, 4 * k:4 * k + 4, nb * 512:(nb + 1) * 512], 4)

            def load_out(u0, w, units):
                for k in range(units):
                    load(u0 + k, w[:, 2 * k:2 * k + 2, :], 2)

            def load_moe(u0, layer):
                gu = moe_w_gu[layer].rearrange("e (p c) f -> e p c f", c=DC)
                dn = moe_w_down[layer].rearrange("e (p c) n -> e p c n", c=2)
                with sp.Fori(0, TURNS) as turn:
                    for j in range(EB):
                        for k in range(UE):
                            u = u0 + UE * j + k
                            e = bass.ds(turn * EB + j, 1)
                            src = gu[e, :, 4 * k:4 * k + 4, :] if k < 2 else dn[e, :, :, :]
                            sp.wait_ge(unit_used, turn * RING + (u - RING + 1))
                            sp.dma_start(unit(u).rearrange("p (c n) -> p c n", c=src.shape[2]),
                                         src.rearrange("e p c f -> (e p) c f")
                                         ).then_inc(unit_loaded[u % RING], 16)

            load_in(0, wm_in, U_ML_IN // 2)
            load_out(U0_ML_OUT, wm_out, U_ML_OUT)
            load_moe(U0_MOE0, 0)
            load_in(U0_DA_IN, wd_in, U_DA_IN // 2)
            load_out(U0_DA_OUT, wd_out, U_DA_OUT)
            load_moe(U0_MOE1, 1)
            for i in range(NT):
                sp.wait_ge(out_ready, i + 1)
                sp.dma_start(out[0, i * P:(i + 1) * P, :], xn[:, i, :]).then_inc(out_stored, 16)
            sp.wait_ge(out_stored, 16 * NT)

        @block.gpsimd
        def _(pool):
            pool.dma_start(par_rows[C_CONV:C_MLN, :], ml_conv[0].rearrange("j (c p) -> (j c) p", p=P)).then_inc(par_loaded, 16)
            pool.dma_start(par_rows[C_MLN:C_DAN, :], ml_norm[0].rearrange("(c p) -> c p", p=P)).then_inc(par_loaded, 16)
            pool.dma_start(par_rows[C_DAN:N_COLS, :], da_norm).then_inc(par_loaded, 16)
            steps = [0]

            def done(ins):
                steps[0] += 1
                ins.then_inc(pool_step, 1)
                pool.wait_ge(pool_step, steps[0])

            done(nc.gpsimd.memset(ident[:], 0.0))
            done(nc.gpsimd.affine_select(out=ident[:], in_=ident[:], compare_op=ALU.not_equal, fill=1.0,
                                         base=0, pattern=[[-1, P]], channel_multiplier=1))
            done(nc.gpsimd.memset(neg_ts[:], 0.0))
            done(nc.gpsimd.affine_select(out=neg_ts[:], in_=neg_ts[:], compare_op=ALU.is_ge, fill=-BIG,
                                         base=0, pattern=[[1, P]], channel_multiplier=-1))
            done(nc.gpsimd.memset(neg_qk[:], 0.0))
            done(nc.gpsimd.affine_select(out=neg_qk[:, P:T], in_=neg_qk[:, P:T], compare_op=ALU.is_ge,
                                         fill=-BIG, base=0, pattern=[[-1, P]], channel_multiplier=1))
            done(nc.gpsimd.memset(head_sel[:], 0.0))
            done(nc.gpsimd.affine_select(out=head_sel[:], in_=head_sel[:], compare_op=ALU.not_equal,
                                         fill=1.0, base=0, pattern=[[-1, HM], [0, P]], channel_multiplier=1))
            done(nc.gpsimd.iota(rank_w[:], [[-1, E]], base=E, channel_multiplier=0,
                                allow_small_or_imprecise_dtypes=True))
            done(nc.gpsimd.memset(ones[:], 1.0))
            done(nc.gpsimd.memset(eps_col[:, 0:1], EPS))
            nc.gpsimd.memset(eps_col[:, 1:2], DA_EPS).then_inc(tables_made, 1)

        @block.scalar
        def _(act):
            for i in range(NT):
                act.dma_start(xres[:, i, :], x[0, i * P:(i + 1) * P, :]).then_inc(x_loaded, 16)
            act.dma_start(g_mix[:], norm_mix.rearrange("l (p c) -> p l c", c=DC)).then_inc(consts_loaded, 16)
            act.dma_start(w_gate[:], wm_in[:, :, U_ML_IN // 2 * 512:]).then_inc(consts_loaded, 16)
            act.dma_start(b_i[:], ml_b_i.rearrange("o h -> h o")).then_inc(consts_loaded, 16)
            act.dma_start(b_f[:], ml_b_f.rearrange("o h -> h o")).then_inc(consts_loaded, 16)
            act.dma_start(g_ffn[:], norm_ffn.rearrange("l (p c) -> p l c", c=DC)).then_inc(consts_loaded, 16)
            act.dma_start(g_fin[:], final_norm.rearrange("(o d) -> o d", o=1).to_broadcast([P, D])).then_inc(consts_loaded, 16)
            for layer in range(2):
                act.dma_start(w_rout[:, layer, :, 0:G], moe_w_group[layer].rearrange("(p c) g -> p c g", c=DC)).then_inc(consts_loaded, 16)
                act.dma_start(w_rout[:, layer, :, G:], moe_w_expert[layer].rearrange("(p c) g -> p c g", c=DC)).then_inc(consts_loaded, 16)
                for i in range(NT):
                    act.dma_start(b_rout[:, layer, i, 0:G], moe_b_group[layer:layer + 1, :].to_broadcast([P, G])).then_inc(consts_loaded, 16)
                    act.dma_start(b_rout[:, layer, i, G:], moe_b_expert[layer:layer + 1, :].to_broadcast([P, E])).then_inc(consts_loaded, 16)
            for n, src in enumerate((da_lq1, da_lk1, da_lq2, da_lk2)):
                act.dma_start(lam_in[:, n, :], src.to_broadcast([P, DH])).then_inc(consts_loaded, 16)

            def norm(n):
                for i in range(NT):
                    if n == 0:
                        act.wait_ge(x_loaded, 16 * NT)
                    else:
                        act.wait_ge(res_done, 4 * n)
                    nc.scalar.activation(xn[:, i, :], xres[:, i, :], ACT.Square,
                                         accum_out=st[:, i:i + 1]).then_inc(squares, 1)
                act.wait_ge(ms_ready, n + 1)
                nc.scalar.activation(st[:, 4:4 + NT], st[:, 2:2 + NT], ACT.Sqrt).then_inc(root_ready, 1)

            def evac_T(n, g_col):
                for b in range(0, DC // 2, 2):
                    act.wait_ge(xn_T, 4 * n + b + 1)
                    for c in (2 * b, 2 * b + 1):
                        nc.scalar.mul(xT[:, c, :], ps[:, 4 + b, c % 2 * T:(c % 2 + 1) * T], g_col[:, c:c + 1]).then_inc(xT_act, 1)

            norm(0)
            act.wait_ge(consts_loaded, CONSTS)
            evac_T(0, g_mix[:, 0, :])
            act.wait_ge(gate_pre, 1)
            nc.scalar.activation(gr[:, 2, :], gr[:, 1, :], ACT.Exp, scale=-1.0).then_inc(act_step, 1)
            act.wait_ge(act_step, 1)
            nc.scalar.activation(gr[:, 3, :], gr[:, 2, :], ACT.Ln, bias=1.0).then_inc(gate_exp, 1)
            act.wait_ge(gate_rows, 1)
            nc.scalar.activation(gr[:, 7, :], gr[:, 6, :], ACT.Exp, scale=-1.0).then_inc(gate_emt, 1)
            for c in range(QC):
                act.wait_ge(conv_done, c + 1)
                nc.scalar.activation(qkT[:, c, :], conv_u[:, c % 2, :], ACT.Silu).then_inc(qk_ready, 1)
            for hb in range(HM):
                for i in range(NT):
                    act.wait_ge(vo_mm, 2 * hb + i + 1)
                    nc.scalar.copy(v_sb[:, i, hb * DV:(hb + 1) * DV], ps[:, (2 * hb + i) % 8, :]).then_inc(vo_read, 1)
            for hb in range(HM):
                for i in range(NT):
                    act.wait_ge(vo_mm, 8 + 2 * hb + i + 1)
                    nc.scalar.activation(og[:, i, hb * DV:(hb + 1) * DV], ps[:, (2 * hb + i) % 8, :],
                                         ACT.Sigmoid).then_inc(vo_read, 1)
            act.wait_ge(gate_cols, 1)
            for h in range(HM):
                act.wait_ge(dm_ready, h + 1)
                nc.scalar.activation(wT[:, h % 2, 0:256], wT[:, h % 2, 0:256], ACT.Exp, bias=gc[:, 0, h:h + 1]).then_inc(wt_ready, 1)
                nc.scalar.activation(wT[:, h % 2, 256:384], wT[:, h % 2, 256:384], ACT.Exp, bias=gc[:, 1, h:h + 1]).then_inc(wt_ready, 1)
                for i in range(NT):
                    k = 2 * h + i
                    act.wait_ge(h_ready, k + 1)
                    nc.scalar.activation(xn[:, i, 0:DV], work[:, i, :], ACT.Square,
                                         accum_out=st[:, 8 + i:9 + i]).then_inc(hsq, 1)
                act.wait_ge(hms, h + 1)
                nc.scalar.activation(st[:, 12:14], st[:, 10:12], ACT.Sqrt).then_inc(hroot, 1)
            for b in range(0, VC // 2, 2):
                act.wait_ge(y_T, b + 1)
                for c in (2 * b, 2 * b + 1):
                    nc.scalar.mul(yT[:, c, :], ps[:, 4 + b % 4, c % 2 * T:(c % 2 + 1) * T], par[:, C_MLN + c:C_MLN + c + 1]).then_inc(yT_act, 1)

            def moe(layer):
                n = 2 * layer + 1
                norm(n)
                evac_T(n, g_ffn[:, layer, :])
                act.wait_ge(gneg, layer + 1)
                for i in range(NT):
                    nc.scalar.activation(rt[:, 0, i, 0:G], lg[:, i, 0:G], ACT.Exp, bias=st[:, 18 + i:19 + i],
                                         accum_out=st[:, 20 + i:21 + i]).then_inc(gsum, 1)
                act.wait_ge(ediff, layer + 1)
                nc.scalar.activation(st[:, 28:30], st[:, 26:28], ACT.Exp).then_inc(eexp, 1)
                with act.Fori(0, TURNS) as turn:
                    for j in range(EB):
                        for i in range(NT):
                            k = 2 * j + i
                            step = turn * (2 * EB) + (layer * 2 * E + k)
                            act.wait_ge(gu_mm, step + 1)
                            act.wait_ge(a_ready, step + 1)
                            nc.scalar.activation(sg_sb[:, k % 2, :], ps[:, 4 + k % 2, 0:F], ACT.Silu).then_inc(silu_done, 1)
                            act.wait_ge(a_T, step + 3)
                            nc.scalar.copy(aT[:, k % 2, :, :], ps[:, 6 + k % 2, 0:2 * P].rearrange("p (c t) -> p c t", c=2)).then_inc(aT_ready, 1)

            act.sem_inc(aT_ready, 2)
            moe(0)
            act.wait_ge(lam_p, 2)
            nc.scalar.activation(lam_s[:, 2:4], lam_s[:, 0:2], ACT.Exp).then_inc(lam_e, 1)
            norm(2)
            evac_T(2, g_mix[:, 1, :])
            for c in range(QC):
                act.wait_ge(qk_mm, QC + c + 1)
                nc.scalar.copy(qkT[:, c, :], ps[:, c % 8, 0:T]).then_inc(qk_ready, 1)
            for hb in range(2):
                for i in range(NT):
                    act.wait_ge(vo_mm, 16 + 2 * hb + i + 1)
                    nc.scalar.copy(vA[:, i, hb * 512:(hb + 1) * 512], ps[:, (2 * hb + i) % 8, :]).then_inc(vo_read, 1)
            for h in range(HA):
                for i in range(NT):
                    s = 2 * h + i
                    kn = P * (i + 1)
                    act.wait_ge(asc_max, s + 1)
                    for c in range(2):
                        nc.scalar.activation(work[:, s % 2, c * T:c * T + kn], work[:, s % 2, c * T:c * T + kn], ACT.Exp,
                                             bias=st[:, 32 + 2 * (s % 2) + c:33 + 2 * (s % 2) + c], scale=DH ** -0.5,
                                             accum_out=st[:, 36 + 2 * (s % 2) + c:37 + 2 * (s % 2) + c]).then_inc(aex, 1)
                act.wait_ge(aw_T, h + 1)
                nc.scalar.copy(sT[:, h % 2, :], ps[:, 4 + h % 2, 0:384]).then_inc(awT_ready, 1)
                act.wait_ge(apv, h + 1)
                for i in range(NT):
                    nc.scalar.activation(conv_u[:, 0, 0:DVA], ps[:, 6 + h % 2, i * P:(i + 1) * P], ACT.Square,
                                         accum_out=st[:, 40 + HA * i + h:41 + HA * i + h]).then_inc(act_step, 1)
                    act.wait_ge(act_step, 1 + 2 * h + i + 1)
                nc.scalar.copy(og[:, 0:2, h * DVA:(h + 1) * DVA], ps[:, 6 + h % 2, 0:2 * P].rearrange("p (i v) -> p i v", i=2)).then_inc(apv_read, 1)
            act.wait_ge(hms, HM + 1)
            nc.scalar.activation(st[:, 40:56], st[:, 40:56], ACT.Sqrt).then_inc(hroot, 1)
            for b in range(0, HA // 2, 2):
                act.wait_ge(y_T, VC // 2 + b + 1)
                for c in (2 * b, 2 * b + 1):
                    nc.scalar.mul(yT[:, c, :], ps[:, 4 + b % 4, c % 2 * T:(c % 2 + 1) * T], lam_s[:, 6:7]).then_inc(yT_act, 1)
            moe(1)
            norm(4)

        @block.vector
        def _(dve):
            steps = [0]

            def done(ins):
                steps[0] += 1
                ins.then_inc(dve_step, 1)
                dve.wait_ge(dve_step, steps[0])

            def norm(n):
                dve.wait_ge(squares, NT * (n + 1))
                nc.vector.tensor_scalar(st[:, 2:4], st[:, 0:2], 1.0 / D, EPS, ALU.mult, ALU.add).then_inc(ms_ready, 1)
                dve.wait_ge(root_ready, n + 1)
                done(nc.vector.reciprocal(st[:, 6:8], st[:, 4:6]))
                for i in range(NT):
                    if n < 4:
                        nc.vector.tensor_scalar(xn[:, i, :], xres[:, i, :], st[:, 6 + i:7 + i], None, ALU.mult).then_inc(xn_ready, 1)
                    else:
                        nc.vector.scalar_tensor_tensor(out=xn[:, i, :], in0=xres[:, i, :], scalar=st[:, 6 + i:7 + i],
                                                       in1=g_fin[:], op0=ALU.mult, op1=ALU.mult).then_inc(out_ready, 1)

            def evac_T(n, g_col):
                for b in range(1, DC // 2, 2):
                    dve.wait_ge(xn_T, 4 * n + b + 1)
                    for c in (2 * b, 2 * b + 1):
                        nc.vector.tensor_scalar(xT[:, c, :], ps[:, 4 + b, c % 2 * T:(c % 2 + 1) * T], g_col[:, c:c + 1], None,
                                                ALU.mult).then_inc(xT_dve, 1)

            def residual(n, signal, count):
                dve.wait_ge(signal, count)
                for i in range(NT):
                    for half in range(2):
                        sl = xres[:, i, half * 512:(half + 1) * 512]
                        nc.vector.tensor_tensor(sl, sl, ps[:, 2 * i + half, :], ALU.add).then_inc(res_done, 1)

            dve.wait_ge(par_T, 1)
            nc.vector.tensor_copy(par[:], ps[:, 0, 0:N_COLS]).then_inc(par_ready, 1)
            norm(0)
            dve.wait_ge(consts_loaded, CONSTS)
            evac_T(0, g_mix[:, 0, :])
            dve.wait_ge(gates_mm, 1)
            nc.vector.tensor_scalar(gr[:, 0, :], ps[0:HM, 7, 0:T], b_i[:, 0:1], None, ALU.add).then_inc(gates_read, 1)
            nc.vector.tensor_scalar(gr[:, 4, :], ps[0:HM, 7, T:2 * T], b_f[:, 0:1], None, ALU.add).then_inc(gates_read, 1)
            dve.wait_ge(gates_read, 2)
            done(nc.vector.tensor_scalar(gr[:, 5, :], gr[:, 4, :], -1.0, None, ALU.mult))
            nc.vector.tensor_tensor(gr[:, 1, :], gr[:, 4, :], gr[:, 5, :], ALU.max).then_inc(gate_pre, 1)
            dve.wait_ge(gate_exp, 1)
            done(nc.vector.scalar_tensor_tensor(out=gr[:, 4, :], in0=gr[:, 4, :], scalar=0.0, in1=gr[:, 3, :],
                                                op0=ALU.min, op1=ALU.subtract))
            done(nc.vector.memset(gr[:, 3, :], 0.0))
            done(nc.vector.tensor_tensor_scan(gr[:, 2, :], gr[:, 4, :], gr[:, 3, :], 0.0, ALU.add, ALU.add))
            done(nc.vector.tensor_tensor(gr[:, 5, :], gr[:, 0, :], gr[:, 2, :], ALU.subtract))
            done(nc.vector.tensor_tensor_scan(gr[:, 4, :], gr[:, 5, :], gr[:, 3, :], 0.0, ALU.max, ALU.max))
            done(nc.vector.tensor_scalar(gr[:, 1, :], gr[:, 4, :], -1.0, None, ALU.mult))
            nc.vector.tensor_tensor(gr[:, 6, :], gr[:, 4, :], gr[:, 2, :], ALU.add).then_inc(gate_rows, 1)
            dve.wait_ge(par_ready, 1)
            for c in range(QC):
                u = conv_u[:, c % 2, :]
                src = ps[:, c % 8, 0:T]
                dve.wait_ge(qk_mm, c + 1)
                if c >= 2:
                    dve.wait_ge(qk_ready, c - 1)
                for tap in range(TAPS - 1, -1, -1):
                    lag = TAPS - 1 - tap
                    w = par[:, C_CONV + tap * QC + c:C_CONV + tap * QC + c + 1]
                    if lag == 0:
                        done(nc.vector.tensor_scalar(u, src, w, None, ALU.mult))
                        continue
                    ins = nc.vector.scalar_tensor_tensor(out=u[:, lag:T], in0=src[:, 0:T - lag], scalar=w,
                                                         in1=u[:, lag:T], op0=ALU.mult, op1=ALU.add)
                    if lag < TAPS - 1:
                        done(ins)
                    else:
                        ins.then_inc(conv_done, 1)
            dve.wait_ge(gate_cols_mm, 1)
            nc.vector.tensor_copy(gc[:], ps[:, 7, 0:NT * 2 * HM].rearrange("p (i k) -> p i k", i=NT)).then_inc(gate_cols, 1)
            dve.wait_ge(rows_bcast, 1)
            dve.wait_ge(gate_cols, 1)
            for h in range(HM):
                b = h % 2
                R = ps[:, h // 2, (h % 2) * T:(h % 2 + 1) * T]
                if h >= 2:
                    dve.wait_ge(s_ready, h - 1)
                done(nc.vector.tensor_tensor(wT[:, b, 0:P], R[:, 0:P], neg_ts[:], ALU.add))
                done(nc.vector.tensor_copy(wT[:, b, P:T], R[:, P:T]))
                nc.vector.tensor_tensor(wT[:, b, T:T + P], R[:, P:T], neg_ts[:], ALU.add).then_inc(dm_ready, 1)
                dve.wait_ge(sc_mm, h + 1)
                dve.wait_ge(wt_ready, 2 * h + 2)
                if h >= 2:
                    dve.wait_ge(pv_mm, 2 * h - 2)
                nc.vector.scalar_tensor_tensor(out=sT[:, b, :], in0=ps[:, 2 + b, 0:384], scalar=DQK ** -0.5,
                                               in1=wT[:, b, :], op0=ALU.mult, op1=ALU.mult).then_inc(s_ready, 1)
                for i in range(NT):
                    k = 2 * h + i
                    dve.wait_ge(pv_mm, k + 1)
                    den = ps[:, 2 + b, 384 + i:385 + i]
                    done(nc.vector.tensor_copy(st[:, 14:15], den))
                    done(nc.vector.scalar_tensor_tensor(out=st[:, 15:16], in0=st[:, 14:15], scalar=-1.0, in1=st[:, 14:15],
                                                        op0=ALU.mult, op1=ALU.max))
                    done(nc.vector.tensor_tensor(st[:, 16:17], st[:, 15:16], gc[:, i, HM + h:HM + h + 1], ALU.max))
                    done(nc.vector.reciprocal(st[:, 17:18], st[:, 16:17]))
                    nc.vector.tensor_scalar(work[:, i, :], ps[:, 4 + 2 * b + i, :], st[:, 17:18], None, ALU.mult).then_inc(h_ready, 1)
                    dve.wait_ge(h_ready, k + 1)
                dve.wait_ge(hsq, 2 * h + 2)
                nc.vector.tensor_scalar(st[:, 10:12], st[:, 8:10], 1.0 / DV, EPS, ALU.mult, ALU.add).then_inc(hms, 1)
                dve.wait_ge(hroot, h + 1)
                done(nc.vector.reciprocal(st[:, 12:14], st[:, 12:14]))
                for i in range(NT):
                    sl = og[:, i, h * DV:(h + 1) * DV]
                    dve.wait_ge(vo_read, 8 + 2 * h + i + 1)
                    nc.vector.scalar_tensor_tensor(out=sl, in0=work[:, i, :], scalar=st[:, 12 + i:13 + i], in1=sl,
                                                   op0=ALU.mult, op1=ALU.mult).then_inc(y_ready, 1)
                dve.wait_ge(y_ready, 2 * h + 2)
            for b in range(1, VC // 2, 2):
                dve.wait_ge(y_T, b + 1)
                for c in (2 * b, 2 * b + 1):
                    nc.vector.tensor_scalar(yT[:, c, :], ps[:, 4 + b % 4, c % 2 * T:(c % 2 + 1) * T],
                                            par[:, C_MLN + c:C_MLN + c + 1], None, ALU.mult).then_inc(yT_dve, 1)
            residual(0, mix_mm, 1)

            def moe(layer):
                n = 2 * layer + 1
                norm(n)
                evac_T(n, g_ffn[:, layer, :])
                dve.wait_ge(log_mm, layer + 1)
                done(nc.vector.tensor_tensor(lg[:], ps[:, 4, 0:NT * LOGITS].rearrange("p (i k) -> p i k", i=NT),
                                             b_rout[:, layer, :, :], ALU.add))
                gl = lg[:, :, 0:G]
                done(nc.vector.tensor_reduce(st[:, 16:18], gl, AX_X, ALU.max))
                nc.vector.tensor_scalar(st[:, 18:20], st[:, 16:18], -1.0, None, ALU.mult).then_inc(gneg, 1)

                def first_max(dst, vals, mx, k, tmp):
                    done(nc.vector.tensor_tensor(tmp, vals, mx.rearrange("p (i o) -> p i o", o=1).to_broadcast([P, NT, k]), ALU.is_equal))
                    done(nc.vector.tensor_tensor(tmp, tmp, rank_w[:, E - k:E].rearrange("p (o k) -> p o k", o=1).to_broadcast([P, NT, k]), ALU.mult))
                    done(nc.vector.tensor_reduce(st[:, 22:24], tmp, AX_X, ALU.max))
                    done(nc.vector.tensor_tensor(dst, tmp, st[:, 22:24].rearrange("p (i o) -> p i o", o=1).to_broadcast([P, NT, k]), ALU.is_equal))

                ghot = rt[:, 1, :, 0:G]
                first_max(ghot, gl, st[:, 16:18], G, rt[:, 1, :, G:2 * G])
                done(nc.vector.tensor_scalar(rt[:, 1, :, 8:8 + G], ghot, 1.0, BIG, ALU.subtract, ALU.mult))
                m32 = rt[:, 2, :, :]
                for i in range(NT):
                    done(nc.vector.tensor_tensor(m32[:, i, :].rearrange("p (g e) -> p g e", g=G),
                                                 lg[:, i, G:].rearrange("p (g e) -> p g e", g=G),
                                                 rt[:, 1, i, 8:8 + G].rearrange("p (g o) -> p g o", o=1).to_broadcast([P, G, EG]), ALU.add))
                done(nc.vector.tensor_reduce(st[:, 24:26], m32, AX_X, ALU.max))
                first_max(rt[:, 3, :, :], m32, st[:, 24:26], E, rt[:, 5, :, :])
                done(nc.vector.scalar_tensor_tensor(out=m32, in0=rt[:, 3, :, :], scalar=-2 * BIG, in1=m32, op0=ALU.mult, op1=ALU.add))
                done(nc.vector.tensor_reduce(st[:, 30:32], m32, AX_X, ALU.max))
                first_max(rt[:, 4, :, :], m32, st[:, 30:32], E, rt[:, 5, :, :])
                nc.vector.tensor_tensor(st[:, 26:28], st[:, 30:32], st[:, 24:26], ALU.subtract).then_inc(ediff, 1)
                dve.wait_ge(eexp, layer + 1)
                dve.wait_ge(gsum, 2 * layer + 2)
                done(nc.vector.tensor_scalar(st[:, 24:26], st[:, 28:30], 1.0, None, ALU.add))
                done(nc.vector.tensor_tensor(st[:, 24:26], st[:, 24:26], st[:, 20:22], ALU.mult))
                done(nc.vector.reciprocal(st[:, 16:18], st[:, 24:26]))
                done(nc.vector.tensor_tensor(st[:, 30:32], st[:, 16:18], st[:, 28:30], ALU.mult))
                for i in range(NT):
                    done(nc.vector.tensor_scalar(rt[:, 5, i, :], rt[:, 3, i, :], st[:, 16 + i:17 + i], None, ALU.mult))
                    ins = nc.vector.scalar_tensor_tensor(out=gate[:, i, :], in0=rt[:, 4, i, :], scalar=st[:, 30 + i:31 + i],
                                                         in1=rt[:, 5, i, :], op0=ALU.mult, op1=ALU.add)
                    ins.then_inc(gate_ready, 1)
                nc.vector.memset(ps[:, 0:4, :], 0.0).then_inc(acc_zero, 1)
                dve.wait_ge(gate_ready, 2 * layer + 2)
                with dve.Fori(0, TURNS) as turn:
                    for j in range(EB):
                        for i in range(NT):
                            k = 2 * j + i
                            step = turn * (2 * EB) + (layer * 2 * E + k)
                            dve.wait_ge(silu_done, step + 1)
                            dve.wait_ge(a_T, step + 1)
                            nc.vector.scalar_tensor_tensor(out=a_sb[:, k % 2, :], in0=sg_sb[:, k % 2, :],
                                                           scalar=gate[:, i, bass.ds(turn * EB + j, 1)],
                                                           in1=ps[:, 4 + k % 2, F:2 * F],
                                                           op0=ALU.mult, op1=ALU.mult).then_inc(a_ready, 1)
                residual(n, moe_mm, layer + 1)

            dve.sem_inc(a_ready, 2)
            moe(0)
            for n in range(2):
                nc.vector.tensor_tensor_reduce(out=work[:, 0, n * DH:(n + 1) * DH], in0=lam_in[:, 2 * n, :], in1=lam_in[:, 2 * n + 1, :],
                                               scale=1.0, scalar=0.0, op0=ALU.mult, op1=ALU.add,
                                               accum_out=lam_s[:, n:n + 1]).then_inc(lam_p, 1)
            dve.wait_ge(lam_e, 1)
            done(nc.vector.tensor_tensor(lam_s[:, 4:5], lam_s[:, 3:4], lam_s[:, 2:3], ALU.subtract))
            done(nc.vector.tensor_scalar(lam_s[:, 5:6], lam_s[:, 4:5], -LAMBDA_INIT, None, ALU.add))
            done(nc.vector.tensor_scalar(lam_s[:, 6:7], par[:, C_DAN:C_DAN + 1], 1.0 - LAMBDA_INIT, None, ALU.mult))
            norm(2)
            evac_T(2, g_mix[:, 1, :])
            for h in range(HA):
                for i in range(NT):
                    s = 2 * h + i
                    kn = P * (i + 1)
                    b = s % 2
                    sc = work[:, b, :].rearrange("p (c k) -> p c k", c=2)
                    dve.wait_ge(asc_mm, s + 1)
                    for c in range(2):
                        nc.vector.tensor_tensor(sc[:, c, 0:kn], ps[:, 2 * b + c, 0:kn], neg_qk[:, T - kn:T], ALU.add).then_inc(asc_masked, 1)
                    dve.wait_ge(asc_masked, 2 * s + 2)
                    done(nc.vector.tensor_reduce(st[:, 8:10], sc[:, :, 0:kn], AX_X, ALU.max))
                    nc.vector.tensor_scalar(st[:, 32 + 2 * b:34 + 2 * b], st[:, 8:10], -DH ** -0.5, None, ALU.mult).then_inc(asc_max, 1)
                    dve.wait_ge(aex, 2 * s + 2)
                    done(nc.vector.reciprocal(st[:, 10:12], st[:, 36 + 2 * b:38 + 2 * b]))
                    done(nc.vector.tensor_scalar(st[:, 12:13], st[:, 11:12], lam_s[:, 5:6], None, ALU.mult))
                    done(nc.vector.tensor_scalar(sc[:, 0, 0:kn], sc[:, 0, 0:kn], st[:, 10:11], None, ALU.mult))
                    if s >= 2:
                        dve.wait_ge(aw_T, h)
                    nc.vector.scalar_tensor_tensor(out=wT[:, i, 0:kn], in0=sc[:, 1, 0:kn], scalar=st[:, 12:13], in1=sc[:, 0, 0:kn],
                                                   op0=ALU.mult, op1=ALU.add).then_inc(aw_ready, 1)
                    dve.wait_ge(aw_ready, s + 1)
            dve.wait_ge(apv_read, HA)
            nc.vector.tensor_scalar(st[:, 40:56], st[:, 40:56], 1.0 / DVA, DA_EPS, ALU.mult, ALU.add).then_inc(hms, 1)
            dve.wait_ge(hroot, HM + 1)
            done(nc.vector.reciprocal(st[:, 40:56], st[:, 40:56]))
            for i in range(NT):
                o = og[:, i, 0:HA * DVA].rearrange("p (h v) -> p h v", h=HA)
                r = st[:, 40 + HA * i:40 + HA * (i + 1)].rearrange("p (h o) -> p h o", o=1).to_broadcast([P, HA, DVA])
                nc.vector.tensor_tensor(o, o, r, ALU.mult).then_inc(y_ready, 1)
            for b in range(1, HA // 2, 2):
                dve.wait_ge(y_T, VC // 2 + b + 1)
                for c in (2 * b, 2 * b + 1):
                    nc.vector.tensor_scalar(yT[:, c, :], ps[:, 4 + b % 4, c % 2 * T:(c % 2 + 1) * T], lam_s[:, 6:7], None,
                                            ALU.mult).then_inc(yT_dve, 1)
            residual(2, mix_mm, 2)
            moe(1)
            norm(4)

        @block.tensor
        def _(pe):
            pe.wait_ge(tables_made, 1)
            pe.wait_ge(par_loaded, 48)
            pe.transpose(ps[:, 0, 0:N_COLS], par_rows[:], ident[0:N_COLS, 0:N_COLS]).then_inc(par_T, 1)

            def input_T(n):
                if n:
                    pe.wait_ge(res_done, 4 * n)
                for c in range(DC):
                    for i in range(NT):
                        if c == 0:
                            pe.wait_ge(xn_ready, NT * n + i + 1)
                        col = (c % 2) * T + i * P
                        mm = pe.transpose(ps[:, 4 + c // 2, col:col + P], xn[:, i, c:D:DC], ident[:])
                    if c % 2:
                        mm.then_inc(xn_T, 1)
                pe.wait_ge(xT_act, 4 * (n + 1))
                pe.wait_ge(xT_dve, 4 * (n + 1))

            def block_w(u0, nb, c):
                u = u0 + 2 * nb + c // 4
                unit_is_there(pe, u)
                return unit(u)[:, (c % 4) * 512:(c % 4 + 1) * 512]

            def project_T(u0, read, base, k):
                for nb in range(QC // 4):
                    if nb >= 2:
                        pe.wait_ge(read, base + 4 * (nb - 1))
                    for c in range(DC):
                        w = block_w(u0, nb, c)
                        for cc in range(4):
                            mm = pe.matmul(ps[:, (nb % 2) * 4 + cc, 0:T], w[:, cc * P:(cc + 1) * P], xT[:, c, :],
                                           start=(c == 0), stop=(c == DC - 1))
                            if c == DC - 1:
                                mm.then_inc(qk_mm, 1)
                        if c % 4 == 3:
                            free_unit(mm, c == DC - 1)

            used = [0]

            def free_unit(mm, has_signal):
                if has_signal:
                    pe.wait_ge(qk_mm, used_qk())
                    pe.sem_inc(unit_used, 1)
                else:
                    mm.then_inc(unit_used, 1)

            def used_qk():
                used[0] += 4
                return used[0]

            def project(u0, nb0, blocks, first, waits):
                for b in range(blocks):
                    waits(b)
                    for c in range(DC):
                        w = block_w(u0, nb0 + b, c)
                        for i in range(NT):
                            mm = pe.matmul(ps[:, (2 * b + i) % 8, :], xT[:, c, i * P:(i + 1) * P], w,
                                           start=(c == 0), stop=(c == DC - 1))
                            if c == DC - 1:
                                mm.then_inc(vo_mm, 1)
                        if c == 3:
                            mm.then_inc(unit_used, 1)
                    pe.wait_ge(vo_mm, first + 2 * b + 2)
                    pe.sem_inc(unit_used, 1)

            def output(u0, chunks, T0, n):
                for c in range(chunks):
                    if c % 2 == 0 and c >= 8:
                        pe.wait_ge(yT_dve if c // 2 % 2 else yT_act, T0 + 2 * ((c // 2 - 4) // 2 + 1))
                    for i in range(NT):
                        col = (c % 2) * T + i * P
                        mm = pe.transpose(ps[:, 4 + c // 2 % 4, col:col + P], og[:, i, c * P:(c + 1) * P], ident[:])
                    if c % 2:
                        mm.then_inc(y_T, 1)
                for c in range(chunks):
                    u = u0 + c // 2
                    unit_is_there(pe, u)
                    pe.wait_ge(yT_dve if c // 2 % 2 else yT_act, T0 + 2 * (c // 4) + c % 2 + 1)
                    for i in range(NT):
                        for half in range(2):
                            w = unit(u)[:, (c % 2) * D + half * 512:(c % 2) * D + (half + 1) * 512]
                            mm = pe.matmul(ps[:, 2 * i + half, :], yT[:, c, i * P:(i + 1) * P], w,
                                           start=(c == 0), stop=(c == chunks - 1))
                    if c % 2:
                        mm.then_inc(unit_used, 1)
                pe.wait_ge(unit_used, u0 + chunks // 2)
                pe.sem_inc(mix_mm, 1)

            pe.wait_ge(consts_loaded, CONSTS)
            input_T(0)
            for g in range(2):
                for c in range(DC):
                    mm = pe.matmul(ps[0:HM, 7, g * T:(g + 1) * T], w_gate[:, c, g * HM:(g + 1) * HM], xT[:, c, :],
                                   start=(c == 0), stop=(c == DC - 1))
            mm.then_inc(gates_mm, 1)
            pe.wait_ge(par_ready, 1)
            pe.wait_ge(gates_read, 2)
            project_T(0, conv_done, 0, 0)

            def v_waits(b):
                pe.wait_ge(conv_done, 12 if b < 2 else 16)
            project(0, 4, 4, 0, v_waits)
            project(0, 8, 4, 8, lambda b: pe.wait_ge(vo_read, 2 * b + 2))
            pe.wait_ge(vo_read, 16)
            pe.wait_ge(gate_rows, 1)
            pe.wait_ge(gate_emt, 1)
            for i in range(NT):
                for k, row in enumerate((5, 7)):
                    mm = pe.transpose(ps[:, 7, (2 * i + k) * HM:(2 * i + k + 1) * HM], gr[:, row, i * P:(i + 1) * P], ident[0:HM, 0:HM])
            mm.then_inc(gate_cols_mm, 1)
            for h in range(HM):
                mm = pe.matmul(ps[:, h // 2, (h % 2) * T:(h % 2 + 1) * T], head_sel[:, h, :], gr[:, 1, :], start=True, stop=True)
            mm.then_inc(rows_bcast, 1)
            pe.wait_ge(gate_cols, 1)
            pe.wait_ge(qk_ready, QC)
            for h in range(HM):
                b = h % 2
                if h >= 2:
                    pe.wait_ge(h_ready, 2 * h - 2)
                for s in range(2):
                    for c in range(2):
                        q, k = qkT[:, 2 * h + c, s * P:T], qkT[:, QC // 2 + 2 * h + c, s * P:(s + 1) * P]
                        mm = pe.matmul(ps[:, 2 + b, s * T:s * T + T - s * P], k, q, start=(c == 0), stop=(c == 1))
                mm.then_inc(sc_mm, 1)
                pe.wait_ge(s_ready, h + 1)
                for i in range(NT):
                    for s in range(i + 1):
                        lhs = sT[:, b, (i + s) * P:(i + s + 1) * P]
                        pe.matmul(ps[:, 2 + b, 384 + i:385 + i], lhs, ones[:, 0:1], start=(s == 0), stop=(s == i))
                for i in range(NT):
                    for s in range(i + 1):
                        lhs = sT[:, b, (i + s) * P:(i + s + 1) * P]
                        mm = pe.matmul(ps[:, 4 + 2 * b + i, :], lhs, v_sb[:, s, h * DV:(h + 1) * DV], start=(s == 0), stop=(s == i))
                    mm.then_inc(pv_mm, 1)
            pe.wait_ge(y_ready, 2 * HM)
            output(U0_ML_OUT, VC, 0, 0)

            def moe(layer, u0):
                input_T(2 * layer + 1)
                for i in range(NT):
                    for c in range(DC):
                        mm = pe.matmul(ps[:, 4, i * LOGITS:(i + 1) * LOGITS], xT[:, c, i * P:(i + 1) * P], w_rout[:, layer, c, :],
                                       start=(c == 0), stop=(c == DC - 1))
                mm.then_inc(log_mm, 1)
                pe.wait_ge(acc_zero, layer + 1)
                with pe.Fori(0, TURNS) as turn:
                    for j in range(EB):
                        for i in range(NT):
                            k = 2 * j + i
                            step = turn * (2 * EB) + (layer * 2 * E + k)
                            pe.wait_ge(a_ready, step + 1)
                            for c in range(DC):
                                u = u0 + UE * j + c // 4
                                if i == 0 and c % 4 == 0:
                                    pe.wait_ge(unit_loaded[u % RING], turn * 16 + 16 * (u // RING + 1))
                                mm = pe.matmul(ps[:, 4 + k % 2, :], xT[:, c, i * P:(i + 1) * P],
                                               unit(u)[:, (c % 4) * 512:(c % 4 + 1) * 512], start=(c == 0), stop=(c == DC - 1))
                            mm.then_inc(gu_mm, 1)
                        pe.wait_ge(gu_mm, turn * (2 * EB) + (layer * 2 * E + 2 * j + 2))
                        pe.sem_inc(unit_used, 2)
                        for i in range(NT):
                            k = 2 * j + i
                            step = turn * (2 * EB) + (layer * 2 * E + k)
                            u = u0 + UE * j + 2
                            pe.wait_ge(a_ready, step + 3)
                            pe.wait_ge(aT_ready, step + 1)
                            for c in range(2):
                                mm = pe.transpose(ps[:, 6 + k % 2, c * P:(c + 1) * P], a_sb[:, k % 2, c:F:2], ident[:])
                            mm.then_inc(a_T, 1)
                            if i == 0:
                                pe.wait_ge(unit_loaded[u % RING], turn * 16 + 16 * (u // RING + 1))
                            pe.wait_ge(aT_ready, step + 3)
                            for c in range(2):
                                for half in range(2):
                                    mm = pe.matmul(ps[:, 2 * i + half, :], aT[:, k % 2, c, :],
                                                   unit(u)[:, c * D + half * 512:c * D + (half + 1) * 512],
                                                   start=False, stop=False, skip_group_check=True)
                        mm.then_inc(unit_used, 1)
                pe.wait_ge(unit_used, u0 + U_MOE)
                pe.sem_inc(moe_mm, 1)

            pe.sem_inc(a_T, 2)
            moe(0, U0_MOE0)
            input_T(2)
            project_T(U0_DA_IN, qk_ready, QC, 1)
            project(U0_DA_IN, 4, 2, 16, lambda b: pe.wait_ge(qk_ready, QC + 12))
            pe.wait_ge(qk_ready, 2 * QC)
            pe.wait_ge(vo_read, 20)

            def a_scores(s):
                h, i = s // 2, s % 2
                if s >= 2:
                    pe.wait_ge(asc_masked, 2 * s - 2)
                for c in range(2):
                    mm = pe.matmul(ps[:, 2 * (s % 2) + c, 0:P * (i + 1)], qkT[c * DH:(c + 1) * DH, h, i * P:(i + 1) * P],
                                   qkT[c * DH:(c + 1) * DH, HA + h, 0:P * (i + 1)], start=True, stop=True)
                mm.then_inc(asc_mm, 1)

            for s in range(2):
                a_scores(s)
            for h in range(HA):
                if h + 1 < HA:
                    for i in range(NT):
                        a_scores(2 * h + 2 + i)
                pe.wait_ge(aw_ready, 2 * h + 2)
                if h >= 2:
                    pe.wait_ge(awT_ready, h - 1)
                for n, (i, k) in enumerate(((0, 0), (1, 0), (1, 1))):
                    mm = pe.transpose(ps[:, 4 + h % 2, n * P:(n + 1) * P], wT[:, i, k * P:(k + 1) * P], ident[:])
                mm.then_inc(aw_T, 1)
                pe.wait_ge(awT_ready, h + 1)
                if h >= 2:
                    pe.wait_ge(apv_read, h - 1)
                for i in range(NT):
                    for s in range(i + 1):
                        mm = pe.matmul(ps[:, 6 + h % 2, i * P:(i + 1) * P], sT[:, h % 2, (i + s) * P:(i + s + 1) * P],
                                       vA[:, s, h * DVA:(h + 1) * DVA], start=(s == 0), stop=(s == i))
                mm.then_inc(apv, 1)
            pe.wait_ge(y_ready, 2 * HM + 2)
            output(U0_DA_OUT, HA, VC // 2, 2)
            moe(1, U0_MOE1)


CONSTS = 16 * (6 + 2 * 6 + 4)

_INS = ['x', 'norm_mix', 'norm_ffn', 'ml_w_in', 'ml_conv', 'ml_b_i', 'ml_b_f', 'ml_norm', 'ml_w_out',
        'da_w_in', 'da_lq1', 'da_lk1', 'da_lq2', 'da_lk2', 'da_norm', 'da_w_out',
        'moe_w_group', 'moe_b_group', 'moe_w_expert', 'moe_b_expert', 'moe_w_gu', 'moe_w_down', 'final_norm']


def kernel(**inputs):
    import numpy as _np
    import concourse.bacc as _bacc
    from concourse.bass_utils import run_bass_kernel_spmd as _run

    nc = _bacc.Bacc("TRN2", target_bir_lowering=False, num_devices=1)
    arrays, args = {}, []
    for name in _INS:
        a = _np.ascontiguousarray(inputs[name])
        arrays[f"in_{name}_dram"] = a
        args.append(nc.dram_tensor(f"in_{name}_dram", a.shape, mybir.dt.from_np(a.dtype), kind="ExternalInput").ap())
    args.append(nc.dram_tensor("out_0_dram", (1, T, D), F32, kind="ExternalOutput").ap())
    program(nc, *args)
    r = _run(nc, [arrays], core_ids=[0])
    return r.results[0]["out_0_dram"]
```

```python
import math
from contextlib import ExitStack

import concourse.bass as bass
from concourse import mybir

F32 = mybir.dt.float32
F32R = mybir.dt.float32r
I32 = mybir.dt.int32
ALU = mybir.AluOpType
ACT = mybir.ActivationFunctionType
AX_X = mybir.AxisListType.X

P = 128
D = 1024
T = 256
NT = T // P
DC = D // P
EPS = 1e-6
HM = 4
DQK = 256
DV = 512
QC = 2 * HM * DQK // P
VM = HM * DV
VC = VM // P
TAPS = 4
HA = 8
DH = 64
DVA = 128
DA_EPS = 1e-5
G = 4
EG = 8
E = G * EG
F = D // 4
LOGITS = G + E
BIG = 1e30
LAMBDA_INIT = 0.8 - 0.6 * math.exp(-0.3 * 1)

UNIT = 2048
RING = 12
CH = 512
BUFS = 4
AFTER = (2, 4, 6, 7)
W = P
NPOS = 2 * T
LEAD = W
XS = LEAD + NPOS + W
NPC = NPOS // P
UE = 3
EB = RING // UE
TURNS = E // EB
U_ML_IN = 24
U_ML_OUT = 8
U_MOE = UE * E
U_DA_IN = 12
U_DA_OUT = 4
U0_ML_OUT = U_ML_IN
U0_MOE0 = U0_ML_OUT + U_ML_OUT
U0_DA_IN = U0_MOE0 + U_MOE
U0_DA_OUT = U0_DA_IN + U_DA_IN
U0_MOE1 = U0_DA_OUT + U_DA_OUT
U_ALL = U0_MOE1 + U_MOE
SPLIT0 = {"ml_in": 0, "moe0": U_ML_IN, "da_in": U_ML_IN + 2 * E, "moe1": U_ML_IN + 2 * E + U_DA_IN}
WHOLE0 = {"ml_out": 0, "moe0": U_ML_OUT, "da_out": U_ML_OUT + E, "moe1": U_ML_OUT + E + U_DA_OUT}

C_CONV = 0
C_MLN = TAPS * QC
C_DAN = C_MLN + VC
N_COLS = C_DAN + 1


def program(nc, x, norm_mix, norm_ffn, ml_w_in, ml_conv, ml_b_i, ml_b_f, ml_norm, ml_w_out,
            da_w_in, da_lq1, da_lk1, da_lq2, da_lk2, da_norm, da_w_out,
            moe_w_group, moe_b_group, moe_w_expert, moe_b_expert, moe_w_gu, moe_w_down,
            final_norm, out):
    with ExitStack() as ctx:
        def sb(name, shape, dt=F32):
            return ctx.enter_context(nc.sbuf_tensor(name, shape, dt))

        def sem(name):
            return ctx.enter_context(nc.semaphore(name))

        ring = sb("ring", [P, RING, UNIT])
        xres = sb("xres", [P, NT, D])
        xTh = sb("xTh", [P, DC, T], F32R)
        xTl = sb("xTl", [P, DC, T], F32R)
        wh = sb("wh", [P, BUFS, CH], F32R)
        wl = sb("wl", [P, BUFS, CH], F32R)
        big = sb("big", [P, 12 * 1024])
        qkT = big[:, 0:QC * T].rearrange("p (c t) -> p c t", c=QC)
        v_sb = big[:, 4096:8192].rearrange("p (i v) -> p i v", i=NT)
        og = big[:, 8192:12288].rearrange("p (i v) -> p i v", i=NT)
        vA = big[:, 4096:6144].rearrange("p (i v) -> p i v", i=NT)
        yT = big[:, 0:VC * T].rearrange("p (c t) -> p c t", c=VC)
        Xs = big[:, 0:DC * XS].rearrange("p (c s) -> p c s", c=DC)
        Ys = big[:, DC * XS:2 * DC * XS].rearrange("p (c s) -> p c s", c=DC)
        Yn = big[:, 0:NPC * D].rearrange("p (k d) -> p k d", k=NPC)
        xn = big[:, 6144:8192].rearrange("p (i d) -> p i d", i=NT)
        hit = big[:, 8192:9216].rearrange("p (i s) -> p i s", i=NT)
        hit_w = big[:, 9216:10240].rearrange("p (i s) -> p i s", i=NT)
        hit_t = big[:, 10240:10752]
        wk = sb("wk", [P, 2560])
        work = wk[:, 0:1024].rearrange("p (b n) -> p b n", b=2)
        sT = wk[:, 1024:1792].rearrange("p (b n) -> p b n", b=2)
        wT = wk[:, 1792:2560].rearrange("p (b n) -> p b n", b=2)
        hitT = wk[:, 0:1024].rearrange("p (k t) -> p k t", k=NPC)
        a_sb = wk[:, 1024:1536].rearrange("p (b f) -> p b f", b=2)
        sg_sb = wk[:, 1536:2048].rearrange("p (b f) -> p b f", b=2)
        aT = wk[:, 2048:2560].rearrange("p (b c t) -> p b c t", b=2, c=2)
        gr = wk[0:HM, 0:8 * T].rearrange("h (r t) -> h r t", t=T)
        conv_u = sb("conv_u", [P, 2, T])
        iota = conv_u[:, :, :].rearrange("p b t -> p (b t)")
        lam_in = wk[:, 0:4 * DH].rearrange("p (n k) -> p n k", n=4)
        lam_x = wk[:, 4 * DH:6 * DH].rearrange("p (n k) -> p n k", n=2)
        ident = sb("ident", [P, P])
        neg_ts = sb("neg_ts", [P, P])
        neg_qk = sb("neg_qk", [P, T])
        ones = sb("ones", [P, P])
        earlier = sb("earlier", [P, P])
        eps_col = sb("eps_col", [P, 2])
        par_rows = sb("par_rows", [N_COLS, P])
        par = sb("par", [P, N_COLS])
        g_mix = sb("g_mix", [P, 2, DC])
        g_ffn = sb("g_ffn", [P, 2, DC])
        w_gate = sb("w_gate", [P, DC, 2 * HM])
        wg_h = sb("wg_h", [P, DC, 2 * HM], F32R)
        wg_l = sb("wg_l", [P, DC, 2 * HM], F32R)
        wr_h = sb("wr_h", [P, DC, LOGITS], F32R)
        wr_l = sb("wr_l", [P, DC, LOGITS], F32R)
        gn = sb("gn", [P, NT, 2 * HM])
        b_i = sb("b_i", [HM, 1])
        b_f = sb("b_f", [HM, 1])
        w_rout = sb("w_rout", [P, 2, DC, LOGITS])
        b_rout = sb("b_rout", [P, 2, NT, LOGITS])
        lam_s = sb("lam_s", [P, 8])
        st = sb("st", [P, 64])
        gc = sb("gc", [P, NT, 2 * HM])
        lg = sb("lg", [P, NT, LOGITS])
        rt = wk[:, 1024:1024 + 6 * NT * E].rearrange("p (n i e) -> p n i e", n=6, i=NT)
        win = sb("win", [1, 2 * E + 1], I32)
        zeros = sb("zeros", [P, E])
        rank_w = sb("rank_w", [P, E])
        ps = ctx.enter_context(nc.psum_tensor("ps", [P, 8, 512], F32))

        class Pass:
            def __init__(self, tag, unit_loaded, h_made, l_made, chunk_used, whole_used):
                self.unit_loaded = unit_loaded
                self.h_made = h_made
                self.l_made = l_made
                self.chunk_used = chunk_used
                self.whole_used = whole_used
                self.xw_h = sem(tag + "xw_h")
                self.xw_l = sem(tag + "xw_l")
                self.silu_done = sem(tag + "silu_done")
                self.a_ready = sem(tag + "a_ready")
                self.a_T = sem(tag + "a_T")
                self.aT_ready = sem(tag + "aT_ready")
                self.y_act = sem(tag + "y_act")
                self.y_dve = sem(tag + "y_dve")

        def ring_sems(tag):
            return [sem(f"{tag}unit_loaded{i}") for i in range(RING)]

        unit_loaded = ring_sems("")
        h_made = sem("h_made")
        l_made = sem("l_made")
        chunk_used = sem("chunk_used")
        whole_used = sem("whole_used")
        main = Pass("", unit_loaded, h_made, l_made, chunk_used, whole_used)
        again = [Pass(f"again{n}_", ring_sems(f"again{n}_"), sem(f"again{n}_h_made"), sem(f"again{n}_l_made"),
                      sem(f"again{n}_chunk_used"), sem(f"again{n}_whole_used")) for n in range(2)]
        ys_act = sem("ys_act")
        ys_dve = sem("ys_dve")
        small_split = sem("small_split")
        xh_ready = sem("xh_ready")
        xl_ready = sem("xl_ready")
        gates_nat = sem("gates_nat")
        gates_copied = sem("gates_copied")
        pads_zero = sem("pads_zero")
        asg_ready = sem("asg_ready")
        rank_mm = sem("rank_mm")
        win_ready = sem("win_ready")
        hit_ready = sem("hit_ready")
        hitw_ready = sem("hitw_ready")
        gath_mm = sem("gath_mm")
        xs_act = sem("xs_act")
        xs_dve = sem("xs_dve")
        hit_T = sem("hit_T")
        hitT_act = sem("hitT_act")
        hitT_dve = sem("hitT_dve")
        ys_T = sem("ys_T")
        yn_act = sem("yn_act")
        yn_dve = sem("yn_dve")
        comb_mm = sem("comb_mm")
        x_loaded = sem("x_loaded")
        g_mix_loaded = sem("g_mix_loaded")
        conv_tap = sem("conv_tap")
        par_loaded = sem("par_loaded")
        consts_loaded = sem("consts_loaded")
        tables_made = sem("tables_made")
        pool_step = sem("pool_step")
        par_T = sem("par_T")
        par_ready = sem("par_ready")
        act_step = sem("act_step")
        dve_step = sem("dve_step")
        squares = sem("squares")
        ms_ready = sem("ms_ready")
        root_ready = sem("root_ready")
        xn_ready = sem("xn_ready")
        xn_T = sem("xn_T")
        gates_mm = sem("gates_mm")
        gates_read = sem("gates_read")
        gate_exp = sem("gate_exp")
        gate_pre = sem("gate_pre")
        gate_rows = sem("gate_rows")
        gate_emt = sem("gate_emt")
        gate_cols_mm = sem("gate_cols_mm")
        gate_cols = sem("gate_cols")
        rows_bcast = sem("rows_bcast")
        qk_read = sem("qk_read")
        conv_done = sem("conv_done")
        qk_ready = sem("qk_ready")
        vo_read = sem("vo_read")
        sc_mm = sem("sc_mm")
        dm_ready = sem("dm_ready")
        wt_ready = sem("wt_ready")
        s_ready = sem("s_ready")
        pv_mm = sem("pv_mm")
        h_ready = sem("h_ready")
        hsq = sem("hsq")
        hms = sem("hms")
        hroot = sem("hroot")
        y_ready = sem("y_ready")
        y_T = sem("y_T")
        yT_act = sem("yT_act")
        yT_dve = sem("yT_dve")
        res_done = sem("res_done")
        log_mm = sem("log_mm")
        gneg = sem("gneg")
        gsum = sem("gsum")
        ediff = sem("ediff")
        eexp = sem("eexp")
        lam_p = sem("lam_p")
        lam_e = sem("lam_e")
        asc_mm = sem("asc_mm")
        asc_masked = sem("asc_masked")
        asc_max = sem("asc_max")
        aex = sem("aex")
        aw_ready = sem("aw_ready")
        aw_T = sem("aw_T")
        awT_ready = sem("awT_ready")
        apv = sem("apv")
        apv_read = sem("apv_read")
        g_fin_loaded = sem("g_fin_loaded")
        out_ready = sem("out_ready")
        out_stored = sem("out_stored")

        wm_in = ml_w_in[0].rearrange("(p c) n -> p c n", c=DC)
        wd_in = da_w_in[0].rearrange("(p c) n -> p c n", c=DC)
        wm_out = ml_w_out[0].rearrange("(c p) n -> p c n", p=P)
        wd_out = da_w_out[0].rearrange("(c p) n -> p c n", p=P)

        def unit(u):
            return ring[:, u % RING, :]

        def unit_is_there(eng, u):
            eng.wait_ge(unit_loaded[u % RING], 16 * (u // RING + 1))

        def bases(layer, again):
            if again:
                return 0, 0, 0, 0
            stage = f"moe{layer}"
            return (U0_MOE0, U0_MOE1)[layer], 4 * SPLIT0[stage], WHOLE0[stage], layer * E

        def loaded_count(u0, turn, j, k):
            return 16 * ((u0 + UE * j + k) // RING + 1) + turn * 16

        def slot(u0, j, k):
            return ring[:, (u0 + UE * j + k) % RING, :]

        def back(turn, j, n):
            return (turn, j - n) if j >= n else (turn - 1, j - n + EB)

        def window(eng, turn, j, again):
            at = turn * EB + j
            if again:
                at = (2 * E - 1 - j) - turn * EB
            return eng.value_load(win[0:1, bass.ds(at, 1)], min_val=0, max_val=LEAD + NPOS)

        def over_experts(eng, step):
            for j in range(EB):
                step(0, j, True, False)
            with eng.Fori(1, TURNS) as turn:
                for j in range(EB):
                    step(turn, j, False, False)
            step(TURNS, 0, False, True)

        block = ctx.enter_context(nc.Block())

        frees = []
        for split, count in ((1, U_ML_IN), (0, U_ML_OUT), (2, E), (1, U_DA_IN), (0, U_DA_OUT), (2, E)):
            for n in range(count):
                frees += [True, True, False] if split == 2 else [bool(split)]

        def slot_free(sp, u):
            old = u - RING
            if old < 0:
                return
            n = sum(f == frees[old] for f in frees[:old + 1])
            if frees[old]:
                sp.wait_ge(l_made, 4 * n)
            else:
                sp.wait_ge(whole_used, n)

        @block.sync
        def _(sp):
            def load(u, src, shape):
                slot_free(sp, u)
                dst = unit(u).rearrange("p (c n) -> p c n", c=shape)
                sp.dma_start(dst, src).then_inc(unit_loaded[u % RING], 16)

            def load_in(u0, w, blocks):
                for nb in range(blocks):
                    for k in range(2):
                        load(u0 + 2 * nb + k, w[:, 4 * k:4 * k + 4, nb * CH:(nb + 1) * CH], 4)

            def load_out(u0, w, units):
                for k in range(units):
                    load(u0 + k, w[:, 2 * k:2 * k + 2, :], 2)

            def load_moe(layer, s, again):
                gu = moe_w_gu[layer].rearrange("e (p c) f -> e p c f", c=DC)
                dn = moe_w_down[layer].rearrange("e (p c) n -> e p c n", c=2)
                u0, cb, wb, _ = bases(layer, again)

                def load_expert(turn, e, j, peeled):
                    e = bass.ds(e, 1)
                    for k in range(UE):
                        u = u0 + UE * j + k
                        if not peeled and k < 2:
                            sp.wait_ge(s.l_made, turn * (8 * EB) + (cb - 8 * EB + 8 * j + 4 * k + 4))
                        elif not peeled:
                            sp.wait_ge(s.whole_used, turn * EB + (wb - EB + j + 1))
                        elif not again:
                            slot_free(sp, u)
                        src = gu[e, :, 4 * k:4 * k + 4, :] if k < 2 else dn[e, :, :, :]
                        sp.dma_start(slot(u0, j, k).rearrange("p (c n) -> p c n", c=src.shape[2]),
                                     src.rearrange("e p c f -> (e p) c f")).then_inc(s.unit_loaded[u % RING], 16)

                for j in range(EB):
                    load_expert(0, (E - 1 - j) if again else j, j, True)
                with sp.Fori(1, TURNS) as turn:
                    first = sp.snap(turn * -EB + (E - 1) if again else turn * EB)
                    for j in range(EB):
                        load_expert(turn, first - j if again else first + j, j, False)

            def moe(layer):
                load_moe(layer, main, False)
                sp.wait_ge(win_ready, layer + 1)
                most = sp.value_load(win[0:1, 2 * E:2 * E + 1], min_val=0, max_val=T)
                with sp.If(most > W):
                    _, cb, wb, _ = bases(layer, False)
                    sp.wait_ge(l_made, cb + 8 * E)
                    sp.wait_ge(whole_used, wb + E)
                    load_moe(layer, again[layer], True)
                    sp.wait_ge(again[layer].l_made, 8 * E)
                    sp.wait_ge(again[layer].whole_used, E)

            for i in range(NT):
                sp.dma_start(xres[:, i, :], x[0, i * P:(i + 1) * P, :]).then_inc(x_loaded, 16)
            sp.dma_start(g_mix[:], norm_mix.rearrange("l (p c) -> p l c", c=DC)).then_inc(g_mix_loaded, 16)
            load_in(0, wm_in, U_ML_IN // 2)
            load_out(U0_ML_OUT, wm_out, U_ML_OUT)
            moe(0)
            load_in(U0_DA_IN, wd_in, U_DA_IN // 2)
            load_out(U0_DA_OUT, wd_out, U_DA_OUT)
            moe(1)
            sp.wait_ge(res_done, 16)
            sp.dma_start(ring[:, 0, 0:D], final_norm.rearrange("(o d) -> o d", o=1).to_broadcast([P, D])).then_inc(g_fin_loaded, 16)
            for i in range(NT):
                sp.wait_ge(out_ready, i + 1)
                sp.dma_start(out[0, i * P:(i + 1) * P, :], xn[:, i, :]).then_inc(out_stored, 16)
            sp.wait_ge(out_stored, 16 * NT)

        @block.gpsimd
        def _(pool):
            pool.dma_start(par_rows[C_CONV:C_MLN, :], ml_conv[0].rearrange("j (c p) -> (j c) p", p=P)).then_inc(par_loaded, 16)
            pool.dma_start(par_rows[C_MLN:C_DAN, :], ml_norm[0].rearrange("(c p) -> c p", p=P)).then_inc(par_loaded, 16)
            pool.dma_start(par_rows[C_DAN:N_COLS, :], da_norm).then_inc(par_loaded, 16)
            steps = [0]

            def done(ins):
                steps[0] += 1
                ins.then_inc(pool_step, 1)
                pool.wait_ge(pool_step, steps[0])

            done(nc.gpsimd.memset(ident[:], 0.0))
            done(nc.gpsimd.affine_select(out=ident[:], in_=ident[:], compare_op=ALU.not_equal, fill=1.0,
                                         base=0, pattern=[[-1, P]], channel_multiplier=1))
            done(nc.gpsimd.memset(neg_ts[:], 0.0))
            done(nc.gpsimd.affine_select(out=neg_ts[:], in_=neg_ts[:], compare_op=ALU.is_ge, fill=-BIG,
                                         base=0, pattern=[[1, P]], channel_multiplier=-1))
            done(nc.gpsimd.memset(neg_qk[:], 0.0))
            done(nc.gpsimd.affine_select(out=neg_qk[:, P:T], in_=neg_qk[:, P:T], compare_op=ALU.is_ge,
                                         fill=-BIG, base=0, pattern=[[-1, P]], channel_multiplier=1))
            done(nc.gpsimd.memset(earlier[:], 1.0))
            done(nc.gpsimd.affine_select(out=earlier[:], in_=earlier[:], compare_op=ALU.is_gt, fill=0.0,
                                         base=0, pattern=[[1, P]], channel_multiplier=-1))
            done(nc.gpsimd.memset(zeros[:], 0.0))
            done(nc.gpsimd.iota(rank_w[:], [[-1, E]], base=E, channel_multiplier=0,
                                allow_small_or_imprecise_dtypes=True))
            done(nc.gpsimd.memset(ones[:], 1.0))
            done(nc.gpsimd.memset(eps_col[:, 0:1], EPS))
            nc.gpsimd.memset(eps_col[:, 1:2], DA_EPS).then_inc(tables_made, 1)
            for layer in range(2):
                pool.wait_ge(res_done, 4 * (2 * layer + 1))
                nc.gpsimd.iota(iota, [[1, NPOS]], base=0, channel_multiplier=0,
                               allow_small_or_imprecise_dtypes=True).then_inc(pads_zero, 1)
                nc.gpsimd.memset(Xs[:, :, 0:LEAD], 0.0).then_inc(pads_zero, 1)
                nc.gpsimd.memset(Xs[:, :, LEAD + NPOS:XS], 0.0).then_inc(pads_zero, 1)

        @block.scalar
        def _(act):
            act.dma_start(w_gate[:], wm_in[:, :, U_ML_IN // 2 * 512:]).then_inc(consts_loaded, 16)
            act.dma_start(b_i[:], ml_b_i.rearrange("o h -> h o")).then_inc(consts_loaded, 16)
            act.dma_start(b_f[:], ml_b_f.rearrange("o h -> h o")).then_inc(consts_loaded, 16)
            act.dma_start(g_ffn[:], norm_ffn.rearrange("l (p c) -> p l c", c=DC)).then_inc(consts_loaded, 16)
            for layer in range(2):
                act.dma_start(w_rout[:, layer, :, 0:G], moe_w_group[layer].rearrange("(p c) g -> p c g", c=DC)).then_inc(consts_loaded, 16)
                act.dma_start(w_rout[:, layer, :, G:], moe_w_expert[layer].rearrange("(p c) g -> p c g", c=DC)).then_inc(consts_loaded, 16)
                for i in range(NT):
                    act.dma_start(b_rout[:, layer, i, 0:G], moe_b_group[layer:layer + 1, :].to_broadcast([P, G])).then_inc(consts_loaded, 16)
                    act.dma_start(b_rout[:, layer, i, G:], moe_b_expert[layer:layer + 1, :].to_broadcast([P, E])).then_inc(consts_loaded, 16)
            for n, src in enumerate((da_lq1, da_lk1, da_lq2, da_lk2)):
                act.dma_start(lam_in[:, n, :], src.to_broadcast([P, DH])).then_inc(consts_loaded, 16)

            def norm(n):
                for i in range(NT):
                    if n == 0:
                        act.wait_ge(x_loaded, 16 * NT)
                    else:
                        act.wait_ge(res_done, 4 * (n - 1) + 2 * (i + 1))
                    nc.scalar.activation(xn[:, i, :], xres[:, i, :], ACT.Square,
                                         accum_out=st[:, i:i + 1]).then_inc(squares, 1)
                act.wait_ge(ms_ready, n + 1)
                nc.scalar.activation(st[:, 4:4 + NT], st[:, 2:2 + NT], ACT.Sqrt).then_inc(root_ready, 1)

            def evac_T(n, g_col):
                for c in range(DC):
                    act.wait_ge(xn_T, 4 * n + c // 2 + 1)
                    nc.scalar.mul(xTh[:, c, :], ps[:, 4 + c // 2, c % 2 * T:(c % 2 + 1) * T], g_col[:, c:c + 1]).then_inc(xh_ready, 1)

            def make_h(s, ch, c, src):
                if not isinstance(ch, int) or ch >= BUFS:
                    act.wait_ge(s.chunk_used, ch - (BUFS - 1))
                nc.scalar.copy(wh[:, c % BUFS, :], src).then_inc(s.h_made, 1)

            def split_block(u0, ch0, nb, after):
                for c in range(DC):
                    u = u0 + 2 * nb + c // 4
                    if c % 4 == 0:
                        unit_is_there(act, u)
                    make_h(main, ch0 + 8 * nb + c, c, unit(u)[:, c % 4 * CH:(c % 4 + 1) * CH])
                    if nb and c in AFTER:
                        after(nb - 1, AFTER.index(c))

            norm(0)
            act.wait_ge(g_mix_loaded, 16)
            evac_T(0, g_mix[:, 0, :])

            def ml_after(nb, k):
                c = 4 * nb + k
                if nb < 4:
                    act.wait_ge(chunk_used, 8 * (nb + 1))
                    if c >= 2:
                        act.wait_ge(qk_ready, c - 1)
                    w = par[:, C_CONV + (TAPS - 1) * QC + c:C_CONV + (TAPS - 1) * QC + c + 1]
                    nc.scalar.mul(conv_u[:, c % 2, :], ps[:, c % 8, 0:T], w).then_inc(conv_tap, 1)
                if 0 < c <= QC:
                    act.wait_ge(conv_done, c)
                    nc.scalar.activation(qkT[:, c - 1, :], conv_u[:, (c - 1) % 2, :], ACT.Silu).then_inc(qk_ready, 1)
                if nb >= 4 and k % 2 == 0:
                    b, i = (nb - 4) % 4, k // 2
                    act.wait_ge(chunk_used, 8 * (nb + 1))
                    src = ps[:, (2 * b + i) % 8, :]
                    if nb < 8:
                        nc.scalar.copy(v_sb[:, i, b * DV:(b + 1) * DV], src).then_inc(vo_read, 1)
                    else:
                        nc.scalar.activation(og[:, i, b * DV:(b + 1) * DV], src, ACT.Sigmoid).then_inc(vo_read, 1)

            for nb in range(12):
                split_block(0, 0, nb, ml_after)
                if nb == 4:
                    act.wait_ge(lam_p, 2)
                    nc.scalar.activation(lam_s[:, 2:4], lam_s[:, 0:2], ACT.Exp).then_inc(lam_e, 1)
                if nb == 6:
                    act.wait_ge(gate_pre, 1)
                    nc.scalar.activation(gr[:, 2, :], gr[:, 1, :], ACT.Exp, scale=-1.0).then_inc(act_step, 1)
                    act.wait_ge(act_step, 1)
                    nc.scalar.activation(gr[:, 3, :], gr[:, 2, :], ACT.Ln, bias=1.0).then_inc(gate_exp, 1)
                if nb == 8:
                    act.wait_ge(gate_rows, 1)
                    nc.scalar.activation(gr[:, 7, :], gr[:, 6, :], ACT.Exp, scale=-1.0).then_inc(gate_emt, 1)
            for k in range(4):
                ml_after(11, k)
            act.wait_ge(gate_cols, 1)
            for h in range(HM):
                act.wait_ge(dm_ready, h + 1)
                nc.scalar.activation(wT[:, h % 2, 0:256], wT[:, h % 2, 0:256], ACT.Exp, bias=gc[:, 0, h:h + 1]).then_inc(wt_ready, 1)
                nc.scalar.activation(wT[:, h % 2, 256:384], wT[:, h % 2, 256:384], ACT.Exp, bias=gc[:, 1, h:h + 1]).then_inc(wt_ready, 1)
                for i in range(NT):
                    k = 2 * h + i
                    act.wait_ge(h_ready, k + 1)
                    if k:
                        act.wait_ge(hsq, k)
                    nc.scalar.activation(iota, work[:, i, :], ACT.Square,
                                         accum_out=st[:, 8 + i:9 + i]).then_inc(hsq, 1)
                act.wait_ge(hms, h + 1)
                nc.scalar.activation(st[:, 12:14], st[:, 10:12], ACT.Sqrt).then_inc(hroot, 1)
            for b in range(0, VC // 2, 2):
                act.wait_ge(y_T, b + 1)
                for c in (2 * b, 2 * b + 1):
                    nc.scalar.mul(yT[:, c, :], ps[:, 4 + b % 4, c % 2 * T:(c % 2 + 1) * T], par[:, C_MLN + c:C_MLN + c + 1]).then_inc(yT_act, 1)

            def experts(layer, s, again):
                u0, cb, wb, eb = bases(layer, again)

                def h_chunks(turn, j, cs):
                    for c in cs:
                        k = c // 4
                        if c % 4 == 0:
                            act.wait_ge(s.unit_loaded[(u0 + UE * j + k) % RING], loaded_count(u0, turn, j, k))
                        make_h(s, turn * (8 * EB) + (cb + 8 * j + c), c, slot(u0, j, k)[:, c % 4 * CH:(c % 4 + 1) * CH])

                def window_h(turn, j):
                    w = window(act, turn, j, again)
                    nc.scalar.copy(xTh[:, :, j % 2 * W:(j % 2 + 1) * W], Xs[:, :, bass.ds(w, W)]).then_inc(s.xw_h, 1)

                def y_out(turn, j):
                    w = window(act, turn, j, again)
                    if not isinstance(turn, int) or turn + j:
                        act.wait_ge(s.y_act, turn * EB + (eb + j))
                    act.wait_ge(s.whole_used, turn * EB + (wb + j + 1))
                    nc.scalar.copy(Ys[:, 4:8, bass.ds(w, W)], ps[:, 2 * (j % 2) + 1, :].rearrange("p (c t) -> p c t", c=4)).then_inc(s.y_act, 1)

                def step(turn, j, first, last):
                    n = turn * EB + (eb + j)
                    b = (j - 1) % 2
                    has_before = not first or j >= 1
                    if not last:
                        h_chunks(turn, j, range(4))
                    if has_before:
                        act.wait_ge(s.chunk_used, turn * (8 * EB) + (cb + 8 * j))
                        if not first or j >= 3:
                            act.wait_ge(s.a_ready, n - 2)
                        nc.scalar.activation(sg_sb[:, b, :], ps[:, 4 + b, 0:F], ACT.Silu).then_inc(s.silu_done, 1)
                    if not last:
                        window_h(turn, j)
                    if not first or j >= 3:
                        y_out(*back(turn, j, 3))
                    if not last:
                        h_chunks(turn, j, range(4, 5))
                    if has_before:
                        act.wait_ge(s.a_T, n)
                        nc.scalar.copy(aT[:, b, :, :], ps[:, 6 + b, 0:2 * P].rearrange("p (c t) -> p c t", c=2)).then_inc(s.aT_ready, 1)
                    if not last:
                        h_chunks(turn, j, range(5, 8))

                over_experts(act, step)
                for j in (EB - 2, EB - 1):
                    y_out(TURNS - 1, j)
                act.wait_ge(s.y_act, eb + E)

            def moe(layer):
                n = 2 * layer + 1
                norm(n)
                evac_T(n, g_ffn[:, layer, :])
                act.wait_ge(gneg, layer + 1)
                for i in range(NT):
                    nc.scalar.activation(rt[:, 0, i, 0:G], lg[:, i, 0:G], ACT.Exp, bias=st[:, 18 + i:19 + i],
                                         accum_out=st[:, 20 + i:21 + i]).then_inc(gsum, 1)
                act.wait_ge(ediff, layer + 1)
                nc.scalar.activation(st[:, 28:30], st[:, 26:28], ACT.Exp).then_inc(eexp, 1)
                for c in range(0, DC, 2):
                    act.wait_ge(gath_mm, DC * layer + c + 1)
                    nc.scalar.mul(Xs[:, c, LEAD:LEAD + NPOS], ps[:, c, :], g_ffn[:, layer, c:c + 1]).then_inc(xs_act, 1)
                act.wait_ge(hit_T, 2 * layer + 1)
                nc.scalar.copy(hitT[:, 0:2, :], ps[:, 0, :].rearrange("p (k t) -> p k t", k=2)).then_inc(hitT_act, 1)
                act.wait_ge(xs_act, 4 * (layer + 1))
                act.wait_ge(xs_dve, 4 * (layer + 1))
                act.wait_ge(pads_zero, 3 * (layer + 1))
                act.wait_ge(win_ready, layer + 1)
                most = act.value_load(win[0:1, 2 * E:2 * E + 1], min_val=0, max_val=T)
                experts(layer, main, False)
                with act.If(most > W):
                    act.wait_ge(main.y_dve, E * (layer + 1))
                    experts(layer, again[layer], True)
                act.sem_inc(ys_act, 1)
                for b in range(0, 2 * NPC, 2):
                    act.wait_ge(ys_T, 2 * NPC * layer + b + 1)
                    nc.scalar.copy(Yn[:, b // 2, 0:512], ps[:, b, :]).then_inc(yn_act, 1)

            moe(0)
            norm(2)
            evac_T(2, g_mix[:, 1, :])
            def da_after(nb, k):
                if nb < 4:
                    c = 4 * nb + k
                    act.wait_ge(chunk_used, 4 * SPLIT0["da_in"] + 8 * (nb + 1))
                    nc.scalar.copy(qkT[:, c, :], ps[:, c % 8, 0:T]).then_inc(qk_ready, 1)
                elif k % 2 == 0:
                    b, i = nb - 4, k // 2
                    act.wait_ge(chunk_used, 4 * SPLIT0["da_in"] + 8 * (nb + 1))
                    nc.scalar.copy(vA[:, i, b * 512:(b + 1) * 512], ps[:, 2 * b + i, :]).then_inc(vo_read, 1)

            for nb in range(6):
                split_block(U0_DA_IN, 4 * SPLIT0["da_in"], nb, da_after)
            for k in range(4):
                da_after(5, k)
            for h in range(HA):
                for i in range(NT):
                    s = 2 * h + i
                    kn = P * (i + 1)
                    act.wait_ge(asc_max, s + 1)
                    for c in range(2):
                        nc.scalar.activation(work[:, s % 2, c * T:c * T + kn], work[:, s % 2, c * T:c * T + kn], ACT.Exp,
                                             bias=st[:, 32 + 2 * (s % 2) + c:33 + 2 * (s % 2) + c], scale=DH ** -0.5,
                                             accum_out=st[:, 36 + 2 * (s % 2) + c:37 + 2 * (s % 2) + c]).then_inc(aex, 1)
                act.wait_ge(aw_T, h + 1)
                nc.scalar.copy(sT[:, h % 2, :], ps[:, 4 + h % 2, 0:384]).then_inc(awT_ready, 1)
                act.wait_ge(apv, h + 1)
                for i in range(NT):
                    nc.scalar.activation(conv_u[:, 0, 0:DVA], ps[:, 6 + h % 2, i * P:(i + 1) * P], ACT.Square,
                                         accum_out=st[:, 40 + HA * i + h:41 + HA * i + h]).then_inc(act_step, 1)
                    act.wait_ge(act_step, 1 + 2 * h + i + 1)
                nc.scalar.copy(og[:, 0:2, h * DVA:(h + 1) * DVA], ps[:, 6 + h % 2, 0:2 * P].rearrange("p (i v) -> p i v", i=2)).then_inc(apv_read, 1)
            act.wait_ge(hms, HM + 1)
            nc.scalar.activation(st[:, 40:56], st[:, 40:56], ACT.Sqrt).then_inc(hroot, 1)
            for b in range(0, HA // 2, 2):
                act.wait_ge(y_T, VC // 2 + b + 1)
                for c in (2 * b, 2 * b + 1):
                    nc.scalar.mul(yT[:, c, :], ps[:, 4 + b % 4, c % 2 * T:(c % 2 + 1) * T], lam_s[:, 6:7]).then_inc(yT_act, 1)
            moe(1)
            norm(4)

        @block.vector
        def _(dve):
            steps = [0]

            def done(ins):
                steps[0] += 1
                ins.then_inc(dve_step, 1)
                dve.wait_ge(dve_step, steps[0])

            def norm(n):
                dve.wait_ge(squares, NT * (n + 1))
                nc.vector.tensor_scalar(st[:, 2:4], st[:, 0:2], 1.0 / D, EPS, ALU.mult, ALU.add).then_inc(ms_ready, 1)
                dve.wait_ge(root_ready, n + 1)
                done(nc.vector.reciprocal(st[:, 6:8], st[:, 4:6]))
                if n == 4:
                    dve.wait_ge(g_fin_loaded, 16)
                for i in range(NT):
                    if n < 4:
                        nc.vector.tensor_scalar(xn[:, i, :], xres[:, i, :], st[:, 6 + i:7 + i], None, ALU.mult).then_inc(xn_ready, 1)
                    else:
                        nc.vector.scalar_tensor_tensor(out=xn[:, i, :], in0=xres[:, i, :], scalar=st[:, 6 + i:7 + i],
                                                       in1=ring[:, 0, 0:D], op0=ALU.mult, op1=ALU.mult).then_inc(out_ready, 1)

            def evac_T(n, g_col):
                for c in range(DC):
                    if c % 2 == 0:
                        dve.wait_ge(xh_ready, DC * n + c + 2)
                    nc.vector.scalar_tensor_tensor(out=xTl[:, c, :], in0=ps[:, 4 + c // 2, c % 2 * T:(c % 2 + 1) * T],
                                                   scalar=g_col[:, c:c + 1], in1=xTh[:, c, :].bitcast(F32),
                                                   op0=ALU.mult, op1=ALU.subtract).then_inc(xl_ready, 1)

            def make_l(s, ch, c, src):
                dve.wait_ge(s.h_made, ch + 1)
                b = c % BUFS
                nc.vector.tensor_tensor(wl[:, b, :], src, wh[:, b, :].bitcast(F32), ALU.subtract).then_inc(s.l_made, 1)

            def split_block(u0, ch0, nb, after):
                for c in range(DC):
                    make_l(main, ch0 + 8 * nb + c, c, unit(u0 + 2 * nb + c // 4)[:, c % 4 * CH:(c % 4 + 1) * CH])
                    if nb and c in AFTER:
                        after(nb - 1, AFTER.index(c))

            def split_small(h, l, w):
                done(nc.vector.tensor_copy(h, w))
                nc.vector.tensor_tensor(l, w, h.bitcast(F32), ALU.subtract).then_inc(small_split, 1)

            def residual(n, signal, count):
                for i in range(NT):
                    for half in range(2):
                        dve.wait_ge(signal, count + (2 * i + half if signal is comb_mm else 0))
                        sl = xres[:, i, half * 512:(half + 1) * 512]
                        nc.vector.tensor_tensor(sl, sl, ps[:, 2 * i + half, :], ALU.add).then_inc(res_done, 1)

            norm(0)
            dve.wait_ge(g_mix_loaded, 16)
            evac_T(0, g_mix[:, 0, :])
            dve.wait_ge(par_T, 1)
            nc.vector.tensor_copy(par[:], ps[:, 0, 0:N_COLS]).then_inc(par_ready, 1)

            def ml_after(nb, k):
                if nb >= 4:
                    return
                c = 4 * nb + k
                u = conv_u[:, c % 2, :]
                src = ps[:, c % 8, 0:T]
                dve.wait_ge(conv_tap, c + 1)
                for tap in range(TAPS - 2, -1, -1):
                    lag = TAPS - 1 - tap
                    w = par[:, C_CONV + tap * QC + c:C_CONV + tap * QC + c + 1]
                    ins = nc.vector.scalar_tensor_tensor(out=u[:, lag:T], in0=src[:, 0:T - lag], scalar=w,
                                                         in1=u[:, lag:T], op0=ALU.mult, op1=ALU.add)
                    if lag < TAPS - 1:
                        done(ins)
                    else:
                        ins.then_inc(conv_done, 1)

            for nb in range(12):
                split_block(0, 0, nb, ml_after)
                if nb == 3:
                    dve.wait_ge(consts_loaded, CONSTS)
                    split_small(wg_h[:], wg_l[:], w_gate[:])
                    for n in range(2):
                        nc.vector.tensor_tensor_reduce(out=lam_x[:, n, :], in0=lam_in[:, 2 * n, :], in1=lam_in[:, 2 * n + 1, :],
                                                       scale=1.0, scalar=0.0, op0=ALU.mult, op1=ALU.add,
                                                       accum_out=lam_s[:, n:n + 1]).then_inc(lam_p, 1)
                if nb == 5:
                    dve.wait_ge(lam_e, 1)
                    done(nc.vector.tensor_tensor(lam_s[:, 4:5], lam_s[:, 3:4], lam_s[:, 2:3], ALU.subtract))
                    done(nc.vector.tensor_scalar(lam_s[:, 5:6], lam_s[:, 4:5], -LAMBDA_INIT, None, ALU.add))
                    done(nc.vector.tensor_scalar(lam_s[:, 6:7], par[:, C_DAN:C_DAN + 1], 1.0 - LAMBDA_INIT, None, ALU.mult))
                    dve.wait_ge(gates_nat, 1)
                    nc.vector.tensor_copy(gn[:], ps[:, 7, 0:NT * 2 * HM].rearrange("p (i k) -> p i k", i=NT)).then_inc(gates_copied, 1)
                if nb == 6:
                    dve.wait_ge(gates_mm, 1)
                    nc.vector.tensor_scalar(gr[:, 0, :], ps[0:HM, 7, 0:T], b_i[:, 0:1], None, ALU.add).then_inc(gates_read, 1)
                    nc.vector.tensor_scalar(gr[:, 4, :], ps[0:HM, 7, T:2 * T], b_f[:, 0:1], None, ALU.add).then_inc(gates_read, 1)
                    dve.wait_ge(gates_read, 2)
                    done(nc.vector.tensor_scalar(gr[:, 5, :], gr[:, 4, :], -1.0, None, ALU.mult))
                    nc.vector.tensor_tensor(gr[:, 1, :], gr[:, 4, :], gr[:, 5, :], ALU.max).then_inc(gate_pre, 1)
                if nb == 7:
                    dve.wait_ge(gate_exp, 1)
                    done(nc.vector.scalar_tensor_tensor(out=gr[:, 4, :], in0=gr[:, 4, :], scalar=0.0, in1=gr[:, 3, :],
                                                        op0=ALU.min, op1=ALU.subtract))
                    done(nc.vector.memset(gr[:, 3, :], 0.0))
                    done(nc.vector.tensor_tensor_scan(gr[:, 2, :], gr[:, 4, :], gr[:, 3, :], 0.0, ALU.add, ALU.add))
                    done(nc.vector.tensor_tensor(gr[:, 5, :], gr[:, 0, :], gr[:, 2, :], ALU.subtract))
                    done(nc.vector.tensor_tensor_scan(gr[:, 4, :], gr[:, 5, :], gr[:, 3, :], 0.0, ALU.max, ALU.max))
                    done(nc.vector.tensor_scalar(gr[:, 1, :], gr[:, 4, :], -1.0, None, ALU.mult))
                    nc.vector.tensor_tensor(gr[:, 6, :], gr[:, 4, :], gr[:, 2, :], ALU.add).then_inc(gate_rows, 1)
            dve.wait_ge(gate_cols_mm, 1)
            nc.vector.tensor_copy(gc[:], ps[:, 7, 0:NT * 2 * HM].rearrange("p (i k) -> p i k", i=NT)).then_inc(gate_cols, 1)
            dve.wait_ge(rows_bcast, 1)
            dve.wait_ge(gate_cols, 1)
            for h in range(HM):
                b = h % 2
                R = ps[:, h // 2, (h % 2) * T:(h % 2 + 1) * T]
                if h >= 2:
                    dve.wait_ge(s_ready, h - 1)
                done(nc.vector.tensor_tensor(wT[:, b, 0:P], R[:, 0:P], neg_ts[:], ALU.add))
                done(nc.vector.tensor_copy(wT[:, b, P:T], R[:, P:T]))
                nc.vector.tensor_tensor(wT[:, b, T:T + P], R[:, P:T], neg_ts[:], ALU.add).then_inc(dm_ready, 1)
                dve.wait_ge(sc_mm, h + 1)
                dve.wait_ge(wt_ready, 2 * h + 2)
                if h >= 2:
                    dve.wait_ge(pv_mm, 2 * h - 2)
                nc.vector.scalar_tensor_tensor(out=sT[:, b, :], in0=ps[:, 2 + b, 0:384], scalar=DQK ** -0.5,
                                               in1=wT[:, b, :], op0=ALU.mult, op1=ALU.mult).then_inc(s_ready, 1)
                for i in range(NT):
                    k = 2 * h + i
                    dve.wait_ge(pv_mm, k + 1)
                    den = ps[:, 2 + b, 384 + i:385 + i]
                    done(nc.vector.tensor_copy(st[:, 14:15], den))
                    done(nc.vector.scalar_tensor_tensor(out=st[:, 15:16], in0=st[:, 14:15], scalar=-1.0, in1=st[:, 14:15],
                                                        op0=ALU.mult, op1=ALU.max))
                    done(nc.vector.tensor_tensor(st[:, 16:17], st[:, 15:16], gc[:, i, HM + h:HM + h + 1], ALU.max))
                    done(nc.vector.reciprocal(st[:, 17:18], st[:, 16:17]))
                    nc.vector.tensor_scalar(work[:, i, :], ps[:, 4 + 2 * b + i, :], st[:, 17:18], None, ALU.mult).then_inc(h_ready, 1)
                    dve.wait_ge(h_ready, k + 1)
                dve.wait_ge(hsq, 2 * h + 2)
                nc.vector.tensor_scalar(st[:, 10:12], st[:, 8:10], 1.0 / DV, EPS, ALU.mult, ALU.add).then_inc(hms, 1)
                dve.wait_ge(hroot, h + 1)
                done(nc.vector.reciprocal(st[:, 12:14], st[:, 12:14]))
                for i in range(NT):
                    sl = og[:, i, h * DV:(h + 1) * DV]
                    dve.wait_ge(vo_read, 8 + 2 * h + i + 1)
                    nc.vector.scalar_tensor_tensor(out=sl, in0=work[:, i, :], scalar=st[:, 12 + i:13 + i], in1=sl,
                                                   op0=ALU.mult, op1=ALU.mult).then_inc(y_ready, 1)
                dve.wait_ge(y_ready, 2 * h + 2)
            for b in range(1, VC // 2, 2):
                dve.wait_ge(y_T, b + 1)
                for c in (2 * b, 2 * b + 1):
                    nc.vector.tensor_scalar(yT[:, c, :], ps[:, 4 + b % 4, c % 2 * T:(c % 2 + 1) * T],
                                            par[:, C_MLN + c:C_MLN + c + 1], None, ALU.mult).then_inc(yT_dve, 1)
            residual(0, whole_used, WHOLE0["moe0"])

            def experts(layer, s, again):
                u0, cb, wb, eb = bases(layer, again)

                def l_chunks(turn, j, cs):
                    for c in cs:
                        make_l(s, turn * (8 * EB) + (cb + 8 * j + c), c, slot(u0, j, c // 4)[:, c % 4 * CH:(c % 4 + 1) * CH])

                def window_l(turn, j):
                    w = window(dve, turn, j, again)
                    dve.wait_ge(s.xw_h, turn * EB + (eb + j + 1))
                    xs = slice(j % 2 * W, (j % 2 + 1) * W)
                    nc.vector.tensor_tensor(xTl[:, :, xs], Xs[:, :, bass.ds(w, W)], xTh[:, :, xs].bitcast(F32),
                                            ALU.subtract).then_inc(s.xw_l, 1)

                def y_out(turn, j):
                    w = window(dve, turn, j, again)
                    if not isinstance(turn, int) or turn + j:
                        dve.wait_ge(s.y_dve, turn * EB + (eb + j))
                    dve.wait_ge(s.whole_used, turn * EB + (wb + j + 1))
                    nc.vector.tensor_copy(Ys[:, 0:4, bass.ds(w, W)], ps[:, 2 * (j % 2), :].rearrange("p (c t) -> p c t", c=4)).then_inc(s.y_dve, 1)

                def step(turn, j, first, last):
                    n = turn * EB + (eb + j)
                    b = (j - 1) % 2
                    if not last:
                        l_chunks(turn, j, range(4))
                    if not first or j >= 1:
                        dve.wait_ge(s.silu_done, n)
                        if not first or j >= 3:
                            dve.wait_ge(s.a_T, n - 2)
                        nc.vector.tensor_tensor(a_sb[:, b, :], sg_sb[:, b, :], ps[:, 4 + b, F:2 * F], ALU.mult).then_inc(s.a_ready, 1)
                    if not last:
                        window_l(turn, j)
                    if not first or j >= 3:
                        y_out(*back(turn, j, 3))
                    if not last:
                        l_chunks(turn, j, range(4, 8))

                over_experts(dve, step)
                for j in (EB - 2, EB - 1):
                    y_out(TURNS - 1, j)
                dve.wait_ge(s.y_dve, eb + E)

            def moe(layer):
                n = 2 * layer + 1
                split_small(wr_h[:], wr_l[:], w_rout[:, layer, :, :])
                norm(n)
                evac_T(n, g_ffn[:, layer, :])
                dve.wait_ge(log_mm, layer + 1)
                done(nc.vector.tensor_tensor(lg[:], ps[:, 4, 0:NT * LOGITS].rearrange("p (i k) -> p i k", i=NT),
                                             b_rout[:, layer, :, :], ALU.add))
                gl = lg[:, :, 0:G]
                done(nc.vector.tensor_reduce(st[:, 16:18], gl, AX_X, ALU.max))
                nc.vector.tensor_scalar(st[:, 18:20], st[:, 16:18], -1.0, None, ALU.mult).then_inc(gneg, 1)

                def first_max(dst, vals, mx, k, tmp):
                    done(nc.vector.tensor_tensor(tmp, vals, mx.rearrange("p (i o) -> p i o", o=1).to_broadcast([P, NT, k]), ALU.is_equal))
                    done(nc.vector.tensor_tensor(tmp, tmp, rank_w[:, E - k:E].rearrange("p (o k) -> p o k", o=1).to_broadcast([P, NT, k]), ALU.mult))
                    done(nc.vector.tensor_reduce(st[:, 22:24], tmp, AX_X, ALU.max))
                    done(nc.vector.tensor_tensor(dst, tmp, st[:, 22:24].rearrange("p (i o) -> p i o", o=1).to_broadcast([P, NT, k]), ALU.is_equal))

                ghot = rt[:, 1, :, 0:G]
                first_max(ghot, gl, st[:, 16:18], G, rt[:, 1, :, G:2 * G])
                done(nc.vector.tensor_scalar(rt[:, 1, :, 8:8 + G], ghot, 1.0, BIG, ALU.subtract, ALU.mult))
                m32 = rt[:, 2, :, :]
                for i in range(NT):
                    done(nc.vector.tensor_tensor(m32[:, i, :].rearrange("p (g e) -> p g e", g=G),
                                                 lg[:, i, G:].rearrange("p (g e) -> p g e", g=G),
                                                 rt[:, 1, i, 8:8 + G].rearrange("p (g o) -> p g o", o=1).to_broadcast([P, G, EG]), ALU.add))
                done(nc.vector.tensor_reduce(st[:, 24:26], m32, AX_X, ALU.max))
                first_max(rt[:, 3, :, :], m32, st[:, 24:26], E, rt[:, 5, :, :])
                done(nc.vector.scalar_tensor_tensor(out=m32, in0=rt[:, 3, :, :], scalar=-2 * BIG, in1=m32, op0=ALU.mult, op1=ALU.add))
                done(nc.vector.tensor_reduce(st[:, 30:32], m32, AX_X, ALU.max))
                first_max(rt[:, 4, :, :], m32, st[:, 30:32], E, rt[:, 5, :, :])
                nc.vector.tensor_tensor(st[:, 26:28], st[:, 30:32], st[:, 24:26], ALU.subtract).then_inc(ediff, 1)
                nc.vector.tensor_tensor(rt[:, 5, :, :], rt[:, 3, :, :], rt[:, 4, :, :], ALU.add).then_inc(asg_ready, 1)
                dve.wait_ge(eexp, layer + 1)
                dve.wait_ge(gsum, 2 * layer + 2)
                done(nc.vector.tensor_scalar(st[:, 24:26], st[:, 28:30], 1.0, None, ALU.add))
                done(nc.vector.tensor_tensor(st[:, 24:26], st[:, 24:26], st[:, 20:22], ALU.mult))
                done(nc.vector.reciprocal(st[:, 16:18], st[:, 24:26]))
                done(nc.vector.tensor_tensor(st[:, 30:32], st[:, 16:18], st[:, 28:30], ALU.mult))
                cnt, cum = rt[:, 0, 0, :], rt[:, 0, 1, :]
                dve.wait_ge(rank_mm, layer + 1)
                done(nc.vector.tensor_copy(cnt, ps[:, 5, 2 * E:3 * E]))
                done(nc.vector.tensor_tensor_scan(cum, cnt, zeros[:], 0.0, ALU.add, ALU.add))
                done(nc.vector.tensor_tensor(rt[:, 5, 0, :], cum, cnt, ALU.subtract))
                for i in range(NT):
                    done(nc.vector.tensor_tensor(rt[:, 1, i, :], ps[:, 5, i * E:(i + 1) * E], rt[:, 5, 0, :], ALU.add))
                for k in range(2):
                    done(nc.vector.tensor_tensor(rt[:, 2, :, :], rt[:, 1, :, :], rt[:, 3 + k, :, :], ALU.mult))
                    done(nc.vector.tensor_reduce(st[:, 56 + 2 * k:58 + 2 * k], rt[:, 2, :, :], AX_X, ALU.add))
                dve.wait_ge(pads_zero, 3 * layer + 1)
                for i in range(NT):
                    done(nc.vector.tensor_scalar(hit[:, i, :], iota, st[:, 56 + i:57 + i], None, ALU.is_equal))
                    nc.vector.scalar_tensor_tensor(out=hit[:, i, :], in0=iota, scalar=st[:, 58 + i:59 + i], in1=hit[:, i, :],
                                                   op0=ALU.is_equal, op1=ALU.add).then_inc(hit_ready, 1)
                done(nc.vector.tensor_reduce(st[0:1, 60:61], cnt[0:1, :], AX_X, ALU.max))
                done(nc.vector.tensor_scalar(win[0:1, 0:E], rt[0:1, 5, 0, :], float(LEAD), None, ALU.add))
                done(nc.vector.tensor_scalar(win[0:1, E:2 * E], cum[0:1, :], float(LEAD - W), None, ALU.add))
                nc.vector.tensor_copy(win[0:1, 2 * E:2 * E + 1], st[0:1, 60:61]).then_inc(win_ready, 1)
                for i in range(NT):
                    done(nc.vector.tensor_scalar(hit_w[:, i, :], iota, st[:, 56 + i:57 + i], st[:, 16 + i:17 + i],
                                                 ALU.is_equal, ALU.mult))
                    done(nc.vector.tensor_scalar(hit_t, iota, st[:, 58 + i:59 + i], st[:, 30 + i:31 + i],
                                                 ALU.is_equal, ALU.mult))
                    nc.vector.tensor_tensor(hit_w[:, i, :], hit_w[:, i, :], hit_t, ALU.add).then_inc(hitw_ready, 1)
                for c in range(1, DC, 2):
                    dve.wait_ge(gath_mm, DC * layer + c + 1)
                    nc.vector.tensor_scalar(Xs[:, c, LEAD:LEAD + NPOS], ps[:, c, :], g_ffn[:, layer, c:c + 1], None,
                                            ALU.mult).then_inc(xs_dve, 1)
                dve.wait_ge(hit_T, 2 * layer + 2)
                nc.vector.tensor_copy(hitT[:, 2:4, :], ps[:, 1, :].rearrange("p (k t) -> p k t", k=2)).then_inc(hitT_dve, 1)
                dve.wait_ge(xs_act, 4 * (layer + 1))
                dve.wait_ge(xs_dve, 4 * (layer + 1))
                dve.wait_ge(pads_zero, 3 * (layer + 1))
                dve.wait_ge(win_ready, layer + 1)
                most = dve.value_load(win[0:1, 2 * E:2 * E + 1], min_val=0, max_val=T)
                experts(layer, main, False)
                with dve.If(most > W):
                    dve.wait_ge(main.y_act, E * (layer + 1))
                    experts(layer, again[layer], True)
                dve.sem_inc(ys_dve, 1)
                for b in range(1, 2 * NPC, 2):
                    dve.wait_ge(ys_T, 2 * NPC * layer + b + 1)
                    nc.vector.tensor_copy(Yn[:, b // 2, 512:1024], ps[:, b, :]).then_inc(yn_dve, 1)
                residual(n, comb_mm, 4 * layer + 1)

            moe(0)
            norm(2)
            evac_T(2, g_mix[:, 1, :])
            for nb in range(6):
                split_block(U0_DA_IN, 4 * SPLIT0["da_in"], nb, lambda nb, k: None)
            for h in range(HA):
                for i in range(NT):
                    s = 2 * h + i
                    kn = P * (i + 1)
                    b = s % 2
                    sc = work[:, b, :].rearrange("p (c k) -> p c k", c=2)
                    dve.wait_ge(asc_mm, s + 1)
                    for c in range(2):
                        nc.vector.tensor_tensor(sc[:, c, 0:kn], ps[:, 2 * b + c, 0:kn], neg_qk[:, T - kn:T], ALU.add).then_inc(asc_masked, 1)
                    dve.wait_ge(asc_masked, 2 * s + 2)
                    done(nc.vector.tensor_reduce(st[:, 8:10], sc[:, :, 0:kn], AX_X, ALU.max))
                    nc.vector.tensor_scalar(st[:, 32 + 2 * b:34 + 2 * b], st[:, 8:10], -DH ** -0.5, None, ALU.mult).then_inc(asc_max, 1)
                    dve.wait_ge(aex, 2 * s + 2)
                    done(nc.vector.reciprocal(st[:, 10:12], st[:, 36 + 2 * b:38 + 2 * b]))
                    done(nc.vector.tensor_scalar(st[:, 12:13], st[:, 11:12], lam_s[:, 5:6], None, ALU.mult))
                    done(nc.vector.tensor_scalar(sc[:, 0, 0:kn], sc[:, 0, 0:kn], st[:, 10:11], None, ALU.mult))
                    if s >= 2:
                        dve.wait_ge(aw_T, h)
                    nc.vector.scalar_tensor_tensor(out=wT[:, i, 0:kn], in0=sc[:, 1, 0:kn], scalar=st[:, 12:13], in1=sc[:, 0, 0:kn],
                                                   op0=ALU.mult, op1=ALU.add).then_inc(aw_ready, 1)
                    dve.wait_ge(aw_ready, s + 1)
            dve.wait_ge(apv_read, HA)
            nc.vector.tensor_scalar(st[:, 40:56], st[:, 40:56], 1.0 / DVA, DA_EPS, ALU.mult, ALU.add).then_inc(hms, 1)
            dve.wait_ge(hroot, HM + 1)
            done(nc.vector.reciprocal(st[:, 40:56], st[:, 40:56]))
            for i in range(NT):
                o = og[:, i, 0:HA * DVA].rearrange("p (h v) -> p h v", h=HA)
                r = st[:, 40 + HA * i:40 + HA * (i + 1)].rearrange("p (h o) -> p h o", o=1).to_broadcast([P, HA, DVA])
                nc.vector.tensor_tensor(o, o, r, ALU.mult).then_inc(y_ready, 1)
            for b in range(1, HA // 2, 2):
                dve.wait_ge(y_T, VC // 2 + b + 1)
                for c in (2 * b, 2 * b + 1):
                    nc.vector.tensor_scalar(yT[:, c, :], ps[:, 4 + b % 4, c % 2 * T:(c % 2 + 1) * T], lam_s[:, 6:7], None,
                                            ALU.mult).then_inc(yT_dve, 1)
            residual(2, whole_used, WHOLE0["moe1"])
            moe(1)
            norm(4)

        @block.tensor
        def _(pe):
            def split_mm(dst, lhs, rhs, start, stop):
                pe.matmul(dst, lhs[0], rhs[0], start=start, stop=False)
                pe.matmul(dst, lhs[1], rhs[0], start=False, stop=False)
                return pe.matmul(dst, lhs[0], rhs[1], start=False, stop=stop)

            def input_T(n):
                if n:
                    pe.wait_ge(res_done, 4 * n)
                for c in range(DC):
                    for i in range(NT):
                        if c == 0:
                            pe.wait_ge(xn_ready, NT * n + i + 1)
                        col = (c % 2) * T + i * P
                        mm = pe.transpose(ps[:, 4 + c // 2, col:col + P], xn[:, i, c:D:DC], ident[:])
                    if c % 2:
                        mm.then_inc(xn_T, 1)
                if n == 0:
                    pe.wait_ge(tables_made, 1)
                    pe.wait_ge(par_loaded, 48)
                    pe.transpose(ps[:, 0, 0:N_COLS], par_rows[:], ident[0:N_COLS, 0:N_COLS]).then_inc(par_T, 1)
                    pe.wait_ge(par_ready, 1)
                pe.wait_ge(xl_ready, DC * (n + 1))

            def x_tile(c, i):
                return xTh[:, c, i * P:(i + 1) * P], xTl[:, c, i * P:(i + 1) * P]

            def w_chunk(ch, cols=slice(0, CH)):
                return wh[:, ch % BUFS, cols], wl[:, ch % BUFS, cols]

            def project_T(ch0, nb):
                for c in range(DC):
                    ch = ch0 + 8 * nb + c
                    pe.wait_ge(l_made, ch + 1)
                    for cc in range(4):
                        mm = split_mm(ps[:, (nb % 2) * 4 + cc, 0:T], w_chunk(ch, slice(cc * P, (cc + 1) * P)),
                                      (xTh[:, c, :], xTl[:, c, :]), c == 0, c == DC - 1)
                    mm.then_inc(chunk_used, 1)

            def project(ch0, nb, bank):
                for c in range(DC):
                    ch = ch0 + 8 * nb + c
                    pe.wait_ge(l_made, ch + 1)
                    for i in range(NT):
                        mm = split_mm(ps[:, bank + i, :], x_tile(c, i), w_chunk(ch), c == 0, c == DC - 1)
                    mm.then_inc(chunk_used, 1)

            def output(u0, chunks, T0, n):
                for c in range(chunks):
                    if c % 2 == 0 and c >= 8:
                        pe.wait_ge(yT_dve if c // 2 % 2 else yT_act, T0 + 2 * ((c // 2 - 4) // 2 + 1))
                    for i in range(NT):
                        col = (c % 2) * T + i * P
                        mm = pe.transpose(ps[:, 4 + c // 2 % 4, col:col + P], og[:, i, c * P:(c + 1) * P], ident[:])
                    if c % 2:
                        mm.then_inc(y_T, 1)
                for c in range(chunks):
                    u = u0 + c // 2
                    unit_is_there(pe, u)
                    pe.wait_ge(yT_dve if c // 2 % 2 else yT_act, T0 + 2 * (c // 4) + c % 2 + 1)
                    for i in range(NT):
                        for half in range(2):
                            w = unit(u)[:, (c % 2) * D + half * 512:(c % 2) * D + (half + 1) * 512]
                            mm = pe.matmul(ps[:, 2 * i + half, :], yT[:, c, i * P:(i + 1) * P], w,
                                           start=(c == 0), stop=(c == chunks - 1))
                    if c % 2:
                        mm.then_inc(whole_used, 1)

            pe.wait_ge(pool_step, 2)
            input_T(0)
            for nb in range(12):
                if nb < 4:
                    if nb >= 2:
                        pe.wait_ge(conv_done, 4 * (nb - 1))
                    project_T(0, nb)
                    continue
                if nb < 8:
                    pe.wait_ge(conv_done, 12 if nb < 6 else 16)
                else:
                    pe.wait_ge(vo_read, 2 * (nb - 7))
                if nb == 7:
                    pe.wait_ge(gates_read, 2)
                project(0, nb, 2 * nb % 8)
                if nb == 4:
                    pe.wait_ge(conv_done, 16)
                    pe.wait_ge(small_split, 1)
                    for i in range(NT):
                        for c in range(DC):
                            mm = split_mm(ps[:, 7, i * 2 * HM:(i + 1) * 2 * HM], x_tile(c, i), (wg_h[:, c, :], wg_l[:, c, :]),
                                          c == 0, c == DC - 1)
                    mm.then_inc(gates_nat, 1)
                if nb == 5:
                    pe.wait_ge(gates_copied, 1)
                    for g in range(2):
                        for i in range(NT):
                            mm = pe.transpose(ps[0:HM, 7, g * T + i * P:g * T + (i + 1) * P], gn[:, i, g * HM:(g + 1) * HM], ident[:])
                    mm.then_inc(gates_mm, 1)
            pe.wait_ge(vo_read, 16)
            pe.wait_ge(gate_rows, 1)
            pe.wait_ge(gate_emt, 1)
            for i in range(NT):
                for k, row in enumerate((5, 7)):
                    mm = pe.transpose(ps[:, 7, (2 * i + k) * HM:(2 * i + k + 1) * HM], gr[:, row, i * P:(i + 1) * P], ident[0:HM, 0:HM])
            mm.then_inc(gate_cols_mm, 1)
            for h in range(HM):
                mm = pe.matmul(ps[:, h // 2, (h % 2) * T:(h % 2 + 1) * T], ident[0:HM, h:h + 1].to_broadcast([HM, P]), gr[:, 1, :], start=True, stop=True)
            mm.then_inc(rows_bcast, 1)
            pe.wait_ge(gate_cols, 1)
            pe.wait_ge(qk_ready, QC)
            for h in range(HM):
                b = h % 2
                if h >= 2:
                    pe.wait_ge(h_ready, 2 * h - 2)
                for s in range(2):
                    for c in range(2):
                        q, k = qkT[:, 2 * h + c, s * P:T], qkT[:, QC // 2 + 2 * h + c, s * P:(s + 1) * P]
                        mm = pe.matmul(ps[:, 2 + b, s * T:s * T + T - s * P], k, q, start=(c == 0), stop=(c == 1))
                mm.then_inc(sc_mm, 1)
                pe.wait_ge(s_ready, h + 1)
                for i in range(NT):
                    for s in range(i + 1):
                        lhs = sT[:, b, (i + s) * P:(i + s + 1) * P]
                        pe.matmul(ps[:, 2 + b, 384 + i:385 + i], lhs, ones[:, 0:1], start=(s == 0), stop=(s == i))
                for i in range(NT):
                    for s in range(i + 1):
                        lhs = sT[:, b, (i + s) * P:(i + s + 1) * P]
                        mm = pe.matmul(ps[:, 4 + 2 * b + i, :], lhs, v_sb[:, s, h * DV:(h + 1) * DV], start=(s == 0), stop=(s == i))
                    mm.then_inc(pv_mm, 1)
            pe.wait_ge(y_ready, 2 * HM)
            output(U0_ML_OUT, VC, 0, 0)

            def experts(layer, s, again):
                u0, cb, wb, eb = bases(layer, again)

                def step(turn, j, first, last):
                    n = turn * EB + (eb + j)
                    pt, pj = (turn, j - 1) if j else (turn - 1, EB - 1)
                    has_before = not (first and j == 0)
                    if has_before:
                        pe.wait_ge(s.a_ready, n)
                        if not first or j >= 3:
                            pe.wait_ge(s.aT_ready, n - 2)
                        for c in range(2):
                            mm = pe.transpose(ps[:, 6 + pj % 2, c * P:(c + 1) * P], a_sb[:, pj % 2, c:F:2], ident[:])
                        mm.then_inc(s.a_T, 1)
                    if not last:
                        pe.wait_ge(s.xw_l, n + 1)
                        xs = slice(j % 2 * W, (j % 2 + 1) * W)
                        for c in range(DC):
                            pe.wait_ge(s.l_made, turn * (8 * EB) + (cb + 8 * j + c + 1))
                            mm = split_mm(ps[:, 4 + j % 2, :], (xTh[:, c, xs], xTl[:, c, xs]), w_chunk(c), c == 0, c == DC - 1)
                            mm.then_inc(s.chunk_used, 1)
                    if has_before:
                        pe.wait_ge(s.unit_loaded[(u0 + UE * pj + 2) % RING], loaded_count(u0, pt, pj, 2))
                        pe.wait_ge(s.aT_ready, n)
                        if not first or j >= 3:
                            pe.wait_ge(s.y_act, n - 2)
                            pe.wait_ge(s.y_dve, n - 2)
                        w = slot(u0, pj, 2)
                        for c in range(DC):
                            for k in range(2):
                                mm = pe.matmul(ps[:, 2 * (pj % 2) + c // 4, c % 4 * P:(c % 4 + 1) * P],
                                               w[:, k * D + c * P:k * D + (c + 1) * P], aT[:, pj % 2, k, :], start=(k == 0), stop=(k == 1))
                        mm.then_inc(s.whole_used, 1)

                over_experts(pe, step)

            def moe(layer):
                input_T(2 * layer + 1)
                pe.wait_ge(small_split, 2 + layer)
                for i in range(NT):
                    for c in range(DC):
                        mm = split_mm(ps[:, 4, i * LOGITS:(i + 1) * LOGITS], x_tile(c, i), (wr_h[:, c, :], wr_l[:, c, :]),
                                      c == 0, c == DC - 1)
                mm.then_inc(log_mm, 1)
                pe.wait_ge(asg_ready, layer + 1)
                pe.matmul(ps[:, 5, 0:E], earlier[:], rt[:, 5, 0, :], start=True, stop=True)
                pe.matmul(ps[:, 5, E:2 * E], earlier[:], rt[:, 5, 1, :], start=True, stop=False)
                pe.matmul(ps[:, 5, E:2 * E], ones[:], rt[:, 5, 0, :], start=False, stop=True)
                pe.matmul(ps[:, 5, 2 * E:3 * E], ones[:], rt[:, 5, 0, :], start=True, stop=False)
                pe.matmul(ps[:, 5, 2 * E:3 * E], ones[:], rt[:, 5, 1, :], start=False, stop=True).then_inc(rank_mm, 1)
                pe.wait_ge(hit_ready, 2 * layer + 2)
                for c in range(DC):
                    for i in range(NT):
                        mm = pe.matmul(ps[:, c, :], xn[:, i, c:D:DC], hit[:, i, :], start=(i == 0), stop=(i == NT - 1))
                    mm.then_inc(gath_mm, 1)
                pe.wait_ge(hitw_ready, 2 * layer + 2)
                pe.wait_ge(xs_act, 4 * layer + 1)
                pe.wait_ge(xs_dve, 4 * layer + 1)
                for k in range(NPC):
                    for i in range(NT):
                        mm = pe.transpose(ps[:, k // 2, k % 2 * T + i * P:k % 2 * T + (i + 1) * P], hit_w[:, i, k * P:(k + 1) * P], ident[:])
                    if k % 2:
                        mm.then_inc(hit_T, 1)
                pe.wait_ge(hitT_act, layer + 1)
                pe.wait_ge(hitT_dve, layer + 1)
                pe.wait_ge(xs_act, 4 * layer + 4)
                pe.wait_ge(xs_dve, 4 * layer + 4)
                pe.wait_ge(win_ready, layer + 1)
                most = pe.value_load(win[0:1, 2 * E:2 * E + 1], min_val=0, max_val=T)
                experts(layer, main, False)
                with pe.If(most > W):
                    pe.wait_ge(main.y_act, E * (layer + 1))
                    pe.wait_ge(main.y_dve, E * (layer + 1))
                    experts(layer, again[layer], True)
                pe.wait_ge(ys_act, layer + 1)
                pe.wait_ge(ys_dve, layer + 1)
                for b in range(2 * NPC):
                    for c in range(4):
                        mm = pe.transpose(ps[:, b, c * P:(c + 1) * P], Ys[:, b % 2 * 4 + c, LEAD + b // 2 * P:LEAD + (b // 2 + 1) * P], ident[:])
                    mm.then_inc(ys_T, 1)
                pe.wait_ge(yn_act, NPC * (layer + 1))
                pe.wait_ge(yn_dve, NPC * (layer + 1))
                for i in range(NT):
                    for half in range(2):
                        for k in range(NPC):
                            mm = pe.matmul(ps[:, 2 * i + half, :], hitT[:, k, i * P:(i + 1) * P], Yn[:, k, half * 512:(half + 1) * 512],
                                           start=(k == 0), stop=(k == NPC - 1))
                        mm.then_inc(comb_mm, 1)

            moe(0)
            input_T(2)
            for nb in range(6):
                if nb in (2, 3):
                    pe.wait_ge(qk_ready, QC + 4 * (nb - 1))
                if nb >= 4:
                    pe.wait_ge(qk_ready, QC + 12)
                    project(4 * SPLIT0["da_in"], nb, 2 * (nb - 4))
                else:
                    project_T(4 * SPLIT0["da_in"], nb)
            pe.wait_ge(qk_ready, 2 * QC)
            pe.wait_ge(vo_read, 20)

            def a_scores(s):
                h, i = s // 2, s % 2
                if s >= 2:
                    pe.wait_ge(asc_masked, 2 * s - 2)
                for c in range(2):
                    mm = pe.matmul(ps[:, 2 * (s % 2) + c, 0:P * (i + 1)], qkT[c * DH:(c + 1) * DH, h, i * P:(i + 1) * P],
                                   qkT[c * DH:(c + 1) * DH, HA + h, 0:P * (i + 1)], start=True, stop=True)
                mm.then_inc(asc_mm, 1)

            for s in range(2):
                a_scores(s)
            for h in range(HA):
                if h + 1 < HA:
                    for i in range(NT):
                        a_scores(2 * h + 2 + i)
                pe.wait_ge(aw_ready, 2 * h + 2)
                if h >= 2:
                    pe.wait_ge(awT_ready, h - 1)
                for n, (i, k) in enumerate(((0, 0), (1, 0), (1, 1))):
                    mm = pe.transpose(ps[:, 4 + h % 2, n * P:(n + 1) * P], wT[:, i, k * P:(k + 1) * P], ident[:])
                mm.then_inc(aw_T, 1)
                pe.wait_ge(awT_ready, h + 1)
                if h >= 2:
                    pe.wait_ge(apv_read, h - 1)
                for i in range(NT):
                    for s in range(i + 1):
                        mm = pe.matmul(ps[:, 6 + h % 2, i * P:(i + 1) * P], sT[:, h % 2, (i + s) * P:(i + s + 1) * P],
                                       vA[:, s, h * DVA:(h + 1) * DVA], start=(s == 0), stop=(s == i))
                mm.then_inc(apv, 1)
            pe.wait_ge(y_ready, 2 * HM + 2)
            output(U0_DA_OUT, HA, VC // 2, 2)
            moe(1)


CONSTS = 16 * (4 + 2 * 6 + 4)

_INS = ['x', 'norm_mix', 'norm_ffn', 'ml_w_in', 'ml_conv', 'ml_b_i', 'ml_b_f', 'ml_norm', 'ml_w_out',
        'da_w_in', 'da_lq1', 'da_lk1', 'da_lq2', 'da_lk2', 'da_norm', 'da_w_out',
        'moe_w_group', 'moe_b_group', 'moe_w_expert', 'moe_b_expert', 'moe_w_gu', 'moe_w_down', 'final_norm']


def kernel(**inputs):
    import numpy as _np
    import concourse.bacc as _bacc
    from concourse.bass_utils import run_bass_kernel_spmd as _run

    nc = _bacc.Bacc("TRN2", target_bir_lowering=False, num_devices=1)
    arrays, args = {}, []
    for name in _INS:
        a = _np.ascontiguousarray(inputs[name])
        arrays[f"in_{name}_dram"] = a
        args.append(nc.dram_tensor(f"in_{name}_dram", a.shape, mybir.dt.from_np(a.dtype), kind="ExternalInput").ap())
    args.append(nc.dram_tensor("out_0_dram", (1, T, D), F32, kind="ExternalOutput").ap())
    program(nc, *args)
    r = _run(nc, [arrays], core_ids=[0])
    return r.results[0]["out_0_dram"]
```

```python
import math
from contextlib import ExitStack

import concourse.bass as bass
from concourse import mybir

F32 = mybir.dt.float32
F32R = mybir.dt.float32r
BF16 = mybir.dt.bfloat16
I32 = mybir.dt.int32
ALU = mybir.AluOpType
ACT = mybir.ActivationFunctionType
AX_X = mybir.AxisListType.X

P = 128
D = 1024
T = 256
NT = T // P
DC = D // P
EPS = 1e-6
HM = 4
DQK = 256
DV = 512
QC = 2 * HM * DQK // P
VM = HM * DV
VC = VM // P
TAPS = 4
HA = 8
DH = 64
DVA = 128
DA_EPS = 1e-5
G = 4
EG = 8
E = G * EG
F = D // 4
LOGITS = G + E
BIG = 1e30
LAMBDA_INIT = 0.8 - 0.6 * math.exp(-0.3 * 1)

UNIT = 2048
RING = 12
CH = 512
BUFS = 4
ML_FIRST = 2
MOE_FIRST = 2
AFTER = (2, 4, 6, 7)
W = P
NPOS = 2 * T
LEAD = W
XS = LEAD + NPOS + W
NPC = NPOS // P
UE = 3
EB = RING // UE
TURNS = E // EB
U_ML_IN = 24
U_ML_OUT = 8
U_MOE = UE * E
U_DA_IN = 12
U_DA_OUT = 4
U0_ML_OUT = U_ML_IN
U0_MOE0 = U0_ML_OUT + U_ML_OUT
U0_DA_IN = U0_MOE0 + U_MOE
U0_DA_OUT = U0_DA_IN + U_DA_IN
U0_MOE1 = U0_DA_OUT + U_DA_OUT
U_ALL = U0_MOE1 + U_MOE
SPLIT0 = {"ml_in": 0, "ml_out": U_ML_IN, "moe0": U_ML_IN + U_ML_OUT}
SPLIT0["da_in"] = SPLIT0["moe0"] + 2 * E
SPLIT0["da_out"] = SPLIT0["da_in"] + U_DA_IN
SPLIT0["moe1"] = SPLIT0["da_out"] + U_DA_OUT
WHOLE0 = {"moe0": 0, "moe1": E}

C_CONV = 0
C_MLN = TAPS * QC
C_DAN = C_MLN + VC
N_COLS = C_DAN + 1


def program(nc, x, norm_mix, norm_ffn, ml_w_in, ml_conv, ml_b_i, ml_b_f, ml_norm, ml_w_out,
            da_w_in, da_lq1, da_lk1, da_lq2, da_lk2, da_norm, da_w_out,
            moe_w_group, moe_b_group, moe_w_expert, moe_b_expert, moe_w_gu, moe_w_down,
            final_norm, out):
    with ExitStack() as ctx:
        def sb(name, shape, dt=F32):
            return ctx.enter_context(nc.sbuf_tensor(name, shape, dt))

        def sem(name):
            return ctx.enter_context(nc.semaphore(name))

        ring = sb("ring", [P, RING, UNIT])
        xres = sb("xres", [P, NT, D])
        xTh = sb("xTh", [P, DC, T], F32R)
        xTl = sb("xTl", [P, DC, T], F32R)
        wh = sb("wh", [P, BUFS, CH], F32R)
        wl = sb("wl", [P, BUFS, CH], F32R)
        big = sb("big", [P, 12 * 1024])
        qkT = big[:, 0:QC * T].rearrange("p (c t) -> p c t", c=QC)
        v_sb = big[:, 4096:8192].rearrange("p (i v) -> p i v", i=NT)
        og = big[:, 8192:12288].rearrange("p (i v) -> p i v", i=NT)
        vA = big[:, 4096:6144].rearrange("p (i v) -> p i v", i=NT)
        Xs = big[:, 0:DC * XS].rearrange("p (c s) -> p c s", c=DC)
        Ys = big[:, DC * XS:2 * DC * XS].rearrange("p (c s) -> p c s", c=DC)
        xn = big[:, 6144:8192].rearrange("p (i d) -> p i d", i=NT)
        hit_w = big[:, 9216:10240].rearrange("p (i s) -> p i s", i=NT)
        hit_t = big[:, 10240:10752]
        wk = sb("wk", [P, 2304])
        wT = wk[:, 0:4 * 384].rearrange("p (h n) -> p h n", h=HM)
        ew = wk[:, 0:4 * 384].rearrange("p (b c n) -> p b c n", b=2, c=2)
        sT = wk[:, 1536:2304].rearrange("p (b n) -> p b n", b=2)
        diag = wk[:, 0:2 * HM * P].rearrange("p (h i t) -> p h i t", h=HM, i=NT)
        aT = wk[:, 0:512].rearrange("p (b c t) -> p b c t", b=2, c=2)
        a_sb = wk[:, 1024:1536].rearrange("p (b f) -> p b f", b=2)
        sg_sb = wk[:, 1536:2048].rearrange("p (b f) -> p b f", b=2)
        lgT = wk[0:LOGITS, 1536:1536 + T]
        gr = wk[0:HM, 0:8 * T].rearrange("h (r t) -> h r t", t=T)
        hitT = sb("hitT", [P, NPC, T], F32R)
        w_pos = sb("w_pos", [P, NPC])
        conv_u = sb("conv_u", [P, 2, T])
        iota = conv_u[:, :, :].rearrange("p b t -> p (b t)")
        lam_in = wk[:, 0:4 * DH].rearrange("p (n k) -> p n k", n=4)
        lam_x = wk[:, 4 * DH:6 * DH].rearrange("p (n k) -> p n k", n=2)
        ident = sb("ident", [P, P])
        neg_ts = sb("neg_ts", [P, P])
        ident_b = sb("ident_b", [P, P], BF16)
        neg_qk = sb("neg_qk", [P, P], BF16)
        att_r = sb("att_r", [P, HA, 4])
        ones = sb("ones", [P, P])
        earlier = sb("earlier", [P, P])
        warm_in = sb("warm_in", [P, 1])
        warm_out = sb("warm_out", [P, 1])
        par_rows = sb("par_rows", [N_COLS, P])
        par = sb("par", [P, N_COLS])
        g_mix = sb("g_mix", [P, 2, DC])
        g_ffn = sb("g_ffn", [P, 2, DC])
        w_gate = sb("w_gate", [P, DC, 2 * HM])
        wg_h = wh[:, 2:4, :].rearrange("p b (k m) -> p (b k) m", m=P)
        wg_l = wl[:, 2:4, :].rearrange("p b (k m) -> p (b k) m", m=P)
        wr_h = wh[:, 0:2, :].rearrange("p b (k m) -> p (b k) m", m=P)
        wr_l = wl[:, 0:2, :].rearrange("p b (k m) -> p (b k) m", m=P)
        xnh = xTh[:, :, :].rearrange("p c t -> p (c t)").rearrange("p (i d) -> p i d", i=NT)
        xnl = xTl[:, :, :].rearrange("p c t -> p (c t)").rearrange("p (i d) -> p i d", i=NT)
        hit = wh[:, 2:4, :]
        gT = wk[0:2 * HM, 2048:2048 + T]
        b_i = sb("b_i", [HM, 1])
        b_f = sb("b_f", [HM, 1])
        w_rout = sb("w_rout", [P, 2, DC, LOGITS])
        b_rout = sb("b_rout", [P, 2, NT, LOGITS])
        lam_s = sb("lam_s", [P, 8])
        st = sb("st", [P, 64])
        gc = sb("gc", [P, NT, 2 * HM])
        lg = sb("lg", [P, NT, LOGITS])
        rt = wk[:, 1024:1024 + 6 * NT * E].rearrange("p (n i e) -> p n i e", n=6, i=NT)
        win = sb("win", [1, 2 * E + 1], I32)
        zeros = sb("zeros", [P, E])
        rank_w = sb("rank_w", [P, E])
        ps = ctx.enter_context(nc.psum_tensor("ps", [P, 8, 512], F32))

        class Pass:
            def __init__(self, tag, unit_loaded, h_made, l_made, chunk_used, whole_used):
                self.unit_loaded = unit_loaded
                self.h_made = h_made
                self.l_made = l_made
                self.chunk_used = chunk_used
                self.whole_used = whole_used
                self.xw_h = sem(tag + "xw_h")
                self.xw_l = sem(tag + "xw_l")
                self.silu_done = sem(tag + "silu_done")
                self.a_ready = sem(tag + "a_ready")
                self.a_T = sem(tag + "a_T")
                self.aT_ready = sem(tag + "aT_ready")
                self.y_act = sem(tag + "y_act")
                self.y_dve = sem(tag + "y_dve")

        def expert_sems(tag):
            return [sem(f"{tag}expert_loaded{j}") for j in range(EB)]

        unit_loaded = [sem(f"unit_loaded{i}") for i in range(RING)]
        h_made = sem("h_made")
        l_made = sem("l_made")
        chunk_used = sem("chunk_used")
        whole_used = sem("whole_used")
        main = Pass("", unit_loaded, h_made, l_made, chunk_used, whole_used)
        again = [Pass(f"again{n}_", expert_sems(f"again{n}_"), sem(f"again{n}_h_made"), sem(f"again{n}_l_made"),
                      sem(f"again{n}_chunk_used"), sem(f"again{n}_whole_used")) for n in range(2)]
        ys_act = sem("ys_act")
        ys_dve = sem("ys_dve")
        small_split = sem("small_split")
        wg_zero = sem("wg_zero")
        xh_ready = sem("xh_ready")
        xl_ready = sem("xl_ready")
        gates_sel = sem("gates_sel")
        gates_copied = sem("gates_copied")
        pads_zero = sem("pads_zero")
        asg_ready = sem("asg_ready")
        rank_mm = sem("rank_mm")
        win_ready = sem("win_ready")
        hit_ready = sem("hit_ready")
        hitw_ready = sem("hitw_ready")
        gath_mm = sem("gath_mm")
        xs_act = sem("xs_act")
        xs_dve = sem("xs_dve")
        hit_T = sem("hit_T")
        hitT_act = sem("hitT_act")
        hitT_dve = sem("hitT_dve")
        ys_T = sem("ys_T")
        yn_act = sem("yn_act")
        yn_dve = sem("yn_dve")
        comb_mm = sem("comb_mm")
        x_loaded = sem("x_loaded")
        g_mix_loaded = sem("g_mix_loaded")
        w_gate_loaded = sem("w_gate_loaded")
        conv_tap = sem("conv_tap")
        act_warm = sem("act_warm")
        warm_ready = sem("warm_ready")
        lgT_ready = sem("lgT_ready")
        log_T = sem("log_T")
        xnh_ready = sem("xnh_ready")
        xnl_ready = sem("xnl_ready")
        par_loaded = sem("par_loaded")
        consts_loaded = sem("consts_loaded")
        tables_made = sem("tables_made")
        pool_step = sem("pool_step")
        par_T = sem("par_T")
        par_ready = sem("par_ready")
        act_step = sem("act_step")
        dve_step = sem("dve_step")
        squares = sem("squares")
        ms_ready = sem("ms_ready")
        root_ready = sem("root_ready")
        xn_ready = sem("xn_ready")
        xn_T = sem("xn_T")
        gates_mm = sem("gates_mm")
        gates_read = sem("gates_read")
        gate_exp = sem("gate_exp")
        gate_pre = sem("gate_pre")
        gate_rows = sem("gate_rows")
        gate_emt = sem("gate_emt")
        gate_cols_mm = sem("gate_cols_mm")
        gate_cols = sem("gate_cols")
        rows_bcast = sem("rows_bcast")
        conv_done = sem("conv_done")
        qk_ready = sem("qk_ready")
        vo_read = sem("vo_read")
        sc_mm = sem("sc_mm")
        dm_ready = sem("dm_ready")
        wt_ready = sem("wt_ready")
        s_ready = sem("s_ready")
        pv_mm = sem("pv_mm")
        hsq = sem("hsq")
        hms = sem("hms")
        hroot = sem("hroot")
        y_ready = sem("y_ready")
        y_T = sem("y_T")
        yh_ready = sem("yh_ready")
        yl_ready = sem("yl_ready")
        diag_ready = sem("diag_ready")
        res_done = sem("res_done")
        log_mm = sem("log_mm")
        gneg = sem("gneg")
        gsum = sem("gsum")
        ediff = sem("ediff")
        eexp = sem("eexp")
        lam_p = sem("lam_p")
        lam_e = sem("lam_e")
        asc_mm = sem("asc_mm")
        asc_max = sem("asc_max")
        aex = sem("aex")
        aw_ready = sem("aw_ready")
        aw_T = sem("aw_T")
        awT_ready = sem("awT_ready")
        apv = sem("apv")
        apv_read = sem("apv_read")
        g_fin_loaded = sem("g_fin_loaded")
        out_ready = sem("out_ready")
        out_stored = sem("out_stored")

        wm_in = ml_w_in[0].rearrange("(p c) n -> p c n", c=DC)
        wd_in = da_w_in[0].rearrange("(p c) n -> p c n", c=DC)
        wm_out = ml_w_out[0].rearrange("(c p) n -> p c n", p=P)
        wd_out = da_w_out[0].rearrange("(c p) n -> p c n", p=P)

        def unit(u):
            return ring[:, u % RING, :]

        def unit_is_there(eng, u):
            eng.wait_ge(unit_loaded[u % RING], 16 * (u // RING + 1))

        def bases(layer, again):
            if again:
                return 0, 0, 0, 0
            stage = f"moe{layer}"
            return (U0_MOE0, U0_MOE1)[layer], 4 * SPLIT0[stage], WHOLE0[stage], layer * E

        def loaded(s, u0, turn, j, k):
            if s is not main:
                return s.unit_loaded[j], turn * (16 * UE) + 16 * UE
            u = u0 + UE * j + k
            return s.unit_loaded[u % RING], turn * 16 + 16 * (u // RING + 1)

        def slot(u0, j, k):
            return ring[:, (u0 + UE * j + k) % RING, :]

        def back(turn, j, n):
            return (turn, j - n) if j >= n else (turn - 1, j - n + EB)

        def window(eng, turn, j, again):
            at = turn * EB + j
            if again:
                at = (2 * E - 1 - j) - turn * EB
            return eng.value_load(win[0:1, bass.ds(at, 1)], min_val=0, max_val=LEAD + NPOS)

        def over_experts(eng, step):
            for j in range(EB):
                step(0, j, True, False)
            with eng.Fori(1, TURNS) as turn:
                for j in range(EB):
                    step(turn, j, False, False)
            step(TURNS, 0, False, True)

        def Yn(b):
            if b < NPC:
                lo = slice(b % NPC * CH, (b % NPC + 1) * CH)
                return [t[:, :, :].rearrange("p c t -> p (c t)")[:, lo] for t in (xTh, xTl)]
            return wh[:, b - NPC, :], wl[:, b - NPC, :]

        block = ctx.enter_context(nc.Block())

        frees = []
        for split, count in ((1, U_ML_IN + U_ML_OUT), (2, E), (1, U_DA_IN + U_DA_OUT), (2, E)):
            for n in range(count):
                frees += [True, True, False] if split == 2 else [bool(split)]

        def slot_free(sp, u):
            old = u - RING
            if old < 0:
                return
            n = sum(f == frees[old] for f in frees[:old + 1])
            if frees[old]:
                sp.wait_ge(l_made, 4 * n)
            else:
                sp.wait_ge(whole_used, n)

        @block.sync
        def _(sp):
            def load(u, src, shape):
                slot_free(sp, u)
                dst = unit(u).rearrange("p (c n) -> p c n", c=shape)
                sp.dma_start(dst, src).then_inc(unit_loaded[u % RING], 16)

            def load_in(u0, w, blocks):
                for nb in blocks:
                    for k in range(2):
                        load(u0 + 2 * nb + k, w[:, 4 * k:4 * k + 4, nb * CH:(nb + 1) * CH], 4)

            def load_out(u0, w, units):
                for k in range(units):
                    load(u0 + k, w[:, 2 * k:2 * k + 2, :], 2)

            def load_moe(layer, s, again):
                gu = moe_w_gu[layer].rearrange("e (p c) f -> e p c f", c=DC)
                dn = moe_w_down[layer].rearrange("e (p c) n -> e p c n", c=2)
                u0, cb, wb, _ = bases(layer, again)

                def load_expert(turn, e, j, peeled):
                    e = bass.ds(e, 1)
                    for k in range(UE):
                        u = u0 + UE * j + k
                        if not peeled and k < 2:
                            sp.wait_ge(s.l_made, turn * (8 * EB) + (cb - 8 * EB + 8 * j + 4 * k + 4))
                        elif not peeled:
                            sp.wait_ge(s.whole_used, turn * EB + (wb - EB + j + 1))
                        elif not again:
                            slot_free(sp, u)
                        src = gu[e, :, 4 * k:4 * k + 4, :] if k < 2 else dn[e, :, :, :]
                        sp.dma_start(slot(u0, j, k).rearrange("p (c n) -> p c n", c=src.shape[2]),
                                     src.rearrange("e p c f -> (e p) c f")).then_inc(loaded(s, u0, 0, j, k)[0], 16)

                for j in range(EB):
                    load_expert(0, (E - 1 - j) if again else j, j, True)
                with sp.Fori(1, TURNS) as turn:
                    first = sp.snap(turn * -EB + (E - 1) if again else turn * EB)
                    for j in range(EB):
                        load_expert(turn, first - j if again else first + j, j, False)

            def moe(layer):
                load_moe(layer, main, False)
                sp.wait_ge(win_ready, layer + 1)
                most = sp.value_load(win[0:1, 2 * E:2 * E + 1], min_val=0, max_val=T)
                with sp.If(most > W):
                    _, cb, wb, _ = bases(layer, False)
                    sp.wait_ge(l_made, cb + 8 * E)
                    sp.wait_ge(whole_used, wb + E)
                    load_moe(layer, again[layer], True)
                    sp.wait_ge(again[layer].l_made, 8 * E)
                    sp.wait_ge(again[layer].whole_used, E)

            for i in range(NT):
                sp.dma_start(xres[:, i, :], x[0, i * P:(i + 1) * P, :]).then_inc(x_loaded, 16)
            sp.dma_start(g_mix[:], norm_mix.rearrange("l (p c) -> p l c", c=DC)).then_inc(g_mix_loaded, 16)
            sp.dma_start(w_gate[:], wm_in[:, :, U_ML_IN // 2 * 512:]).then_inc(w_gate_loaded, 16)
            load_in(0, wm_in, range(RING // 2))
            sp.dma_start(b_i[:], ml_b_i.rearrange("o h -> h o")).then_inc(consts_loaded, 16)
            sp.dma_start(b_f[:], ml_b_f.rearrange("o h -> h o")).then_inc(consts_loaded, 16)
            sp.dma_start(g_ffn[:], norm_ffn.rearrange("l (p c) -> p l c", c=DC)).then_inc(consts_loaded, 16)
            for layer in range(2):
                sp.dma_start(w_rout[:, layer, :, 0:G], moe_w_group[layer].rearrange("(p c) g -> p c g", c=DC)).then_inc(consts_loaded, 16)
                sp.dma_start(w_rout[:, layer, :, G:], moe_w_expert[layer].rearrange("(p c) g -> p c g", c=DC)).then_inc(consts_loaded, 16)
                for i in range(NT):
                    sp.dma_start(b_rout[:, layer, i, 0:G], moe_b_group[layer:layer + 1, :].to_broadcast([P, G])).then_inc(consts_loaded, 16)
                    sp.dma_start(b_rout[:, layer, i, G:], moe_b_expert[layer:layer + 1, :].to_broadcast([P, E])).then_inc(consts_loaded, 16)
            for n, src in enumerate((da_lq1, da_lk1, da_lq2, da_lk2)):
                sp.dma_start(lam_in[:, n, :], src.to_broadcast([P, DH])).then_inc(consts_loaded, 16)
            load_in(0, wm_in, range(RING // 2, U_ML_IN // 2))
            load_out(U0_ML_OUT, wm_out, U_ML_OUT)
            moe(0)
            load_in(U0_DA_IN, wd_in, range(U_DA_IN // 2))
            load_out(U0_DA_OUT, wd_out, U_DA_OUT)
            moe(1)
            sp.wait_ge(res_done, 16)
            sp.dma_start(ring[:, 0, 0:D], final_norm.rearrange("(o d) -> o d", o=1).to_broadcast([P, D])).then_inc(g_fin_loaded, 16)
            for i in range(NT):
                sp.wait_ge(out_ready, i + 1)
                sp.dma_start(out[0, i * P:(i + 1) * P, :], xn[:, i, :]).then_inc(out_stored, 16)
            sp.wait_ge(out_stored, 16 * NT)

        @block.gpsimd
        def _(pool):
            pool.dma_start(par_rows[C_CONV:C_MLN, :], ml_conv[0].rearrange("j (c p) -> (j c) p", p=P)).then_inc(par_loaded, 16)
            pool.dma_start(par_rows[C_MLN:C_DAN, :], ml_norm[0].rearrange("(c p) -> c p", p=P)).then_inc(par_loaded, 16)
            pool.dma_start(par_rows[C_DAN:N_COLS, :], da_norm).then_inc(par_loaded, 16)
            nc.gpsimd.memset(warm_in[:], 1.0).then_inc(warm_ready, 1)
            steps = [0]

            def done(ins):
                steps[0] += 1
                ins.then_inc(pool_step, 1)
                pool.wait_ge(pool_step, steps[0])

            done(nc.gpsimd.memset(ident[:], 0.0))
            done(nc.gpsimd.affine_select(out=ident[:], in_=ident[:], compare_op=ALU.not_equal, fill=1.0,
                                         base=0, pattern=[[-1, P]], channel_multiplier=1))
            done(nc.gpsimd.memset(neg_ts[:], 0.0))
            for w in (wg_h, wg_l):
                nc.gpsimd.tensor_copy(w, neg_ts[:].rearrange("p (o m) -> p o m", o=1).to_broadcast([P, DC, P])).then_inc(wg_zero, 1)
            pool.wait_ge(wg_zero, 2)
            done(nc.gpsimd.affine_select(out=neg_ts[:], in_=neg_ts[:], compare_op=ALU.is_ge, fill=-BIG,
                                         base=0, pattern=[[1, P]], channel_multiplier=-1))
            done(nc.gpsimd.memset(neg_qk[:], 0.0))
            done(nc.gpsimd.affine_select(out=neg_qk[:], in_=neg_qk[:], compare_op=ALU.is_ge,
                                         fill=-BIG, base=0, pattern=[[-1, P]], channel_multiplier=1))
            done(nc.gpsimd.tensor_copy(ident_b[:], ident[:]))
            done(nc.gpsimd.memset(earlier[:], 1.0))
            done(nc.gpsimd.affine_select(out=earlier[:], in_=earlier[:], compare_op=ALU.is_gt, fill=0.0,
                                         base=0, pattern=[[1, P]], channel_multiplier=-1))
            done(nc.gpsimd.memset(zeros[:], 0.0))
            done(nc.gpsimd.iota(rank_w[:], [[-1, E]], base=E, channel_multiplier=0,
                                allow_small_or_imprecise_dtypes=True))
            nc.gpsimd.memset(ones[:], 1.0).then_inc(tables_made, 1)
            for layer in range(2):
                pool.wait_ge(res_done, 4 * (2 * layer + 1))
                nc.gpsimd.iota(iota, [[1, NPOS]], base=0, channel_multiplier=0,
                               allow_small_or_imprecise_dtypes=True).then_inc(pads_zero, 1)
                nc.gpsimd.memset(Xs[:, :, 0:LEAD], 0.0).then_inc(pads_zero, 1)
                nc.gpsimd.memset(Xs[:, :, LEAD + NPOS:XS], 0.0).then_inc(pads_zero, 1)
                pool.wait_ge(xnh_ready, layer + 1)
                for i in range(NT):
                    nc.gpsimd.tensor_tensor(xnl[:, i, :], xn[:, i, :], xnh[:, i, :].bitcast(F32), ALU.subtract).then_inc(xnl_ready, 1)

        @block.scalar
        def _(act):
            warmed = [0]

            def warm(func):
                if warmed[0]:
                    act.wait_ge(act_warm, warmed[0])
                nc.scalar.activation(warm_out[:], warm_in[:], func).then_inc(act_warm, 1)
                warmed[0] += 1

            def norm(n):
                if n:
                    warm(ACT.Sqrt)
                for i in range(NT):
                    if n == 0:
                        act.wait_ge(x_loaded, 16 * NT)
                    else:
                        act.wait_ge(res_done, 4 * (n - 1) + 2 * (i + 1))
                    nc.scalar.activation(xn[:, i, :], xres[:, i, :], ACT.Square,
                                         accum_out=st[:, i:i + 1]).then_inc(squares, 1)
                    act.wait_ge(ms_ready, NT * n + i + 1)
                    nc.scalar.activation(st[:, 4 + i:5 + i], st[:, 2 + i:3 + i], ACT.Sqrt).then_inc(root_ready, 1)

            def evac_T(n, g_col):
                for c in range(DC):
                    act.wait_ge(xn_T, 4 * n + c // 2 + 1)
                    nc.scalar.mul(xTh[:, c, :], ps[:, 4 + c // 2, c % 2 * T:(c % 2 + 1) * T], g_col[:, c:c + 1]).then_inc(xh_ready, 1)

            def make_h(s, ch, c, src):
                if not isinstance(ch, int) or ch >= BUFS:
                    act.wait_ge(s.chunk_used, ch - (BUFS - 1))
                nc.scalar.copy(wh[:, c % BUFS, :], src).then_inc(s.h_made, 1)

            def first_h(u0, ch0, n=BUFS):
                unit_is_there(act, u0)
                for c in range(n):
                    make_h(main, ch0 + c, c, unit(u0)[:, c * CH:(c + 1) * CH])

            def output(u0, ch0, chunks, T0, n, g_cols):
                def pair(b):
                    act.wait_ge(y_T, T0 // 2 + b + 1)
                    for c in (2 * b, 2 * b + 1):
                        nc.scalar.mul(xTh[:, c % DC, :], ps[:, 4 + b % 4, c % 2 * T:(c % 2 + 1) * T], g_cols(c)).then_inc(yh_ready, 1)

                for b in range(4):
                    pair(b)
                for c in range(BUFS, 2 * chunks):
                    if c % 4 == 0:
                        unit_is_there(act, u0 + c // 4)
                    make_h(main, ch0 + c, c, unit(u0 + c // 4)[:, c % 4 * CH:(c % 4 + 1) * CH])
                    if c % 4 == 3 and c // 4 + 3 < chunks // 2:
                        pair(c // 4 + 3)

            def split_block(u0, ch0, nb, after, there=BUFS):
                for c in range(there if nb == 0 else 0, DC):
                    u = u0 + 2 * nb + c // 4
                    if c % 4 == 0:
                        unit_is_there(act, u)
                    make_h(main, ch0 + 8 * nb + c, c, unit(u)[:, c % 4 * CH:(c % 4 + 1) * CH])
                    if nb and c in AFTER:
                        after(nb - 1, AFTER.index(c))

            act.wait_ge(warm_ready, 1)
            warm(ACT.Sqrt)
            norm(0)
            first_h(0, 0, ML_FIRST)
            act.wait_ge(g_mix_loaded, 16)
            evac_T(0, g_mix[:, 0, :])

            def ml_after(nb, k):
                c = 4 * nb + k
                if nb < 4:
                    act.wait_ge(chunk_used, 8 * (nb + 1))
                    if c >= 2:
                        act.wait_ge(qk_ready, c - 1)
                    w = par[:, C_CONV + (TAPS - 1) * QC + c:C_CONV + (TAPS - 1) * QC + c + 1]
                    nc.scalar.mul(conv_u[:, c % 2, :], ps[:, c % 8, 0:T], w).then_inc(conv_tap, 1)
                if 0 < c <= QC:
                    act.wait_ge(conv_done, c)
                    nc.scalar.activation(qkT[:, c - 1, :], conv_u[:, (c - 1) % 2, :], ACT.Silu).then_inc(qk_ready, 1)
                if nb >= 4 and k % 2 == 0:
                    b, i = (nb - 4) % 4, k // 2
                    act.wait_ge(chunk_used, 8 * (nb + 1))
                    src = ps[:, (2 * b + i) % 8, :]
                    if nb < 8:
                        nc.scalar.copy(v_sb[:, i, b * DV:(b + 1) * DV], src).then_inc(vo_read, 1)
                    else:
                        nc.scalar.activation(og[:, i, b * DV:(b + 1) * DV], src, ACT.Sigmoid).then_inc(vo_read, 1)

            act.wait_ge(gates_mm, 1)
            for nb in range(12):
                split_block(0, 0, nb, ml_after, ML_FIRST)
                if nb == 4:
                    act.wait_ge(lam_p, 2)
                    nc.scalar.activation(lam_s[:, 2:4], lam_s[:, 0:2], ACT.Exp).then_inc(lam_e, 1)
                if nb == 6:
                    act.wait_ge(gate_pre, 1)
                    nc.scalar.activation(gr[:, 2, :], gr[:, 1, :], ACT.Exp, scale=-1.0).then_inc(act_step, 1)
                    act.wait_ge(act_step, 1)
                    nc.scalar.activation(gr[:, 3, :], gr[:, 2, :], ACT.Ln, bias=1.0).then_inc(gate_exp, 1)
                if nb == 8:
                    act.wait_ge(gate_rows, 1)
                    nc.scalar.activation(gr[:, 7, :], gr[:, 6, :], ACT.Exp, scale=-1.0).then_inc(gate_emt, 1)
            warm(ACT.Exp)
            act.wait_ge(gate_cols, 1)
            for h in range(HM):
                act.wait_ge(dm_ready, h + 1)
                nc.scalar.activation(wT[:, h, 0:256], wT[:, h, 0:256], ACT.Exp, bias=gc[:, 0, h:h + 1]).then_inc(wt_ready, 1)
                nc.scalar.activation(wT[:, h, 256:384], wT[:, h, 256:384], ACT.Exp, bias=gc[:, 1, h:h + 1]).then_inc(wt_ready, 1)
            for k in range(4):
                ml_after(11, k)
            first_h(U0_ML_OUT, 4 * SPLIT0["ml_out"])
            warm(ACT.Sqrt)
            for h in range(HM):
                for i in range(NT):
                    k = 2 * h + i
                    act.wait_ge(y_ready, k + 1)
                    if k:
                        act.wait_ge(hsq, k)
                    nc.scalar.activation(iota, ps[:, 4 + 2 * (h % 2) + i, :], ACT.Square, scale=st[:, 48 + k:49 + k],
                                         accum_out=st[:, 40 + k:41 + k]).then_inc(hsq, 1)
                if h == HM - 2:
                    act.wait_ge(hms, 1)
                    nc.scalar.activation(st[:, 16:22], st[:, 8:14], ACT.Sqrt).then_inc(hroot, 1)
            act.wait_ge(hms, 2)
            nc.scalar.activation(st[:, 22:24], st[:, 14:16], ACT.Sqrt).then_inc(hroot, 1)
            output(U0_ML_OUT, 4 * SPLIT0["ml_out"], VC, 0, 0, lambda c: par[:, C_MLN + c:C_MLN + c + 1])

            def experts(layer, s, again):
                u0, cb, wb, eb = bases(layer, again)

                def h_chunks(turn, j, cs):
                    for c in cs:
                        k = c // 4
                        if c % 4 == 0:
                            act.wait_ge(*loaded(s, u0, turn, j, k))
                        make_h(s, turn * (8 * EB) + (cb + 8 * j + c), c, slot(u0, j, k)[:, c % 4 * CH:(c % 4 + 1) * CH])

                def window_h(turn, j):
                    w = window(act, turn, j, again)
                    if not again and isinstance(turn, int) and turn + j == 0:
                        act.wait_ge(xs_act, 4 * (layer + 1))
                        act.wait_ge(xs_dve, 4 * (layer + 1))
                        act.wait_ge(pads_zero, 3 * (layer + 1))
                    nc.scalar.copy(xTh[:, :, j % 2 * W:(j % 2 + 1) * W], Xs[:, :, bass.ds(w, W)]).then_inc(s.xw_h, 1)

                def y_out(turn, j):
                    w = window(act, turn, j, again)
                    if not isinstance(turn, int) or turn + j:
                        act.wait_ge(s.y_act, turn * EB + (eb + j))
                    act.wait_ge(s.whole_used, turn * EB + (wb + j + 1))
                    nc.scalar.copy(Ys[:, 4:8, bass.ds(w, W)], ps[:, 2 * (j % 2) + 1, :].rearrange("p (c t) -> p c t", c=4)).then_inc(s.y_act, 1)

                def step(turn, j, first, last):
                    n = turn * EB + (eb + j)
                    b = (j - 1) % 2
                    has_before = not first or j >= 1
                    early = first and not again and j < 2
                    if early and j == 0:
                        window_h(0, 0)
                        act.wait_ge(hit_T, 3 * layer + 1)
                        nc.scalar.copy(hitT[:, 0:2, :], ps[:, 0, :].rearrange("p (k t) -> p k t", k=2)).then_inc(hitT_act, 1)
                        act.wait_ge(hit_T, 3 * layer + 2)
                        h_chunks(0, 0, range(MOE_FIRST, 4))
                        window_h(0, 1)
                    elif not last:
                        h_chunks(turn, j, range(4))
                    if has_before:
                        act.wait_ge(s.chunk_used, turn * (8 * EB) + (cb + 8 * j))
                        if not first or j >= 3:
                            act.wait_ge(s.a_ready, n - 2)
                        nc.scalar.activation(sg_sb[:, b, :], ps[:, 4 + b, 0:F], ACT.Silu).then_inc(s.silu_done, 1)
                    if not last and not early:
                        window_h(turn, j)
                    if not first or j >= 3:
                        y_out(*back(turn, j, 3))
                    late = first and j == 1
                    if not last:
                        h_chunks(turn, j, range(4, 8 if late else 5))
                    if has_before:
                        act.wait_ge(s.a_T, n)
                        nc.scalar.copy(aT[:, b, :, :], ps[:, 6 + b, 0:2 * P].rearrange("p (c t) -> p c t", c=2)).then_inc(s.aT_ready, 1)
                    if not last and not late:
                        h_chunks(turn, j, range(5, 8))

                over_experts(act, step)
                for j in (EB - 2, EB - 1):
                    y_out(TURNS - 1, j)
                act.wait_ge(s.y_act, eb + E)

            def moe(layer):
                n = 2 * layer + 1
                norm(n)
                evac_T(n, g_ffn[:, layer, :])
                warm(ACT.Exp)
                act.wait_ge(log_mm, layer + 1)
                nc.scalar.copy(lgT, ps[0:LOGITS, 0, 0:T]).then_inc(lgT_ready, 1)
                nc.scalar.copy(xnh, xn).then_inc(xnh_ready, 1)
                first_h((U0_MOE0, U0_MOE1)[layer], 4 * SPLIT0[f"moe{layer}"], MOE_FIRST)
                act.wait_ge(gneg, layer + 1)
                for i in range(NT):
                    nc.scalar.activation(rt[:, 0, i, 0:G], lg[:, i, 0:G], ACT.Exp, bias=st[:, 18 + i:19 + i],
                                         accum_out=st[:, 20 + i:21 + i]).then_inc(gsum, 1)
                act.wait_ge(ediff, layer + 1)
                nc.scalar.activation(st[:, 28:30], st[:, 26:28], ACT.Exp).then_inc(eexp, 1)
                warm(ACT.Silu)
                for c in range(0, DC, 2):
                    act.wait_ge(gath_mm, DC * layer + c + 1)
                    nc.scalar.mul(Xs[:, c, LEAD:LEAD + NPOS], ps[:, c, :], g_ffn[:, layer, c:c + 1]).then_inc(xs_act, 1)
                act.wait_ge(win_ready, layer + 1)
                most = act.value_load(win[0:1, 2 * E:2 * E + 1], min_val=0, max_val=T)
                experts(layer, main, False)
                with act.If(most > W):
                    act.wait_ge(main.y_dve, E * (layer + 1))
                    experts(layer, again[layer], True)
                act.sem_inc(ys_act, 1)
                act.wait_ge(hitT_dve, layer + 1)
                for b in range(2 * NPC):
                    act.wait_ge(ys_T, 2 * NPC * layer + b + 1)
                    nc.scalar.mul(Yn(b)[0], ps[:, 4 + b % 4, :], w_pos[:, b // 2:b // 2 + 1]).then_inc(yn_act, 1)

            moe(0)
            norm(2)
            first_h(U0_DA_IN, 4 * SPLIT0["da_in"])
            evac_T(2, g_mix[:, 1, :])

            def da_after(nb, k):
                if nb < 4:
                    c = 4 * nb + k
                    act.wait_ge(chunk_used, 4 * SPLIT0["da_in"] + 8 * (nb + 1))
                    nc.scalar.copy(qkT[:, c, :], ps[:, c % 8, 0:T]).then_inc(qk_ready, 1)
                elif k % 2 == 0:
                    b, i = nb - 4, k // 2
                    act.wait_ge(chunk_used, 4 * SPLIT0["da_in"] + 8 * (nb + 1))
                    nc.scalar.copy(vA[:, i, b * 512:(b + 1) * 512], ps[:, 4 * b + i, :]).then_inc(vo_read, 1)

            for nb in range(6):
                split_block(U0_DA_IN, 4 * SPLIT0["da_in"], nb, da_after)
            warm(ACT.Exp)

            def exps(h):
                b = h % 2
                act.wait_ge(asc_max, h + 1)
                for i in range(NT):
                    seg = slice(i * P, (2 * i + 1) * P)
                    for c in range(2):
                        k = 4 * b + 2 * i + c
                        nc.scalar.activation(ew[:, b, c, seg], ps[:, 2 * (1 - b) + c, seg], ACT.Exp,
                                             bias=st[:, 16 + k:17 + k], scale=DH ** -0.5,
                                             accum_out=st[:, 24 + k:25 + k]).then_inc(aex, 1)

            def head_out(h):
                act.wait_ge(apv, h + 1)
                if h:
                    act.wait_ge(apv_read, h)
                for i in range(NT):
                    nc.scalar.activation(conv_u[:, i, 0:DVA], ps[:, 6 + h % 2, i * P:(i + 1) * P], ACT.Square,
                                         scale=att_r[:, h, 2 * i:2 * i + 1], accum_out=st[:, 40 + HA * i + h:41 + HA * i + h])
                for i in range(NT):
                    mul = nc.scalar.mul(og[:, i, h * DVA:(h + 1) * DVA], ps[:, 6 + h % 2, i * P:(i + 1) * P], att_r[:, h, 2 * i:2 * i + 1])
                mul.then_inc(apv_read, 1)

            exps(0)
            for k in range(4):
                da_after(5, k)
            for h in range(HA):
                act.wait_ge(aw_T, h + 1)
                nc.scalar.copy(sT[:, h % 2, :], ps[:, 4 + h % 2, 0:384]).then_inc(awT_ready, 1)
                if h + 1 < HA:
                    exps(h + 1)
                if h:
                    head_out(h - 1)
            first_h(U0_DA_OUT, 4 * SPLIT0["da_out"])
            head_out(HA - 1)
            warm(ACT.Sqrt)
            act.wait_ge(hms, 3)
            nc.scalar.activation(st[:, 40:56], st[:, 40:56], ACT.Sqrt).then_inc(hroot, 1)
            output(U0_DA_OUT, 4 * SPLIT0["da_out"], HA, VC, 2, lambda c: lam_s[:, 6:7])
            moe(1)
            norm(4)

        @block.vector
        def _(dve):
            steps = [0]

            def done(ins):
                steps[0] += 1
                ins.then_inc(dve_step, 1)
                dve.wait_ge(dve_step, steps[0])

            def norm(n):
                for i in range(NT):
                    dve.wait_ge(squares, NT * n + i + 1)
                    nc.vector.tensor_scalar(st[:, 2 + i:3 + i], st[:, i:i + 1], 1.0 / D, EPS, ALU.mult, ALU.add).then_inc(ms_ready, 1)
                    dve.wait_ge(root_ready, NT * n + i + 1)
                    done(nc.vector.reciprocal(st[:, 6 + i:7 + i], st[:, 4 + i:5 + i]))
                    if n < 4:
                        nc.vector.tensor_scalar(xn[:, i, :], xres[:, i, :], st[:, 6 + i:7 + i], None, ALU.mult).then_inc(xn_ready, 1)
                    else:
                        dve.wait_ge(g_fin_loaded, 16)
                        nc.vector.scalar_tensor_tensor(out=xn[:, i, :], in0=xres[:, i, :], scalar=st[:, 6 + i:7 + i],
                                                       in1=ring[:, 0, 0:D], op0=ALU.mult, op1=ALU.mult).then_inc(out_ready, 1)

            def evac_T(n, g_col):
                for c in range(DC):
                    if c % 2 == 0:
                        dve.wait_ge(xh_ready, DC * n + c + 2)
                    nc.vector.scalar_tensor_tensor(out=xTl[:, c, :], in0=ps[:, 4 + c // 2, c % 2 * T:(c % 2 + 1) * T],
                                                   scalar=g_col[:, c:c + 1], in1=xTh[:, c, :].bitcast(F32),
                                                   op0=ALU.mult, op1=ALU.subtract).then_inc(xl_ready, 1)

            def make_l(s, ch, c, src):
                dve.wait_ge(s.h_made, ch + 1)
                b = c % BUFS
                nc.vector.tensor_tensor(wl[:, b, :], src, wh[:, b, :].bitcast(F32), ALU.subtract).then_inc(s.l_made, 1)

            def first_l(u0, ch0, n=BUFS):
                for c in range(n):
                    make_l(main, ch0 + c, c, unit(u0)[:, c * CH:(c + 1) * CH])

            def output(u0, ch0, chunks, T0, n, g_cols):
                def pair(b):
                    dve.wait_ge(yh_ready, T0 + 2 * b + 2)
                    for c in (2 * b, 2 * b + 1):
                        nc.vector.scalar_tensor_tensor(out=xTl[:, c % DC, :], in0=ps[:, 4 + b % 4, c % 2 * T:(c % 2 + 1) * T],
                                                       scalar=g_cols(c), in1=xTh[:, c % DC, :].bitcast(F32),
                                                       op0=ALU.mult, op1=ALU.subtract).then_inc(yl_ready, 1)

                for b in range(4):
                    pair(b)
                for c in range(BUFS, 2 * chunks):
                    make_l(main, ch0 + c, c, unit(u0 + c // 4)[:, c % 4 * CH:(c % 4 + 1) * CH])
                    if c % 4 == 3 and c // 4 + 3 < chunks // 2:
                        pair(c // 4 + 3)
                residual(n, chunk_used, ch0 + 2 * chunks)

            def split_block(u0, ch0, nb, after, there=BUFS):
                for c in range(there if nb == 0 else 0, DC):
                    make_l(main, ch0 + 8 * nb + c, c, unit(u0 + 2 * nb + c // 4)[:, c % 4 * CH:(c % 4 + 1) * CH])
                    if nb and c in AFTER:
                        after(nb - 1, AFTER.index(c))

            def split_small(h, l, w):
                done(nc.vector.tensor_copy(h, w))
                nc.vector.tensor_tensor(l, w, h.bitcast(F32), ALU.subtract).then_inc(small_split, 1)

            def residual(n, signal, count):
                for i in range(NT):
                    for half in range(2):
                        dve.wait_ge(signal, count + (i if signal is comb_mm else 0))
                        sl = xres[:, i, half * 512:(half + 1) * 512]
                        nc.vector.tensor_tensor(sl, sl, ps[:, 2 * i + half, :], ALU.add).then_inc(res_done, 1)

            norm(0)
            dve.wait_ge(w_gate_loaded, 16)
            dve.wait_ge(wg_zero, 2)
            split_small(wg_h[:, :, 0:2 * HM], wg_l[:, :, 0:2 * HM], w_gate[:])
            dve.wait_ge(g_mix_loaded, 16)
            evac_T(0, g_mix[:, 0, :])
            dve.wait_ge(par_T, 1)
            nc.vector.tensor_copy(par[:], ps[:, 0, 0:N_COLS]).then_inc(par_ready, 1)
            first_l(0, 0, ML_FIRST)
            dve.wait_ge(gates_mm, 1)
            nc.vector.tensor_copy(gT, ps[0:2 * HM, 7, 0:T]).then_inc(gates_copied, 1)

            def ml_after(nb, k):
                if nb >= 4:
                    return
                c = 4 * nb + k
                u = conv_u[:, c % 2, :]
                src = ps[:, c % 8, 0:T]
                dve.wait_ge(conv_tap, c + 1)
                for tap in range(TAPS - 2, -1, -1):
                    lag = TAPS - 1 - tap
                    w = par[:, C_CONV + tap * QC + c:C_CONV + tap * QC + c + 1]
                    ins = nc.vector.scalar_tensor_tensor(out=u[:, lag:T], in0=src[:, 0:T - lag], scalar=w,
                                                         in1=u[:, lag:T], op0=ALU.mult, op1=ALU.add)
                    if lag < TAPS - 1:
                        done(ins)
                    else:
                        ins.then_inc(conv_done, 1)

            for nb in range(12):
                split_block(0, 0, nb, ml_after, ML_FIRST)
                if nb == 3:
                    dve.wait_ge(consts_loaded, CONSTS)
                    for n in range(2):
                        nc.vector.tensor_tensor_reduce(out=lam_x[:, n, :], in0=lam_in[:, 2 * n, :], in1=lam_in[:, 2 * n + 1, :],
                                                       scale=1.0, scalar=0.0, op0=ALU.mult, op1=ALU.add,
                                                       accum_out=lam_s[:, n:n + 1]).then_inc(lam_p, 1)
                if nb == 5:
                    dve.wait_ge(lam_e, 1)
                    done(nc.vector.tensor_tensor(lam_s[:, 4:5], lam_s[:, 3:4], lam_s[:, 2:3], ALU.subtract))
                    done(nc.vector.tensor_scalar(lam_s[:, 5:6], lam_s[:, 4:5], -LAMBDA_INIT, None, ALU.add))
                    done(nc.vector.tensor_scalar(lam_s[:, 6:7], par[:, C_DAN:C_DAN + 1], 1.0 - LAMBDA_INIT, None, ALU.mult))
                if nb == 6:
                    dve.wait_ge(gates_sel, 1)
                    nc.vector.tensor_scalar(gr[:, 0, :], ps[0:HM, 7, 0:T], b_i[:, 0:1], None, ALU.add).then_inc(gates_read, 1)
                    nc.vector.tensor_scalar(gr[:, 4, :], ps[0:HM, 7, T:2 * T], b_f[:, 0:1], None, ALU.add).then_inc(gates_read, 1)
                    dve.wait_ge(gates_read, 2)
                    done(nc.vector.tensor_scalar(gr[:, 5, :], gr[:, 4, :], -1.0, None, ALU.mult))
                    nc.vector.tensor_tensor(gr[:, 1, :], gr[:, 4, :], gr[:, 5, :], ALU.max).then_inc(gate_pre, 1)
                if nb == 7:
                    dve.wait_ge(gate_exp, 1)
                    done(nc.vector.scalar_tensor_tensor(out=gr[:, 4, :], in0=gr[:, 4, :], scalar=0.0, in1=gr[:, 3, :],
                                                        op0=ALU.min, op1=ALU.subtract))
                    done(nc.vector.memset(gr[:, 3, :], 0.0))
                    done(nc.vector.tensor_tensor_scan(gr[:, 2, :], gr[:, 4, :], gr[:, 3, :], 0.0, ALU.add, ALU.add))
                    done(nc.vector.tensor_tensor(gr[:, 5, :], gr[:, 0, :], gr[:, 2, :], ALU.subtract))
                    done(nc.vector.tensor_tensor_scan(gr[:, 4, :], gr[:, 5, :], gr[:, 3, :], 0.0, ALU.max, ALU.max))
                    done(nc.vector.tensor_scalar(gr[:, 1, :], gr[:, 4, :], -1.0, None, ALU.mult))
                    nc.vector.tensor_tensor(gr[:, 6, :], gr[:, 4, :], gr[:, 2, :], ALU.add).then_inc(gate_rows, 1)
            dve.wait_ge(gate_cols_mm, 1)
            nc.vector.tensor_copy(gc[:], ps[:, 3, 0:NT * 2 * HM].rearrange("p (i k) -> p i k", i=NT)).then_inc(gate_cols, 1)
            dve.wait_ge(rows_bcast, 1)
            dve.wait_ge(gate_cols, 1)
            for h in range(HM):
                R = ps[:, h // 2, (h % 2) * T:(h % 2 + 1) * T]
                nc.vector.tensor_tensor(wT[:, h, 0:P], R[:, 0:P], neg_ts[:], ALU.add)
                nc.vector.tensor_copy(wT[:, h, P:T], R[:, P:T])
                nc.vector.tensor_tensor(wT[:, h, T:T + P], R[:, P:T], neg_ts[:], ALU.add).then_inc(dm_ready, 1)

            def head_out(h):
                b = h % 2
                dve.wait_ge(pv_mm, h + 1)
                done(nc.vector.tensor_copy(st[:, 56:58], ps[:, b, 0:2]))
                done(nc.vector.scalar_tensor_tensor(out=st[:, 58:60], in0=st[:, 56:58], scalar=-1.0, in1=st[:, 56:58],
                                                    op0=ALU.mult, op1=ALU.max))
                done(nc.vector.tensor_tensor(st[:, 60:62], st[:, 58:60], gc[:, :, HM + h], ALU.max))
                done(nc.vector.reciprocal(st[:, 48 + 2 * h:50 + 2 * h], st[:, 60:62]))
                for i in range(NT):
                    sl = og[:, i, h * DV:(h + 1) * DV]
                    dve.wait_ge(vo_read, 8 + 2 * h + i + 1)
                    nc.vector.scalar_tensor_tensor(out=sl, in0=ps[:, 4 + 2 * b + i, :], scalar=st[:, 48 + 2 * h + i:49 + 2 * h + i], in1=sl,
                                                   op0=ALU.mult, op1=ALU.mult).then_inc(y_ready, 1)

            def head_rms(heads, k):
                lo, hi = 2 * heads[0], 2 * heads[-1] + 2
                dve.wait_ge(hsq, hi)
                nc.vector.tensor_scalar(st[:, 8 + lo:8 + hi], st[:, 40 + lo:40 + hi], 1.0 / DV, EPS, ALU.mult, ALU.add).then_inc(hms, 1)
                dve.wait_ge(hroot, k + 1)
                done(nc.vector.reciprocal(st[:, 24 + lo:24 + hi], st[:, 16 + lo:16 + hi]))
                for h in heads:
                    for i in range(NT):
                        nc.vector.tensor_scalar(diag[:, h, i, :], ident[:], st[:, 24 + 2 * h + i:25 + 2 * h + i], None,
                                                ALU.mult).then_inc(diag_ready, 1)

            for h in range(HM):
                dve.wait_ge(sc_mm, h + 1)
                dve.wait_ge(wt_ready, 2 * h + 2)
                if h >= 2:
                    dve.wait_ge(pv_mm, h - 1)
                nc.vector.scalar_tensor_tensor(out=sT[:, h % 2, :], in0=ps[:, 2 + h % 2, 0:384], scalar=DQK ** -0.5,
                                               in1=wT[:, h, :], op0=ALU.mult, op1=ALU.mult).then_inc(s_ready, 1)
                if h == 1:
                    first_l(U0_ML_OUT, 4 * SPLIT0["ml_out"])
                if h:
                    head_out(h - 1)
            dve.wait_ge(s_ready, HM)
            head_rms(range(HM - 1), 0)
            head_out(HM - 1)
            head_rms((HM - 1,), 1)
            output(U0_ML_OUT, 4 * SPLIT0["ml_out"], VC, 0, 0, lambda c: par[:, C_MLN + c:C_MLN + c + 1])

            def experts(layer, s, again):
                u0, cb, wb, eb = bases(layer, again)

                def l_chunks(turn, j, cs):
                    for c in cs:
                        make_l(s, turn * (8 * EB) + (cb + 8 * j + c), c, slot(u0, j, c // 4)[:, c % 4 * CH:(c % 4 + 1) * CH])

                def window_l(turn, j):
                    w = window(dve, turn, j, again)
                    if not again and isinstance(turn, int) and turn + j == 0:
                        dve.wait_ge(xs_act, 4 * (layer + 1))
                        dve.wait_ge(xs_dve, 4 * (layer + 1))
                        dve.wait_ge(pads_zero, 3 * (layer + 1))
                    dve.wait_ge(s.xw_h, turn * EB + (eb + j + 1))
                    xs = slice(j % 2 * W, (j % 2 + 1) * W)
                    nc.vector.tensor_tensor(xTl[:, :, xs], Xs[:, :, bass.ds(w, W)], xTh[:, :, xs].bitcast(F32),
                                            ALU.subtract).then_inc(s.xw_l, 1)

                def y_out(turn, j):
                    w = window(dve, turn, j, again)
                    if not isinstance(turn, int) or turn + j:
                        dve.wait_ge(s.y_dve, turn * EB + (eb + j))
                    dve.wait_ge(s.whole_used, turn * EB + (wb + j + 1))
                    nc.vector.tensor_copy(Ys[:, 0:4, bass.ds(w, W)], ps[:, 2 * (j % 2), :].rearrange("p (c t) -> p c t", c=4)).then_inc(s.y_dve, 1)

                def step(turn, j, first, last):
                    n = turn * EB + (eb + j)
                    b = (j - 1) % 2
                    early = first and not again and j < 2
                    if early and j == 0:
                        window_l(0, 0)
                        l_chunks(0, 0, range(MOE_FIRST, 4))
                        window_l(0, 1)
                        dve.wait_ge(hit_T, 3 * layer + 3)
                        nc.vector.tensor_copy(w_pos[:], ps[:, 2, 0:NPC])
                        nc.vector.tensor_copy(hitT[:, 2:4, :], ps[:, 1, :].rearrange("p (k t) -> p k t", k=2)).then_inc(hitT_dve, 1)
                    elif not last:
                        l_chunks(turn, j, range(4))
                    if not first or j >= 1:
                        dve.wait_ge(s.silu_done, n)
                        if not first or j >= 3:
                            dve.wait_ge(s.a_T, n - 2)
                        nc.vector.tensor_tensor(a_sb[:, b, :], sg_sb[:, b, :], ps[:, 4 + b, F:2 * F], ALU.mult).then_inc(s.a_ready, 1)
                    if not last and not early:
                        window_l(turn, j)
                    if not first or j >= 3:
                        y_out(*back(turn, j, 3))
                    if not last:
                        l_chunks(turn, j, range(4, 8))

                over_experts(dve, step)
                for j in (EB - 2, EB - 1):
                    y_out(TURNS - 1, j)
                dve.wait_ge(s.y_dve, eb + E)

            def moe(layer):
                n = 2 * layer + 1
                norm(n)
                split_small(wr_h[:, :, 0:LOGITS], wr_l[:, :, 0:LOGITS], w_rout[:, layer, :, :])
                evac_T(n, g_ffn[:, layer, :])
                dve.wait_ge(log_T, layer + 1)
                done(nc.vector.tensor_tensor(lg[:], ps[:, 5, 0:NT * LOGITS].rearrange("p (i k) -> p i k", i=NT),
                                             b_rout[:, layer, :, :], ALU.add))
                gl = lg[:, :, 0:G]
                done(nc.vector.tensor_reduce(st[:, 16:18], gl, AX_X, ALU.max))
                nc.vector.tensor_scalar(st[:, 18:20], st[:, 16:18], -1.0, None, ALU.mult).then_inc(gneg, 1)

                def first_max(dst, vals, mx, k, tmp):
                    done(nc.vector.tensor_tensor(tmp, vals, mx.rearrange("p (i o) -> p i o", o=1).to_broadcast([P, NT, k]), ALU.is_equal))
                    done(nc.vector.tensor_tensor(tmp, tmp, rank_w[:, E - k:E].rearrange("p (o k) -> p o k", o=1).to_broadcast([P, NT, k]), ALU.mult))
                    done(nc.vector.tensor_reduce(st[:, 22:24], tmp, AX_X, ALU.max))
                    done(nc.vector.tensor_tensor(dst, tmp, st[:, 22:24].rearrange("p (i o) -> p i o", o=1).to_broadcast([P, NT, k]), ALU.is_equal))

                ghot = rt[:, 1, :, 0:G]
                first_max(ghot, gl, st[:, 16:18], G, rt[:, 1, :, G:2 * G])
                done(nc.vector.tensor_scalar(rt[:, 1, :, 8:8 + G], ghot, 1.0, BIG, ALU.subtract, ALU.mult))
                m32 = rt[:, 2, :, :]
                for i in range(NT):
                    done(nc.vector.tensor_tensor(m32[:, i, :].rearrange("p (g e) -> p g e", g=G),
                                                 lg[:, i, G:].rearrange("p (g e) -> p g e", g=G),
                                                 rt[:, 1, i, 8:8 + G].rearrange("p (g o) -> p g o", o=1).to_broadcast([P, G, EG]), ALU.add))
                done(nc.vector.tensor_reduce(st[:, 24:26], m32, AX_X, ALU.max))
                first_max(rt[:, 3, :, :], m32, st[:, 24:26], E, rt[:, 5, :, :])
                done(nc.vector.scalar_tensor_tensor(out=m32, in0=rt[:, 3, :, :], scalar=-2 * BIG, in1=m32, op0=ALU.mult, op1=ALU.add))
                done(nc.vector.tensor_reduce(st[:, 30:32], m32, AX_X, ALU.max))
                first_max(rt[:, 4, :, :], m32, st[:, 30:32], E, rt[:, 5, :, :])
                nc.vector.tensor_tensor(st[:, 26:28], st[:, 30:32], st[:, 24:26], ALU.subtract).then_inc(ediff, 1)
                nc.vector.tensor_tensor(rt[:, 5, :, :], rt[:, 3, :, :], rt[:, 4, :, :], ALU.add).then_inc(asg_ready, 1)
                first_l((U0_MOE0, U0_MOE1)[layer], 4 * SPLIT0[f"moe{layer}"], MOE_FIRST)
                dve.wait_ge(eexp, layer + 1)
                dve.wait_ge(gsum, 2 * layer + 2)
                done(nc.vector.tensor_scalar(st[:, 24:26], st[:, 28:30], 1.0, None, ALU.add))
                done(nc.vector.tensor_tensor(st[:, 24:26], st[:, 24:26], st[:, 20:22], ALU.mult))
                done(nc.vector.reciprocal(st[:, 16:18], st[:, 24:26]))
                done(nc.vector.tensor_tensor(st[:, 30:32], st[:, 16:18], st[:, 28:30], ALU.mult))
                cnt, cum = rt[:, 0, 0, :], rt[:, 0, 1, :]
                dve.wait_ge(rank_mm, layer + 1)
                done(nc.vector.tensor_copy(cnt, ps[:, 5, 2 * E:3 * E]))
                done(nc.vector.tensor_tensor_scan(cum, cnt, zeros[:], 0.0, ALU.add, ALU.add))
                done(nc.vector.tensor_tensor(rt[:, 5, 0, :], cum, cnt, ALU.subtract))
                for i in range(NT):
                    done(nc.vector.tensor_tensor(rt[:, 1, i, :], ps[:, 5, i * E:(i + 1) * E], rt[:, 5, 0, :], ALU.add))
                for k in range(2):
                    done(nc.vector.tensor_tensor(rt[:, 2, :, :], rt[:, 1, :, :], rt[:, 3 + k, :, :], ALU.mult))
                    done(nc.vector.tensor_reduce(st[:, 56 + 2 * k:58 + 2 * k], rt[:, 2, :, :], AX_X, ALU.add))
                dve.wait_ge(pads_zero, 3 * layer + 1)
                for i in range(NT):
                    done(nc.vector.tensor_scalar(hit[:, i, :], iota, st[:, 56 + i:57 + i], None, ALU.is_equal))
                    nc.vector.scalar_tensor_tensor(out=hit[:, i, :], in0=iota, scalar=st[:, 58 + i:59 + i], in1=hit[:, i, :].bitcast(F32),
                                                   op0=ALU.is_equal, op1=ALU.add).then_inc(hit_ready, 1)
                done(nc.vector.tensor_reduce(st[0:1, 60:61], cnt[0:1, :], AX_X, ALU.max))
                done(nc.vector.tensor_scalar(win[0:1, 0:E], rt[0:1, 5, 0, :], float(LEAD), None, ALU.add))
                done(nc.vector.tensor_scalar(win[0:1, E:2 * E], cum[0:1, :], float(LEAD - W), None, ALU.add))
                nc.vector.tensor_copy(win[0:1, 2 * E:2 * E + 1], st[0:1, 60:61]).then_inc(win_ready, 1)
                for i in range(NT):
                    done(nc.vector.tensor_scalar(hit_w[:, i, :], iota, st[:, 56 + i:57 + i], st[:, 16 + i:17 + i],
                                                 ALU.is_equal, ALU.mult))
                    done(nc.vector.tensor_scalar(hit_t, iota, st[:, 58 + i:59 + i], st[:, 30 + i:31 + i],
                                                 ALU.is_equal, ALU.mult))
                    nc.vector.tensor_tensor(hit_w[:, i, :], hit_w[:, i, :], hit_t, ALU.add).then_inc(hitw_ready, 1)
                for c in range(1, DC, 2):
                    dve.wait_ge(gath_mm, DC * layer + c + 1)
                    nc.vector.tensor_scalar(Xs[:, c, LEAD:LEAD + NPOS], ps[:, c, :], g_ffn[:, layer, c:c + 1], None,
                                            ALU.mult).then_inc(xs_dve, 1)
                dve.wait_ge(win_ready, layer + 1)
                most = dve.value_load(win[0:1, 2 * E:2 * E + 1], min_val=0, max_val=T)
                experts(layer, main, False)
                with dve.If(most > W):
                    dve.wait_ge(main.y_act, E * (layer + 1))
                    experts(layer, again[layer], True)
                dve.sem_inc(ys_dve, 1)
                for b in range(2 * NPC):
                    dve.wait_ge(yn_act, 2 * NPC * layer + b + 1)
                    nc.vector.scalar_tensor_tensor(out=Yn(b)[1], in0=ps[:, 4 + b % 4, :], scalar=w_pos[:, b // 2:b // 2 + 1],
                                                   in1=Yn(b)[0].bitcast(F32), op0=ALU.mult, op1=ALU.subtract).then_inc(yn_dve, 1)
                residual(n, comb_mm, NT * layer + 1)

            moe(0)
            norm(2)
            first_l(U0_DA_IN, 4 * SPLIT0["da_in"])
            evac_T(2, g_mix[:, 1, :])
            for nb in range(6):
                split_block(U0_DA_IN, 4 * SPLIT0["da_in"], nb, lambda nb, k: None)

            def maxima(h):
                k = 4 * (h % 2)
                dve.wait_ge(asc_mm, h + 1)
                for i in range(NT):
                    red = nc.vector.tensor_reduce(st[:, 8 + k + 2 * i:10 + k + 2 * i], ps[:, 2 - k // 2:4 - k // 2, i * P:(2 * i + 1) * P], AX_X, ALU.max)
                done(red)
                nc.vector.tensor_scalar(st[:, 16 + k:20 + k], st[:, 8 + k:12 + k], -DH ** -0.5, None, ALU.mult).then_inc(asc_max, 1)

            maxima(0)
            for h in range(HA):
                b = h % 2
                dve.wait_ge(aex, 4 * (h + 1))
                done(nc.vector.reciprocal(att_r[:, h, :], st[:, 24 + 4 * b:28 + 4 * b]))
                done(nc.vector.scalar_tensor_tensor(out=st[:, 56:58], in0=st[:, 24 + 4 * b:28 + 4 * b:2], scalar=lam_s[:, 5:6],
                                                    in1=att_r[:, h, 1:4:2], op0=ALU.mult, op1=ALU.mult))
                for i in range(NT):
                    seg = slice(i * P, (2 * i + 1) * P)
                    nc.vector.scalar_tensor_tensor(out=ew[:, b, 0, seg], in0=ew[:, b, 1, seg], scalar=st[:, 56 + i:57 + i], in1=ew[:, b, 0, seg],
                                                   op0=ALU.mult, op1=ALU.add).then_inc(aw_ready, 1)
                dve.wait_ge(aw_ready, 2 * h + 2)
                if h + 1 < HA:
                    maxima(h + 1)
            first_l(U0_DA_OUT, 4 * SPLIT0["da_out"])
            dve.wait_ge(apv_read, HA)
            nc.vector.tensor_scalar(st[:, 40:56], st[:, 40:56], 1.0 / DVA, DA_EPS, ALU.mult, ALU.add).then_inc(hms, 1)
            dve.wait_ge(hroot, 3)
            done(nc.vector.reciprocal(st[:, 40:56], st[:, 40:56]))
            for half in range(2):
                for i in range(NT):
                    o = og[:, i, half * HA // 2 * DVA:(half + 1) * HA // 2 * DVA].rearrange("p (h v) -> p h v", h=HA // 2)
                    r = st[:, 40 + HA * i + half * HA // 2:40 + HA * i + (half + 1) * HA // 2].rearrange("p (h o) -> p h o", o=1)
                    nc.vector.tensor_tensor(o, o, r.to_broadcast([P, HA // 2, DVA]), ALU.mult).then_inc(y_ready, 1)
            output(U0_DA_OUT, 4 * SPLIT0["da_out"], HA, VC, 2, lambda c: lam_s[:, 6:7])
            moe(1)
            norm(4)

        @block.tensor
        def _(pe):
            def split_mm(dst, lhs, rhs, start, stop):
                pe.matmul(dst, lhs[0], rhs[0], start=start, stop=False)
                pe.matmul(dst, lhs[1], rhs[0], start=False, stop=False)
                return pe.matmul(dst, lhs[0], rhs[1], start=False, stop=stop)

            def input_T(n):
                if n:
                    pe.wait_ge(res_done, 4 * n)
                for i in range(NT):
                    pe.wait_ge(xn_ready, NT * n + i + 1)
                    for c in range(DC):
                        col = (c % 2) * T + i * P
                        mm = pe.transpose(ps[:, 4 + c // 2, col:col + P], xn[:, i, c:D:DC], ident[:])
                        if i == NT - 1 and c % 2:
                            mm.then_inc(xn_T, 1)
                if n == 0:
                    pe.wait_ge(tables_made, 1)
                    pe.wait_ge(par_loaded, 48)
                    pe.transpose(ps[:, 0, 0:N_COLS], par_rows[:], ident[0:N_COLS, 0:N_COLS]).then_inc(par_T, 1)
                    pe.wait_ge(par_ready, 1)
                if n == 0:
                    pe.wait_ge(xl_ready, DC)

            def x_tile(c, i):
                return xTh[:, c, i * P:(i + 1) * P], xTl[:, c, i * P:(i + 1) * P]

            def w_chunk(ch, cols=slice(0, CH)):
                return wh[:, ch % BUFS, cols], wl[:, ch % BUFS, cols]

            def project_T(ch0, nb, n):
                for c in range(DC):
                    if nb == 0:
                        pe.wait_ge(xl_ready, DC * n + c + 1)
                    ch = ch0 + 8 * nb + c
                    pe.wait_ge(l_made, ch + 1)
                    for cc in range(4):
                        mm = split_mm(ps[:, (nb % 2) * 4 + cc, 0:T], w_chunk(ch, slice(cc * P, (cc + 1) * P)),
                                      (xTh[:, c, :], xTl[:, c, :]), c == 0, c == DC - 1)
                    mm.then_inc(chunk_used, 1)

            def project(ch0, nb, bank):
                for c in range(DC):
                    ch = ch0 + 8 * nb + c
                    pe.wait_ge(l_made, ch + 1)
                    for i in range(NT):
                        mm = split_mm(ps[:, bank + i, :], x_tile(c, i), w_chunk(ch), c == 0, c == DC - 1)
                    mm.then_inc(chunk_used, 1)

            def output(ch0, chunks, T0, to_T, before):
                def pair(b):
                    if b >= 4:
                        pe.wait_ge(yl_ready, T0 + 2 * b - 6)
                    for c in (2 * b, 2 * b + 1):
                        before(c)
                        for i in range(NT):
                            mm = to_T(ps[:, 4 + b % 4, c % 2 * T + i * P:c % 2 * T + (i + 1) * P], c, i)
                    mm.then_inc(y_T, 1)

                for b in range(4):
                    pair(b)
                for c in range(chunks):
                    pe.wait_ge(yl_ready, T0 + c + 1)
                    for half in range(2):
                        ch = ch0 + 2 * c + half
                        pe.wait_ge(l_made, ch + 1)
                        for i in range(NT):
                            mm = split_mm(ps[:, 2 * i + half, :], x_tile(c % DC, i), w_chunk(ch), c == 0, c == chunks - 1)
                        mm.then_inc(chunk_used, 1)
                    if c % 2 and c // 2 + 4 < chunks // 2:
                        pair(c // 2 + 4)

            pe.wait_ge(pool_step, 2)
            input_T(0)
            pe.wait_ge(small_split, 1)
            for c in range(DC):
                mm = split_mm(ps[:, 7, 0:T], (wg_h[:, c, :], wg_l[:, c, :]), (xTh[:, c, :], xTl[:, c, :]), c == 0, c == DC - 1)
            mm.then_inc(gates_mm, 1)
            def gate_parts():
                pe.wait_ge(vo_read, 12)
                pe.wait_ge(gate_rows, 1)
                pe.wait_ge(gate_emt, 1)
                for i in range(NT):
                    for k, row in enumerate((5, 7)):
                        mm = pe.transpose(ps[:, 3, (2 * i + k) * HM:(2 * i + k + 1) * HM], gr[:, row, i * P:(i + 1) * P], ident[0:HM, 0:HM])
                mm.then_inc(gate_cols_mm, 1)
                for h in range(HM):
                    mm = pe.matmul(ps[:, h // 2, (h % 2) * T:(h % 2 + 1) * T], ident[0:HM, h:h + 1].to_broadcast([HM, P]), gr[:, 1, :], start=True, stop=True)
                mm.then_inc(rows_bcast, 1)
                pe.wait_ge(qk_ready, QC)

            def scores(h):
                if h >= 2:
                    pe.wait_ge(s_ready, h - 1)
                for s in range(2):
                    for c in range(2):
                        q, k = qkT[:, 2 * h + c, s * P:T], qkT[:, QC // 2 + 2 * h + c, s * P:(s + 1) * P]
                        mm = pe.matmul(ps[:, 2 + h % 2, s * T:s * T + T - s * P], k, q, start=(c == 0), stop=(c == 1))
                mm.then_inc(sc_mm, 1)

            for nb in range(12):
                if nb < 4:
                    if nb == 1:
                        pe.wait_ge(gates_copied, 1)
                    if nb >= 2:
                        pe.wait_ge(conv_done, 4 * (nb - 1))
                    project_T(0, nb, 0)
                    continue
                if nb == 11:
                    gate_parts()
                    scores(0)
                if nb < 8:
                    pe.wait_ge(conv_done, 12 if nb < 6 else 16)
                else:
                    pe.wait_ge(vo_read, 2 * (nb - 7))
                if nb == 7:
                    pe.wait_ge(gates_read, 2)
                project(0, nb, 2 * nb % 8)
                if nb == 5:
                    pe.wait_ge(conv_done, 16)
                    for g in range(2):
                        mm = pe.matmul(ps[0:HM, 7, g * T:(g + 1) * T], ident[0:2 * HM, g * HM:(g + 1) * HM], gT, start=True, stop=True)
                    mm.then_inc(gates_sel, 1)
            pe.wait_ge(gate_cols, 1)
            pe.wait_ge(dm_ready, HM)
            for h in range(HM):
                if h + 1 < HM:
                    scores(h + 1)
                if h < 2:
                    pe.wait_ge(vo_read, 14 + 2 * h)
                else:
                    pe.wait_ge(hsq, 2 * h - 2)
                pe.wait_ge(s_ready, h + 1)
                for i in range(NT):
                    for s in range(i + 1):
                        lhs = sT[:, h % 2, (i + s) * P:(i + s + 1) * P]
                        pe.matmul(ps[:, h % 2, i:i + 1], lhs, ones[:, 0:1], start=(s == 0), stop=(s == i))
                for i in range(NT):
                    for s in range(i + 1):
                        lhs = sT[:, h % 2, (i + s) * P:(i + s + 1) * P]
                        mm = pe.matmul(ps[:, 4 + 2 * (h % 2) + i, :], lhs, v_sb[:, s, h * DV:(h + 1) * DV], start=(s == 0), stop=(s == i))
                mm.then_inc(pv_mm, 1)

            def ml_before(c):
                if c % 4 == 0:
                    pe.wait_ge(diag_ready, 2 * (c // 4 + 1))
                if c == 4:
                    pe.wait_ge(hsq, 2 * HM)

            def ml_to_T(dst, c, i):
                return pe.matmul(dst, og[:, i, c * P:(c + 1) * P], diag[:, c // 4, i, :], start=True, stop=True)

            output(4 * SPLIT0["ml_out"], VC, 0, ml_to_T, ml_before)

            def experts(layer, s, again):
                u0, cb, wb, eb = bases(layer, again)

                def step(turn, j, first, last):
                    n = turn * EB + (eb + j)
                    pt, pj = (turn, j - 1) if j else (turn - 1, EB - 1)
                    has_before = not (first and j == 0)

                    def transpose_a():
                        pe.wait_ge(s.a_ready, n)
                        if not first or j >= 3:
                            pe.wait_ge(s.aT_ready, n - 2)
                        for c in range(2):
                            mm = pe.transpose(ps[:, 6 + pj % 2, c * P:(c + 1) * P], a_sb[:, pj % 2, c:F:2], ident[:])
                        mm.then_inc(s.a_T, 1)

                    late = first and j == 1
                    if has_before and not late:
                        transpose_a()
                    if not last:
                        pe.wait_ge(s.xw_l, n + 1)
                        xs = slice(j % 2 * W, (j % 2 + 1) * W)
                        for c in range(DC):
                            pe.wait_ge(s.l_made, turn * (8 * EB) + (cb + 8 * j + c + 1))
                            mm = split_mm(ps[:, 4 + j % 2, :], (xTh[:, c, xs], xTl[:, c, xs]), w_chunk(c), c == 0, c == DC - 1)
                            mm.then_inc(s.chunk_used, 1)
                    if late:
                        transpose_a()
                        pe.wait_ge(hitT_act, layer + 1)
                        pe.wait_ge(hitT_dve, layer + 1)
                    if has_before:
                        pe.wait_ge(*loaded(s, u0, pt, pj, 2))
                        pe.wait_ge(s.aT_ready, n)
                        if not first or j >= 3:
                            pe.wait_ge(s.y_act, n - 2)
                            pe.wait_ge(s.y_dve, n - 2)
                        w = slot(u0, pj, 2)
                        for c in range(DC):
                            for k in range(2):
                                mm = pe.matmul(ps[:, 2 * (pj % 2) + c // 4, c % 4 * P:(c % 4 + 1) * P],
                                               w[:, k * D + c * P:k * D + (c + 1) * P], aT[:, pj % 2, k, :], start=(k == 0), stop=(k == 1))
                        mm.then_inc(s.whole_used, 1)

                over_experts(pe, step)

            def moe(layer):
                input_T(2 * layer + 1)
                pe.wait_ge(small_split, 2 + layer)
                for c in range(DC):
                    pe.wait_ge(xl_ready, DC * (2 * layer + 1) + c + 1)
                    mm = split_mm(ps[:, 0, 0:T], (wr_h[:, c, :], wr_l[:, c, :]), (xTh[:, c, :], xTl[:, c, :]), c == 0, c == DC - 1)
                mm.then_inc(log_mm, 1)
                pe.wait_ge(lgT_ready, layer + 1)
                for i in range(NT):
                    mm = pe.transpose(ps[:, 5, i * LOGITS:(i + 1) * LOGITS], lgT[:, i * P:(i + 1) * P], ident[0:LOGITS, 0:LOGITS])
                mm.then_inc(log_T, 1)
                pe.wait_ge(asg_ready, layer + 1)
                pe.matmul(ps[:, 5, 0:E], earlier[:], rt[:, 5, 0, :], start=True, stop=True)
                pe.matmul(ps[:, 5, E:2 * E], earlier[:], rt[:, 5, 1, :], start=True, stop=False)
                pe.matmul(ps[:, 5, E:2 * E], ones[:], rt[:, 5, 0, :], start=False, stop=True)
                pe.matmul(ps[:, 5, 2 * E:3 * E], ones[:], rt[:, 5, 0, :], start=True, stop=False)
                pe.matmul(ps[:, 5, 2 * E:3 * E], ones[:], rt[:, 5, 1, :], start=False, stop=True).then_inc(rank_mm, 1)
                pe.wait_ge(hit_ready, 2 * layer + 2)
                pe.wait_ge(xnh_ready, layer + 1)
                pe.wait_ge(xnl_ready, NT * (layer + 1))
                for c in range(DC):
                    for i in range(NT):
                        pe.matmul(ps[:, c, :], xnh[:, i, c:D:DC], hit[:, i, :], start=(i == 0), stop=False)
                        mm = pe.matmul(ps[:, c, :], xnl[:, i, c:D:DC], hit[:, i, :], start=False, stop=(i == NT - 1))
                    mm.then_inc(gath_mm, 1)
                pe.wait_ge(hitw_ready, 2 * layer + 2)
                pe.wait_ge(xs_act, 4 * layer + 1)
                pe.wait_ge(xs_dve, 4 * layer + 1)
                for k in range(NPC):
                    for i in range(NT):
                        mm = pe.transpose(ps[:, k // 2, k % 2 * T + i * P:k % 2 * T + (i + 1) * P],
                                          hit[:, i, k * P:(k + 1) * P].bitcast(F32), ident[:])
                    if k % 2:
                        mm.then_inc(hit_T, 1)
                pe.wait_ge(xs_act, 4 * layer + 2)
                for k in range(NPC):
                    for i in range(NT):
                        mm = pe.matmul(ps[:, 2, k:k + 1], hit_w[:, i, k * P:(k + 1) * P], ones[:, 0:1], start=(i == 0), stop=(i == NT - 1))
                mm.then_inc(hit_T, 1)
                pe.wait_ge(xs_act, 4 * layer + 4)
                pe.wait_ge(xs_dve, 4 * layer + 4)
                pe.wait_ge(win_ready, layer + 1)
                most = pe.value_load(win[0:1, 2 * E:2 * E + 1], min_val=0, max_val=T)
                experts(layer, main, False)
                with pe.If(most > W):
                    pe.wait_ge(main.y_act, E * (layer + 1))
                    pe.wait_ge(main.y_dve, E * (layer + 1))
                    experts(layer, again[layer], True)
                pe.wait_ge(ys_act, layer + 1)
                pe.wait_ge(ys_dve, layer + 1)
                def positions(b):
                    if b >= 4:
                        pe.wait_ge(yn_dve, 2 * NPC * layer + b - 3)
                    for c in range(4):
                        mm = pe.transpose(ps[:, 4 + b % 4, c * P:(c + 1) * P], Ys[:, b % 2 * 4 + c, LEAD + b // 2 * P:LEAD + (b // 2 + 1) * P], ident[:])
                    mm.then_inc(ys_T, 1)

                for b in range(4):
                    positions(b)
                def combine(b, i):
                    k, half = b // 2, b % 2
                    ts = slice(i * P, (i + 1) * P)
                    pe.matmul(ps[:, 2 * i + half, :], hitT[:, k, ts], Yn(b)[0], start=(k == 0), stop=False)
                    return pe.matmul(ps[:, 2 * i + half, :], hitT[:, k, ts], Yn(b)[1], start=False, stop=(k == NPC - 1))

                for b in range(2 * NPC - 2):
                    pe.wait_ge(yn_dve, 2 * NPC * layer + b + 1)
                    for i in range(NT):
                        combine(b, i)
                    if b + 4 < 2 * NPC:
                        positions(b + 4)
                pe.wait_ge(yn_dve, 2 * NPC * (layer + 1))
                for i in range(NT):
                    for b in (2 * NPC - 2, 2 * NPC - 1):
                        mm = combine(b, i)
                    mm.then_inc(comb_mm, 1)

            moe(0)
            input_T(2)
            def a_scores(h):
                if h >= 2:
                    pe.wait_ge(aex, 4 * (h - 1))
                for i in range(NT):
                    for c in range(2):
                        bank = ps[:, 2 - 2 * (h % 2) + c, :]
                        lo, hi = i * P, (2 * i + 1) * P
                        part = slice(c * DH, (c + 1) * DH)
                        if i:
                            pe.matmul(bank[:, lo:lo + P], qkT[part, h, P:T], qkT[part, HA + h, 0:P], start=True, stop=True)
                        pe.matmul(bank[:, hi - P:hi], qkT[part, h, i * P:(i + 1) * P], qkT[part, HA + h, i * P:(i + 1) * P], start=True, stop=False)
                        mm = pe.matmul(bank[:, hi - P:hi], ident_b[:], neg_qk[:], start=False, stop=True)
                mm.then_inc(asc_mm, 1)

            for nb in range(6):
                if nb in (2, 3):
                    pe.wait_ge(qk_ready, QC + 4 * (nb - 1))
                if nb < 4:
                    project_T(4 * SPLIT0["da_in"], nb, 2)
                    continue
                if nb == 4:
                    pe.wait_ge(qk_ready, QC + 12)
                else:
                    pe.wait_ge(qk_ready, 2 * QC)
                    a_scores(0)
                project(4 * SPLIT0["da_in"], nb, 4 * (nb - 4))
            pe.wait_ge(vo_read, 18)
            a_scores(1)
            pe.wait_ge(vo_read, 20)
            for h in range(HA):
                pe.wait_ge(aw_ready, 2 * h + 2)
                if h >= 2:
                    pe.wait_ge(awT_ready, h - 1)
                for n in range(3):
                    mm = pe.transpose(ps[:, 4 + h % 2, n * P:(n + 1) * P], ew[:, h % 2, 0, n * P:(n + 1) * P], ident[:])
                mm.then_inc(aw_T, 1)
                if h + 2 < HA:
                    a_scores(h + 2)
                pe.wait_ge(awT_ready, h + 1)
                if h >= 2:
                    pe.wait_ge(apv_read, h - 1)
                for i in range(NT):
                    for s in range(i + 1):
                        mm = pe.matmul(ps[:, 6 + h % 2, i * P:(i + 1) * P], sT[:, h % 2, (i + s) * P:(i + s + 1) * P],
                                       vA[:, s, h * DVA:(h + 1) * DVA], start=(s == 0), stop=(s == i))
                mm.then_inc(apv, 1)

            def da_before(c):
                if c % (HA // 2) == 0:
                    pe.wait_ge(y_ready, 2 * HM + (2 if c == 0 else 4))

            output(4 * SPLIT0["da_out"], HA, VC, lambda dst, c, i: pe.transpose(dst, og[:, i, c * P:(c + 1) * P], ident[:]), da_before)
            moe(1)


CONSTS = 16 * (3 + 2 * 6 + 4)

_INS = ['x', 'norm_mix', 'norm_ffn', 'ml_w_in', 'ml_conv', 'ml_b_i', 'ml_b_f', 'ml_norm', 'ml_w_out',
        'da_w_in', 'da_lq1', 'da_lk1', 'da_lq2', 'da_lk2', 'da_norm', 'da_w_out',
        'moe_w_group', 'moe_b_group', 'moe_w_expert', 'moe_b_expert', 'moe_w_gu', 'moe_w_down', 'final_norm']


def kernel(**inputs):
    import numpy as _np
    import concourse.bacc as _bacc
    from concourse.bass_utils import run_bass_kernel_spmd as _run

    nc = _bacc.Bacc("TRN2", target_bir_lowering=False, num_devices=1)
    arrays, args = {}, []
    for name in _INS:
        a = _np.ascontiguousarray(inputs[name])
        arrays[f"in_{name}_dram"] = a
        args.append(nc.dram_tensor(f"in_{name}_dram", a.shape, mybir.dt.from_np(a.dtype), kind="ExternalInput").ap())
    args.append(nc.dram_tensor("out_0_dram", (1, T, D), F32, kind="ExternalOutput").ap())
    program(nc, *args)
    r = _run(nc, [arrays], core_ids=[0])
    return r.results[0]["out_0_dram"]
```
